# Optimizing a Trainium2 kernel written in Bass

```python
import jax, jax.numpy as jnp
from jax import lax
import numpy as np

D_MODEL = 1024
BATCH = 1
SEQ = 512
DEPTH = 2

CTX_LEN = 256
GRID_W = 64
HEAD_DIM = 64
GLA_HEADS = 4
GLA_DK = 32
GLA_DV = 64
GLA_RANK = 16
GLA_TAU = 16.0
GLA_CHUNK = 64
NAT_HEADS = 4
NAT_WIN_ROWS = 8
NAT_WIN_COLS = 16
SWA_Q_HEADS = 8
SWA_KV_HEADS = 2
SWA_WINDOW = 128
SWA_BLOCK = SWA_WINDOW
ROPE_BASE = 10000.0
N_EXPERTS = 16
EXPERT_FF = 1024
CAPACITY_FACTOR = 2
NORM_EPS = 1e-6

GLA_WIDTH = GLA_HEADS * GLA_DV
NAT_WIDTH = NAT_HEADS * HEAD_DIM
SWA_WIDTH = SWA_Q_HEADS * HEAD_DIM
MIX_WIDTH = GLA_WIDTH + NAT_WIDTH + SWA_WIDTH
KV_WIDTHS = (GLA_HEADS * GLA_DK, GLA_WIDTH, GLA_RANK, GLA_RANK, NAT_WIDTH, NAT_WIDTH, SWA_KV_HEADS * HEAD_DIM, SWA_KV_HEADS * HEAD_DIM)
Q_WIDTHS = (GLA_HEADS * GLA_DK, GLA_WIDTH, NAT_WIDTH, SWA_WIDTH)
KV_WIDTH = sum(KV_WIDTHS)
IN_WIDTH = KV_WIDTH + sum(Q_WIDTHS)

kernel_name = 'hybrid_dit_gla_natten_swa_ecmoe'

def _split(a, widths):
    idx = np.cumsum(widths)[:-1].tolist()
    return jnp.split(a, idx, axis=-1)

def _heads(a, n):
    return a.reshape(a.shape[0], a.shape[1], n, -1)

def _flip(a):
    return jnp.flip(a, axis=1)

def rms_norm(x, gain):
    xf = x.astype(jnp.float32)
    y = xf * lax.rsqrt(jnp.mean(xf * xf, axis=-1, keepdims=True) + NORM_EPS)
    return (y * gain.astype(jnp.float32)).astype(x.dtype)

def modulate(x, shift, scale):
    return x * (1 + scale) + shift

def _rope_axis(x, pos):
    half = x.shape[-1] // 2
    freqs = ROPE_BASE ** (-jnp.arange(half, dtype=jnp.float32) / half)
    ang = pos.astype(jnp.float32)[:, None] * freqs
    cos = jnp.cos(ang)[:, None, :]
    sin = jnp.sin(ang)[:, None, :]
    xf = x.astype(jnp.float32)
    x1, x2 = xf[..., :half], xf[..., half:]
    return jnp.concatenate([x1 * cos - x2 * sin, x2 * cos + x1 * sin], axis=-1).astype(x.dtype)

def axial_rope(x):
    t = jnp.arange(x.shape[1])
    half = x.shape[-1] // 2
    return jnp.concatenate([_rope_axis(x[..., :half], t // GRID_W), _rope_axis(x[..., half:], t % GRID_W)], axis=-1)

def gla_log_decay(a_low, w_up, b_up):
    z = (a_low @ w_up + b_up).astype(jnp.float32)
    la = jax.nn.log_sigmoid(z) / GLA_TAU
    return la.reshape(la.shape[0], la.shape[1], GLA_HEADS, GLA_DK)

def gla_chunk_scan(q, k, v, log_a, s0):
    bsz, t, h, _ = q.shape
    nc = t // GLA_CHUNK

    def to_chunks(a):
        return a.reshape(bsz, nc, GLA_CHUNK, *a.shape[2:]).swapaxes(0, 1)

    causal = jnp.tril(jnp.ones((GLA_CHUNK, GLA_CHUNK), dtype=bool))[None, :, :, None, None]

    def step(state, inp):
        qc, kc, vc, lc = inp
        cum = jnp.cumsum(lc, axis=1)
        inter = jnp.einsum('bchk,bhkv->bchv', qc * jnp.exp(cum), state)
        diff = jnp.where(causal, cum[:, :, None] - cum[:, None, :], -jnp.inf)
        scores = jnp.einsum('bihk,bjhk,bijhk->bhij', qc, kc, jnp.exp(diff))
        intra = jnp.einsum('bhij,bjhv->bihv', scores, vc)
        last = cum[:, -1]
        state = jnp.exp(last)[..., None] * state + jnp.einsum('bjhk,bjhv->bhkv', kc * jnp.exp(last[:, None] - cum), vc)
        return state, inter + intra

    s_fin, o = lax.scan(step, s0, (to_chunks(q), to_chunks(k), to_chunks(v), to_chunks(log_a)))
    return o.swapaxes(0, 1).reshape(bsz, t, h, v.shape[-1]), s_fin

def gla_bidir(q, k, v, la_f, la_b, s0_f, s0_b):
    o_f, s_f = gla_chunk_scan(q, k, v, la_f, s0_f)
    o_b, s_b = gla_chunk_scan(_flip(q), _flip(k), _flip(v), _flip(la_b), s0_b)
    return o_f + _flip(o_b), s_f, s_b

def gla_final_state(k, v, log_a):
    cum = jnp.cumsum(log_a, axis=1)
    return jnp.einsum('bthk,bthv->bhkv', k * jnp.exp(cum[:, -1:] - cum), v)

def gla_group_out(o, gate, gain, dtype):
    o = rms_norm(o, gain)
    return (o.reshape(o.shape[0], o.shape[1], -1) * jax.nn.silu(gate.astype(jnp.float32))).astype(dtype)

def neighborhood_attention(q, k, v, k_ctx, v_ctx, rpb):
    bsz, s, h, d = q.shape
    rows = s // GRID_W
    wr = min(NAT_WIN_ROWS, rows)
    n_loc = wr * NAT_WIN_COLS
    qg = q.reshape(bsz, rows, GRID_W, h, d)
    kg = k.reshape(bsz, rows, GRID_W, h, d)
    vg = v.reshape(bsz, rows, GRID_W, h, d)
    cols = jnp.arange(GRID_W)
    col_start = jnp.clip(cols - NAT_WIN_COLS // 2, 0, GRID_W - NAT_WIN_COLS)
    col_idx = col_start[:, None] + jnp.arange(NAT_WIN_COLS)
    col_bias_idx = col_idx - cols[:, None] + NAT_WIN_COLS - 1
    scale = d ** -0.5

    def row_block(r):
        r_start = jnp.clip(r - wr // 2, 0, rows - wr)
        q_r = lax.dynamic_index_in_dim(qg, r, axis=1, keepdims=False)
        k_nb = lax.dynamic_slice_in_dim(kg, r_start, wr, axis=1)[:, :, col_idx]
        v_nb = lax.dynamic_slice_in_dim(vg, r_start, wr, axis=1)[:, :, col_idx]
        s_loc = jnp.einsum('bchd,brckhd->bhcrk', q_r, k_nb).astype(jnp.float32) * scale
        row_bias_idx = r_start + jnp.arange(wr) - r + NAT_WIN_ROWS - 1
        bias = rpb[:, row_bias_idx][:, :, col_bias_idx]
        s_loc = s_loc + bias.transpose(0, 2, 1, 3).astype(jnp.float32)[None]
        s_ctx = jnp.einsum('bchd,bmhd->bhcm', q_r, k_ctx).astype(jnp.float32) * scale
        logits = jnp.concatenate([s_loc.reshape(bsz, h, GRID_W, n_loc), s_ctx], axis=-1)
        p = jax.nn.softmax(logits, axis=-1).astype(v.dtype)
        p_loc = p[..., :n_loc].reshape(bsz, h, GRID_W, wr, NAT_WIN_COLS)
        return (jnp.einsum('bhcrk,brckhd->bchd', p_loc, v_nb)
                + jnp.einsum('bhcm,bmhd->bchd', p[..., n_loc:], v_ctx))

    out = lax.map(row_block, jnp.arange(rows))
    return out.transpose(1, 0, 2, 3, 4).reshape(bsz, s, h * d)

def sliding_window_attention(q, k, v, k_ctx, v_ctx, sink):
    bsz, s, hq, d = q.shape
    hkv = k.shape[2]
    g = hq // hkv
    nb = s // SWA_BLOCK
    n_loc = 3 * SWA_BLOCK
    m = k_ctx.shape[1]
    scale = d ** -0.5
    qb = q.reshape(bsz, nb, SWA_BLOCK, hkv, g, d)

    def band(a):
        ap = jnp.pad(a, ((0, 0), (SWA_BLOCK, SWA_BLOCK), (0, 0), (0, 0)))
        ab = ap.reshape(bsz, nb + 2, SWA_BLOCK, hkv, d)
        return jnp.concatenate([ab[:, :-2], ab[:, 1:-1], ab[:, 2:]], axis=2)

    kb, vb = band(k), band(v)
    blk = jnp.arange(nb)[:, None] * SWA_BLOCK
    q_pos = (blk + jnp.arange(SWA_BLOCK))[:, :, None]
    k_pos = (blk - SWA_BLOCK + jnp.arange(n_loc))[:, None, :]
    valid = (jnp.abs(k_pos - q_pos) <= SWA_WINDOW) & (k_pos >= 0) & (k_pos < s)
    s_loc = jnp.einsum('bnqhgd,bnkhd->bnhgqk', qb, kb).astype(jnp.float32) * scale
    s_loc = jnp.where(valid[None, :, None, None], s_loc, -jnp.inf)
    s_ctx = jnp.einsum('bnqhgd,bmhd->bnhgqm', qb, k_ctx).astype(jnp.float32) * scale
    sink_col = jnp.broadcast_to(sink.astype(jnp.float32).reshape(1, 1, hkv, g, 1, 1), (bsz, nb, hkv, g, SWA_BLOCK, 1))
    p = jax.nn.softmax(jnp.concatenate([s_loc, s_ctx, sink_col], axis=-1), axis=-1).astype(v.dtype)
    out = (jnp.einsum('bnhgqk,bnkhd->bnqhgd', p[..., :n_loc], vb)
           + jnp.einsum('bnhgqm,bmhd->bnqhgd', p[..., n_loc:n_loc + m], v_ctx))
    return out.reshape(bsz, s, hq * d)

def dense_ctx_attention(q, k, v, sink):
    bsz, m, hq, d = q.shape
    hkv = k.shape[2]
    g = hq // hkv
    n_keys = k.shape[1]
    qg = q.reshape(bsz, m, hkv, g, d)
    logits = jnp.einsum('bqhgd,bkhd->bhgqk', qg, k).astype(jnp.float32) * d ** -0.5
    if sink is not None:
        sink_col = jnp.broadcast_to(sink.astype(jnp.float32).reshape(1, hkv, g, 1, 1), (bsz, hkv, g, m, 1))
        logits = jnp.concatenate([logits, sink_col], axis=-1)
    p = jax.nn.softmax(logits, axis=-1)[..., :n_keys].astype(v.dtype)
    return jnp.einsum('bhgqk,bkhd->bqhgd', p, v).reshape(bsz, m, hq * d)

def token_mixers(h, hc, w_in, a_up, a_bias, gla_gain, rpb, sink, update_ctx):
    f32 = jnp.float32
    bsz = h.shape[0]
    (gk, gv, gaf, gab, nk, nv, sk, sv, gq, gg, nq, sq) = _split(h @ w_in, KV_WIDTHS + Q_WIDTHS)
    if update_ctx:
        (cgk, cgv, cgaf, cgab, cnk, cnv, csk, csv, cgq, cgg, cnq, csq) = _split(hc @ w_in, KV_WIDTHS + Q_WIDTHS)
    else:
        (cgk, cgv, cgaf, cgab, cnk, cnv, csk, csv) = _split(hc @ w_in[:, :KV_WIDTH], KV_WIDTHS)

    ck = _heads(cgk, GLA_HEADS).astype(f32)
    cv = _heads(cgv, GLA_HEADS).astype(f32)
    cla_f = gla_log_decay(cgaf, a_up[0], a_bias[0])
    cla_b = gla_log_decay(cgab, a_up[1], a_bias[1])
    if update_ctx:
        cq = _heads(cgq, GLA_HEADS).astype(f32) * GLA_DK ** -0.5
        zero = jnp.zeros((bsz, GLA_HEADS, GLA_DK, GLA_DV), f32)
        co, s_f, s_b = gla_bidir(cq, ck, cv, cla_f, cla_b, zero, zero)
    else:
        s_f = gla_final_state(ck, cv, cla_f)
        s_b = gla_final_state(_flip(ck), _flip(cv), _flip(cla_b))
    q = _heads(gq, GLA_HEADS).astype(f32) * GLA_DK ** -0.5
    k = _heads(gk, GLA_HEADS).astype(f32)
    v = _heads(gv, GLA_HEADS).astype(f32)
    la_f = gla_log_decay(gaf, a_up[0], a_bias[0])
    la_b = gla_log_decay(gab, a_up[1], a_bias[1])
    o, _, _ = gla_bidir(q, k, v, la_f, la_b, s_f, s_b)
    gla_lat = gla_group_out(o, gg, gla_gain, h.dtype)

    nk_c, nv_c = _heads(cnk, NAT_HEADS), _heads(cnv, NAT_HEADS)
    nat_lat = neighborhood_attention(_heads(nq, NAT_HEADS), _heads(nk, NAT_HEADS), _heads(nv, NAT_HEADS), nk_c, nv_c, rpb)

    sk_c, sv_c = _heads(csk, SWA_KV_HEADS), _heads(csv, SWA_KV_HEADS)
    swa_lat = sliding_window_attention(axial_rope(_heads(sq, SWA_Q_HEADS)), axial_rope(_heads(sk, SWA_KV_HEADS)),
                                       _heads(sv, SWA_KV_HEADS), sk_c, sv_c, sink)

    lat = jnp.concatenate([gla_lat, nat_lat, swa_lat], axis=-1)
    if not update_ctx:
        return lat, None
    ctx_out = jnp.concatenate([
        gla_group_out(co, cgg, gla_gain, hc.dtype),
        dense_ctx_attention(_heads(cnq, NAT_HEADS), nk_c, nv_c, None),
        dense_ctx_attention(_heads(csq, SWA_Q_HEADS), sk_c, sv_c, sink),
    ], axis=-1)
    return lat, ctx_out

def expert_choice_ffn(h, w_router, w_gate, w_up, w_down):
    bsz, n, _ = h.shape
    cap = CAPACITY_FACTOR * n // N_EXPERTS
    aff = jax.nn.softmax(jnp.einsum('bnd,de->bne', h, w_router).astype(jnp.float32), axis=-1)
    g, idx = lax.top_k(aff.transpose(0, 2, 1), cap)
    bidx = jnp.arange(bsz)[:, None, None]
    xs = h[bidx, idx]
    hid = jax.nn.silu(jnp.einsum('becd,edf->becf', xs, w_gate)) * jnp.einsum('becd,edf->becf', xs, w_up)
    y = jnp.einsum('becf,efd->becd', hid, w_down) * g[..., None].astype(h.dtype)
    return jnp.zeros_like(h).at[bidx, idx].add(y)

def setup_inputs(seed: int = 0) -> dict:
    key = jax.random.key(seed)
    ks = jax.random.split(key, 18)

    def nrm(k, shape, scale):
        return jax.random.normal(k, shape, jnp.float32) * scale

    return {
        'x': nrm(ks[0], (BATCH, SEQ, D_MODEL), 1.0),
        'c': nrm(ks[1], (BATCH, D_MODEL), 1.0),
        'ctx': nrm(ks[2], (BATCH, CTX_LEN, D_MODEL), 1.0),
        'c_ctx': nrm(ks[3], (D_MODEL,), 1.0),
        'w_mod': nrm(ks[4], (DEPTH, D_MODEL, 6 * D_MODEL), 0.5 * D_MODEL ** -0.5),
        'b_mod': nrm(ks[5], (DEPTH, 6 * D_MODEL), 0.02),
        'norm_gains': 1.0 + nrm(ks[6], (DEPTH, 4, D_MODEL), 0.05),
        'w_in': nrm(ks[7], (DEPTH, D_MODEL, IN_WIDTH), D_MODEL ** -0.5),
        'w_out': nrm(ks[8], (DEPTH, MIX_WIDTH, D_MODEL), MIX_WIDTH ** -0.5),
        'gla_a_up': nrm(ks[9], (DEPTH, 2, GLA_RANK, GLA_HEADS * GLA_DK), GLA_RANK ** -0.5),
        'gla_a_bias': 1.0 + nrm(ks[10], (DEPTH, 2, GLA_HEADS * GLA_DK), 0.5),
        'gla_norm': 1.0 + nrm(ks[11], (DEPTH, GLA_DV), 0.05),
        'nat_rpb': nrm(ks[12], (DEPTH, NAT_HEADS, 2 * NAT_WIN_ROWS - 1, 2 * NAT_WIN_COLS - 1), 0.02),
        'swa_sink': nrm(ks[13], (DEPTH, SWA_Q_HEADS), 0.5),
        'w_router': nrm(ks[14], (DEPTH, D_MODEL, N_EXPERTS), D_MODEL ** -0.5),
        'w_gate': nrm(ks[15], (DEPTH, N_EXPERTS, D_MODEL, EXPERT_FF), D_MODEL ** -0.5),
        'w_up': nrm(ks[16], (DEPTH, N_EXPERTS, D_MODEL, EXPERT_FF), D_MODEL ** -0.5),
        'w_down': nrm(ks[17], (DEPTH, N_EXPERTS, EXPERT_FF, D_MODEL), EXPERT_FF ** -0.5),
    }

def reference(x, c, ctx, c_ctx, w_mod, b_mod, norm_gains, w_in, w_out, gla_a_up, gla_a_bias, gla_norm,
              nat_rpb, swa_sink, w_router, w_gate, w_up, w_down):
    xc = ctx
    for l in range(DEPTH):
        update_ctx = l < DEPTH - 1
        mod = jax.nn.silu(c) @ w_mod[l] + b_mod[l]
        mod_c = jax.nn.silu(c_ctx) @ w_mod[l] + b_mod[l]
        sh_a, sc_a, gt_a, sh_f, sc_f, gt_f = jnp.split(mod[:, None, :], 6, axis=-1)
        csh_a, csc_a, cgt_a, csh_f, csc_f, cgt_f = jnp.split(mod_c, 6, axis=-1)
        g_pre_a, g_post_a, g_pre_f, g_post_f = norm_gains[l]

        h = modulate(rms_norm(x, g_pre_a), sh_a, sc_a)
        hc = modulate(rms_norm(xc, g_pre_a), csh_a, csc_a)
        mix, mix_c = token_mixers(h, hc, w_in[l], gla_a_up[l], gla_a_bias[l], gla_norm[l], nat_rpb[l], swa_sink[l], update_ctx)
        x = x + gt_a * rms_norm(mix @ w_out[l], g_post_a)
        if update_ctx:
            xc = xc + cgt_a * rms_norm(mix_c @ w_out[l], g_post_a)

        h = modulate(rms_norm(x, g_pre_f), sh_f, sc_f)
        x = x + gt_f * rms_norm(expert_choice_ffn(h, w_router[l], w_gate[l], w_up[l], w_down[l]), g_post_f)
        if update_ctx:
            hc = modulate(rms_norm(xc, g_pre_f), csh_f, csc_f)
            xc = xc + cgt_f * rms_norm(expert_choice_ffn(hc, w_router[l], w_gate[l], w_up[l], w_down[l]), g_post_f)
    return x


_drawn_inputs = setup_inputs


def setup_inputs(seed=0):
    import zlib

    import numpy as np

    out = dict(_drawn_inputs(seed))
    spreads = {}
    factors = {'nat_rpb': 8.0, 'swa_sink': 8.0}
    for name, (base, spread) in spreads.items():
        noise = np.random.default_rng([zlib.crc32(name.encode()), seed]).standard_normal(out[name].shape)
        drawn = base * np.exp(spread * noise) if base else spread * noise
        out[name] = __import__('jax').numpy.asarray(drawn.astype(out[name].dtype))
    for name, factor in factors.items():
        out[name] = (out[name] * factor).astype(out[name].dtype)
    return out
```

```python
import concourse.bass as bass
from concourse import mybir
from contextlib import ExitStack

P = 128
D = 1024
KC = D // P
LAT, CTX = 512, 256
TOK = LAT + CTX
NLT, NCT = LAT // P, CTX // P
NT = NLT + NCT
DEPTH = 2
GRID_W = 64
NAT_H, SWA_H, GLA_H = 4, 8, 4
NAT_ROWS, NAT_COLS = 8, 16
WINDOW = 128
HD = 64
DK, DV = 32, 64
TAU = 16.0
NE = 16
PAIRS = NE // 2
CAP_L, CAP_C = 2 * LAT // NE, 2 * CTX // NE
EPS = 1e-6
NEG = -1e30
SCALE = HD ** -0.5
UNIT = 4096
RING = 4
MOD_UNITS, IN_UNITS, OUT_UNITS, FFN_UNITS = 12, 5, 2, 6 * NE
CW = CAP_L + CAP_C

MOD_AT = [0, MOD_UNITS + IN_UNITS]
IN_AT = [MOD_UNITS, 2 * MOD_UNITS + IN_UNITS + OUT_UNITS + FFN_UNITS]
OUT_AT = [2 * MOD_UNITS + IN_UNITS, IN_AT[1] + IN_UNITS]
FFN_AT = [OUT_AT[0] + OUT_UNITS, OUT_AT[1] + OUT_UNITS]
N_UNITS = FFN_AT[1] + FFN_UNITS

GK, GQ, NQ, NK, SK, SQ, AL = 0, 1, 2, 4, 6, 7, 11
NFM = 12
HV = HD + 1
TM_GV, TM_NV, TM_SV, TM_GG = 0, 256, 256 + NAT_H * HV, 256 + (NAT_H + 2) * HV
TMW = TM_GG + 256

C_ID, C_MF, C_MB, C_BAND, C_COS, C_SIN, C_ROT, C_HM, C_IOTA = 0, 128, 256, 384, 768, 1280, 1792, 1920, 1924
CONSTS = C_IOTA + NLT
P_BMOD, P_GAIN, P_AUP, P_AB, P_GG, P_SINK = 0, 96, 128, 256, 258, 322
PARAMS = P_SINK + SWA_H


PER = {"z": 2, "z_out": 2, "softplus": 2, "scan": 12, "totc": 2, "ke_arg": 2, "ke_exp": 2, "ke": 2,
       "tot_exp": 1, "keT": 3, "keT_out": 1, "dSm": 10, "dS": 5, "state": 10, "rope": 5, "rot": 5,
       "q_arg": 6, "q_exp": 6, "qk": 6, "gla_ms": 1, "gla_rs": 1, "gate_exp": 1, "gla_o": 1, "router_in": 1,
       "logits": 1, "logit_sub": 1, "logit_exp": 1, "aff": 1, "affT": 1, "picked": 1, "iota": 16, "vones": 1,
       "silu": 32, "yl": 8, "ptok": 8, "sel": 8, "xs": 8, "yt": 32, "bias": 16 * NAT_H * NLT // 4}


PASSES = {"diag": (2, 2, 1, 1),
          "grow": (2, 2, 1, 1),
          "grow_out": (1, 1, 1, 1),
          "psq": (NT, NT, NLT, NLT),
          "prs": (NT, NT, NLT, NLT),
          "y_used": (NT, NT, NLT, NLT),
          "sq": (NT, NT, NT, NLT),
          "xn": (NT, NT, NT, NLT)}


def before(name, l, half):
    return sum(PASSES[name][:2 * l + (half == "f")])


def bass_hybrid_dit(nc, x_all, cvec, consts, iotarow_d, params_d, nat_bias, wstream, xkeep, pick_d, out):
    f32 = mybir.dt.float32
    u32 = mybir.dt.uint32
    ALU = mybir.AluOpType
    ACT = mybir.ActivationFunctionType
    AX = mybir.AxisListType.X
    V, S, T = nc.vector, nc.scalar, nc.tensor

    ctx = ExitStack()
    with ctx:
        def sb(name, n, dt=f32):
            return ctx.enter_context(nc.sbuf_tensor(name, [P, n], dt))

        ring = sb("ring", RING * UNIT)
        hT = sb("hT", KC * TOK)
        big = sb("big", NFM * TOK + NT * TMW)
        cst = sb("cst", CONSTS)
        prm = sb("prm", DEPTH * PARAMS)
        ones = sb("ones", P)
        modc = sb("modc", DEPTH * 96)
        cols = sb("cols", 2 * 2 * 2 * KC)
        gcol = sb("gcol", 2 * KC)
        router = sb("router", P)
        small = sb("small", 2 * 8 + 2 * 8 + 8 + 24 + 24)
        glao = sb("glao", NT * 256)
        work = sb("work", 10752)
        ps = ctx.enter_context(nc.psum_tensor("ps", [P, 8 * 512], f32))

        def bank(b, n=512, at=0):
            return ps[:, b * 512 + at:b * 512 + at + n]

        def v3(ap, a):
            return ap.rearrange("p (a b) -> p a b", a=a)

        ident = cst[:, C_ID:C_ID + P]
        X = v3(big[:, 0:NT * D], NT)
        XN = v3(big[:, NT * D:2 * NT * D], NT)
        GROW = v3(big[:, 2 * NT * D:2 * NT * D + 2 * D], 2)
        FM = v3(big[:, 0:NFM * TOK], NFM)
        TM = v3(big[:, NFM * TOK:], NT)
        hTv = v3(hT[:, :], KC)
        ACC = v3(hT[:, :], NT)
        ringv = v3(ring[:, :], RING)
        colv = cols[:, :].rearrange("p (s w m k) -> p s w m k", s=2, w=2, m=2)
        modv = modc[:, :].rearrange("p (l n w) -> p l n w", l=DEPTH, w=2)
        ss = small[:, 0:12]
        rs = small[:, 16:16 + 12]
        tmp8 = small[:, 32:40]
        gss = small[:, 40:64]
        grs = small[:, 64:88]

        def w(at, n):
            return work[:, at:at + n]

        CUM = [w(0, TOK), w(TOK, TOK)]
        E = [w((2 + i) * TOK, TOK) for i in range(6)]
        STATE = [v3(w(8 * TOK + d * NT * 256, NT * 256), NT) for d in range(2)]
        GX = 8 * TOK + 2 * NT * 256
        KET = v3(w(GX, 12 * P), 12)
        A_SB = w(GX, 512)
        A_TMP = w(GX + 512, 512)
        QBLK = [w(CUM_AT, 512) for CUM_AT in (0, 512)]
        SC = [w(512 * i, 512) for i in range(2)]
        PR = [w(1024 + TOK * i, TOK) for i in range(2)]
        PT = [v3(w(1024 + 2 * TOK + TOK * i, TOK), NT) for i in range(2)]
        MIX = [w(1024 + 4 * TOK + 768 * i, 768) for i in range(2)]
        BIAS = [w(1024 + 4 * TOK + 2 * 768 + 512 * i, 512) for i in range(4)]
        AST = w(1024 + 4 * TOK + 2 * 768 + 2048, 64)
        CS = sb("silu_c", 16)[:, :]
        CTMP = w(16, 32)
        AFMX = sb("route_stats", 16)
        AFM = AFMX[:, :]
        DIAG = [w(0, D), w(D, D)]
        JUNK = w(2 * D, D)
        YT_ = w(3 * D, D)
        at = [0]

        def take(n):
            at[0] += n
            assert at[0] <= 10752
            return w(at[0] - n, n)

        SEL_L, SEL_C = v3(take(512), 4), v3(take(128), 2)
        PT_L, PT_C = take(512), take(256)
        XST = take(KC * 2 * CW).rearrange("p (k e c) -> p k e c", k=KC, e=2)
        HID = take(2 * KC * CW).rearrange("p (e k c) -> p e k c", e=2, k=KC)
        SG = [glao[:, 4 * CW * i:4 * CW * (i + 1)] for i in range(2)]
        YTL, YTC = v3(take(KC * P), KC), v3(take(KC * 64), KC)
        YL, YC = take(D), take(D)
        IDXL, IDXC = take(NE * CAP_L), take(NE * CAP_C)
        IDXLC, VALLC, IDXCC, VALCC = take(PAIRS), take(PAIRS), take(PAIRS), take(PAIRS)
        IOTAR = take(LAT)
        AFF = v3(take(NLT * 48), NLT)
        LOG = v3(take(NT * NE), NT)
        VALS, IDXF = take(CAP_L), take(CAP_L)
        AFT0, AFT1 = YL, YC
        idxu = sb("idxu", CAP_L, u32)

        sems = {}

        def sem(name):
            if name not in sems:
                sems[name] = ctx.enter_context(nc.semaphore(name))
            return sems[name]

        ring_full = [sem(f"ring_full{i}") for i in range(RING)]
        ring_used = [sem(f"ring_used{i}") for i in range(RING)]

        class Chain:

            def __init__(self, eng, name):
                self.eng, self.sem, self.n = eng, sem(name), 0

            def __call__(self, ins):
                self.n += 1
                ins.then_inc(self.sem, 1)
                self.eng.wait_ge(self.sem, self.n)

        def width(l):
            return TOK if l < DEPTH - 1 else LAT

        def tiles(l):
            return [4, 5, 0, 1, 2, 3] if l < DEPTH - 1 else [0, 1, 2, 3]

        def token_parts(l, kv):
            return [(0, LAT)] + ([(LAT, CTX)] if kv or l < DEPTH - 1 else [])

        def fm_items(l, unit):
            blocks = {0: [GK, AL, GQ, SK], 3: [NK, NK + 1, NQ, NQ + 1], 4: [SQ, SQ + 1, SQ + 2, SQ + 3]}[unit]
            return [(j, b, t0, n) for j, b in enumerate(blocks)
                    for t0, n in token_parts(l, b in (GK, AL, SK, NK, NK + 1))]

        def n_items(l, upto):
            return sum(NT if u in (1, 2) else len(fm_items(l, u)) for u in range(upto))

        def units(l):
            out_ = []
            for ti, t in enumerate(tiles(l)):
                for kind, h in [("n", h) for h in range(NAT_H)] + [("s", h) for h in range(SWA_H)]:
                    out_.append((ti, t, kind, h))
            return out_

        UPT = NAT_H + SWA_H

        def local_keys(t, kind):
            if t >= NLT:
                return 0, 0
            if kind == "n":
                return 0, LAT
            a, b = max(t - 1, 0), min(t + 2, NLT)
            return a * P, (b - a) * P

        F_ORD, B_ORD = [4, 5, 0, 1, 2, 3], [5, 4, 3, 2, 1, 0]

        def cw(l):
            return CW if l < DEPTH - 1 else CAP_L

        def acc_total(l):
            return 4 + PAIRS * 2 * len(tiles(l))

        block = ctx.enter_context(nc.Block())

        @block.sync
        def _(sp):
            for s in range(RING):
                sp.dma_start(ringv[:, s, :], wstream[s, :, :]).then_inc(ring_full[s], 16)
            with sp.Fori(1, N_UNITS // RING) as g:
                for s in range(RING):
                    sp.wait_ge(ring_used[s], g)
                    sp.dma_start(ringv[:, s, :], wstream[g * RING + s, :, :]).then_inc(ring_full[s], 16)
            for n in range(N_UNITS // RING * RING, N_UNITS):
                sp.wait_ge(ring_used[n % RING], n // RING)
                sp.dma_start(ringv[:, n % RING, :], wstream[n, :, :]).then_inc(ring_full[n % RING], 16)

        @block.gpsimd
        def _(pool):
            pool.dma_start(cst[:, :], consts).then_inc(sem("const_in"), 16)
            pool.dma_start(v3(prm[:, :], DEPTH), params_d.rearrange("l p c -> p l c")).then_inc(sem("param_in"), 16)
            pool.dma_start(CS, cvec).then_inc(sem("c_in"), 16)
            pool.dma_start(X, x_all.rearrange("(t p) d -> p t d", p=P)).then_inc(sem("x_in"), 16)
            pool.memset(ones[:, :], 1.0).then_inc(sem("ones_set"), 1)
            for l in range(DEPTH):
                us = units(l)
                if l:
                    for t in range(NLT):
                        pool.wait_ge(sem(f"x_ready{l}"), t + 1)
                        pool.dma_start(xkeep[t * P:(t + 1) * P, :], X[:, t, :]).then_inc(sem("x_kept"), 16)
                pool.wait_ge(sem(f"h_t{l}a"), 2 * KC)
                for t in range(NT):
                    m = pool.memset(TM[:, t, TM_NV:TM_GG].rearrange("p (h v) -> p h v", v=HV)[:, :, HD:HV], 1.0)
                m.then_inc(sem("vones"), 1)
                n = 0
                pool.wait_ge(sem("gla_o"), 1 + l * PER["gla_o"])
                stts = [u for u, x in enumerate(us) if x[2] == "n" and x[1] < NLT]
                for n, u in enumerate(stts):
                    if n >= 4:
                        pool.wait_ge(sem(f"max{l}"), stts[n - 4] + 1)
                    pool.dma_start(BIAS[n % 4], nat_bias[l, us[u][1], us[u][3], :, :]).then_inc(sem(f"bias{n % 4}"), 16)
                pool.wait_ge(sem(f"pv{l}"), len(us))
                for t in tiles(l):
                    src = x_all if l == 0 else xkeep
                    pool.dma_start(X[:, t, :], src[t * P:(t + 1) * P, :]).then_inc(sem(f"x_back{t}"), 16)
                pool.wait_ge(sem("logits"), 1 + l * PER["logits"])
                for t in tiles(l):
                    pool.memset(ACC[:, t, :], 0.0).then_inc(sem(f"acc_zero{l}"), 1)
                pool.dma_start(IOTAR, iotarow_d).then_inc(sem("iota"), 16)
                pool.wait_ge(sem("picked"), 1 + l * PER["picked"])
                k = 0
                ctx_too = l < DEPTH - 1
                for i, src in enumerate((IDXF, VALS)):
                    pool.dma_start(pick_d[l, i, 0, :].rearrange("(e r) -> e r", r=CAP_L), src[0:NE, :])\
                        .then_inc(sem(f"pick_out{l}"), 16)
                    k += 16
                    if ctx_too:
                        pool.dma_start(pick_d[l, i, 1, 0:NE * CAP_C].rearrange("(e r) -> e r", r=CAP_C),
                                       src[32:32 + NE, 0:CAP_C]).then_inc(sem(f"pick_out{l}"), 16)
                        k += 16
                pool.wait_ge(sem(f"pick_out{l}"), k)
                pool.dma_start(IDXL, pick_d[l, 0, 0, :].partition_broadcast(P)).then_inc(sem(f"pick_in{l}"), 16)
                with nc.allow_non_contiguous_dma(reason="slot columns"):
                    for i, dst in enumerate((IDXLC, VALLC)):
                        pool.dma_start(dst, pick_d[l, i, 0, :].rearrange("(a p) -> p a", p=P)).then_inc(sem(f"pick_in{l}"), 16)
                    if ctx_too:
                        pool.dma_start(IDXC, pick_d[l, 0, 1, 0:NE * CAP_C].partition_broadcast(P)).then_inc(sem(f"pick_in{l}"), 16)
                        for i, dst in enumerate((IDXCC, VALCC)):
                            pool.dma_start(dst[0:64, :], pick_d[l, i, 1, 0:NE * CAP_C].rearrange("(a p) -> p a", p=64))\
                                .then_inc(sem(f"pick_in{l}"), 16)
            for t in range(NLT):
                pool.wait_ge(sem(f"x_ready{DEPTH}"), t + 1)
                pool.dma_start(out[t * P:(t + 1) * P, :], X[:, t, :]).then_inc(sem("stored"), 16)
            pool.wait_ge(sem("stored"), 16 * NLT)

        def picks(l):
            return 16 * (6 if l < DEPTH - 1 else 3)

        @block.scalar
        def _(act):
            chain = Chain(act, "act_chain")
            act.wait_ge(sem("c_in"), 16)
            S.activation(CTMP[:, 0:16], CS, ACT.Exp, scale=-1.0).then_inc(sem("c_exp"), 1)

            def norm_rows(l, half):
                ts = range(NT) if half == "a" else tiles(l)
                for i, t in enumerate(ts):
                    if half == "a":
                        if l == 0:
                            act.wait_ge(sem("x_in"), 16)
                        elif t < NLT:
                            act.wait_ge(sem(f"x_ready{l}"), t + 1)
                        else:
                            act.wait_ge(sem(f"xc_ready{l}"), t - NLT + 1)
                    else:
                        act.wait_ge(sem(f"x_mid{l}"), i + 1)
                    S.activation(XN[:, t, :], X[:, t, :], ACT.Square, accum_out=ss[:, t:t + 1])\
                        .then_inc(sem("sq"), 1)
                    act.wait_ge(sem("sq"), i + 1 + before("sq", l, half))
                    chain(S.activation(rs[:, t:t + 1], ss[:, t:t + 1], ACT.Ln, scale=1.0 / D, bias=EPS))
                    chain(S.activation(rs[:, t:t + 1], rs[:, t:t + 1], ACT.Exp, scale=-0.5))
                    S.activation(XN[:, t, :], X[:, t, :], ACT.Copy, scale=rs[:, t:t + 1]).then_inc(sem("xn"), 1)

            def project_out(l, unit, parts):
                n = n_items(l, unit)
                for dst, b, k, shape in parts:
                    act.wait_ge(sem(f"proj{l}"), n + 1)
                    S.activation(dst, shape(bank(n % 4, k)), ACT.Copy).then_inc(sem(f"proj_out{l}"), 1)
                    n += 1

            def fm_parts(l, unit):
                return [(FM[0:48 if b == AL else P, b, t0:t0 + n], b, n,
                         (lambda ap, b=b: ap[0:48 if b == AL else P, :])) for j, b, t0, n in fm_items(l, unit)]

            def gla_exps(l):
                for d in range(2):
                    act.wait_ge(sem("z_out"), d + 1 + l * PER["z_out"])
                    chain(S.activation(E[2 + d], E[d], ACT.Abs))
                    chain(S.activation(E[2 + d], E[2 + d], ACT.Exp, scale=-1.0))
                    S.activation(E[2 + d], E[2 + d], ACT.Ln, bias=1.0).then_inc(sem("softplus"), 1)

            def gla_keys(l):
                for d in range(2):
                    act.wait_ge(sem("ke_arg"), d + 1 + l * PER["ke_arg"])
                    S.activation(E[d], E[d], ACT.Exp).then_inc(sem("ke_exp"), 1)
                act.wait_ge(sem("totc"), 2 + l * PER["totc"])
                S.activation(grs[:, 0:12], gss[:, 0:12], ACT.Exp).then_inc(sem("tot_exp"), 1)
                act.wait_ge(sem("keT"), 3 + l * PER["keT"])
                S.activation(w(GX, 12 * P), ps[:, 4 * 512:4 * 512 + 12 * P], ACT.Copy).then_inc(sem("keT_out"), 1)

            def gla_queries(l):
                n = width(l)
                for d in range(2):
                    for i in range(3):
                        act.wait_ge(sem("q_arg"), 3 * d + i + 1 + l * PER["q_arg"])
                        S.activation(E[3 * d + i][:, 0:n], E[3 * d + i][:, 0:n], ACT.Exp).then_inc(sem("q_exp"), 1)

            def gla_gate(l):
                n = width(l) // P
                act.wait_ge(sem("gla_ms"), 1 + l * PER["gla_ms"])
                chain(S.activation(grs[:, 0:4 * n], gss[:, 0:4 * n], ACT.Ln, scale=1.0 / DV, bias=EPS))
                S.activation(grs[:, 0:4 * n], grs[:, 0:4 * n], ACT.Exp, scale=-0.5).then_inc(sem("gla_rs"), 1)
                act.wait_ge(sem(f"proj_out{l}"), n_items(l, 3))
                S.activation(v3(w(0, n * 256), n), TM[:, 0:n, TM_GG:TM_GG + 256], ACT.Exp, scale=-1.0)\
                    .then_inc(sem("gate_exp"), 1)

            def attend(l):
                us = units(l)
                for u in range(len(us) + 3):
                    if u < len(us):
                        ti, t, kind, h = us[u]
                        k0, nl = local_keys(t, kind)
                        act.wait_ge(sem(f"max{l}"), u + 1)
                        if u >= 2:
                            act.wait_ge(sem(f"T{l}"), u - 1)
                        nm = AST[:, 8 * (u % 2) + 2:8 * (u % 2) + 3]
                        if nl:
                            S.activation(PR[u % 2][:, 0:nl], SC[u % 2][:, 0:nl], ACT.Exp, bias=nm)
                        if kind == "s":
                            es = AST[:, 16 + u % 4:17 + u % 4]
                            orig = h // 2 + 4 * (h % 2)
                            S.activation(es, prm[:, l * PARAMS + P_SINK + orig:l * PARAMS + P_SINK + orig + 1], ACT.Exp, bias=nm)
                        S.activation(PR[u % 2][:, nl:nl + CTX], bank(2 * (u % 2) + 1, CTX), ACT.Exp, bias=nm,
                                     scale=SCALE).then_inc(sem(f"exp{l}"), 1)
                    v = u - 1
                    if 0 <= v < len(us):
                        nk = (local_keys(us[v][1], us[v][2])[1] + CTX) // P
                        act.wait_ge(sem(f"T{l}"), v + 1)
                        if v >= 2:
                            act.wait_ge(sem(f"pv{l}"), v - 1)
                        S.activation(work[:, 1024 + 2 * TOK + TOK * (v % 2):1024 + 2 * TOK + TOK * (v % 2) + nk * P],
                                     ps[:, 4 * 512:4 * 512 + nk * P], ACT.Copy).then_inc(sem(f"pt_out{l}"), 1)
                    v = u - 3
                    if v >= 0 and v % UPT == UPT - 1:
                        t = us[v][1]
                        act.wait_ge(sem(f"mixT{l}"), v // UPT + 1)
                        S.activation(hTv[:, :, t * P:(t + 1) * P], v3(ps[:, 4 * 512:6 * 512], KC), ACT.Copy)\
                            .then_inc(sem(f"mixT_out{l}"), 1)

            def gate_rows(l, half):
                ctx_too = l < DEPTH - 1
                act.wait_ge(sem("grow"), (2 if ctx_too else 1) + before("grow", l, half))
                n = 2 if ctx_too else 1
                S.activation(big[:, 2 * NT * D:2 * NT * D + n * D], ps[:, 4 * 512:4 * 512 + n * D], ACT.Copy)\
                    .then_inc(sem("grow_out"), 1)

            def post(l, half):
                for i, t in enumerate(tiles(l)):
                    if half == "a":
                        act.wait_ge(sem(f"wo{l}"), i + 1)
                        src = ps[:, (i % 2) * D:(i % 2) * D + D]
                    else:
                        act.wait_ge(sem(f"acc{l}"), acc_total(l))
                        src = ACC[:, t, :]
                    S.activation(JUNK, src, ACT.Square, accum_out=ss[:, t:t + 1]).then_inc(sem("psq"), 1)
                    act.wait_ge(sem("psq"), i + 1 + before("psq", l, half))
                    chain(S.activation(rs[:, t:t + 1], ss[:, t:t + 1], ACT.Ln, scale=1.0 / D, bias=EPS))
                    S.activation(rs[:, t:t + 1], rs[:, t:t + 1], ACT.Exp, scale=-0.5).then_inc(sem("prs"), 1)

            def ffn(l):
                ctx_too = l < DEPTH - 1
                base = FFN_AT[l]
                nt = len(tiles(l))
                act.wait_ge(sem("logit_sub"), 1 + l * PER["logit_sub"])
                S.activation(LOG[:, 0:nt, :], LOG[:, 0:nt, :], ACT.Exp).then_inc(sem("logit_exp"), 1)
                with act.Fori(0, PAIRS) as i:
                    for g in range(2):
                        act.wait_ge(sem(f"gather{l}"), i * 3 + (g + 1) if ctx_too else i * 2 + (g + 1))
                        for k in range(4):
                            last = S.activation(XST[:, 4 * g + k, :, 0:CAP_L], v3(bank(6 + g, P, k * P), 2), ACT.Identity,
                                                scale=colv[:, 1, 0, 0, 4 * g + k:4 * g + k + 1],
                                                bias=colv[:, 1, 0, 1, 4 * g + k:4 * g + k + 1])
                    last.then_inc(sem("xs"), 1)
                    for e in range(2):
                        u0 = base + 6 * e
                        for h in range(2):
                            n = u0 + 2 * h
                            act.wait_ge(ring_used[n % RING], i * 3 + (n // RING + 1))
                            S.activation(v3(SG[h], 4)[:, :, 0:cw(l)], v3(bank(2 * h, 4 * CW), 4)[:, :, 0:cw(l)], ACT.Silu)\
                                .then_inc(sem("silu"), 1)
                        for d in range(2):
                            n = u0 + 4 + d
                            act.wait_ge(ring_used[n % RING], i * 3 + (n // RING + 1))
                            y = v3(bank(4 + d, 4 * CW), 4)
                            last = S.activation(YTL[:, 4 * d:4 * d + 4, e * CAP_L:(e + 1) * CAP_L], y[:, :, 0:CAP_L], ACT.Copy)
                            if ctx_too:
                                last = S.activation(YTC[:, 4 * d:4 * d + 4, e * CAP_C:(e + 1) * CAP_C], y[:, :, CAP_L:CW], ACT.Copy)
                            last.then_inc(sem("yt"), 1)
                    if ctx_too:
                        act.wait_ge(sem(f"yturn{l}"), i * 2 + 2)
                        S.activation(YC[0:64, :], ps[0:64, 0:D], ACT.Copy).then_inc(sem(f"yc{l}"), 1)

            for l in range(DEPTH):
                norm_rows(l, "a")
                if l:
                    act.wait_ge(sem("x_kept"), 16 * NLT)
                project_out(l, 0, fm_parts(l, 0))
                n = n_items(l, 1)
                act.wait_ge(sem("vones"), 1 + l * PER["vones"])
                for t in range(NT):
                    act.wait_ge(sem(f"proj{l}"), n + 1)
                    S.activation(TM[:, t, TM_GV:TM_GV + 256], bank(n % 4, 256), ACT.Copy)
                    S.activation(TM[:, t, TM_NV:TM_SV].rearrange("p (h v) -> p h v", v=HV)[:, :, 0:HD],
                                 v3(bank(n % 4, 256, 256), NAT_H), ACT.Copy).then_inc(sem(f"proj_out{l}"), 1)
                    n += 1
                gla_exps(l)
                ru = IN_AT[l] + 2
                act.wait_ge(ring_full[ru % RING], 16 * (ru // RING + 1))
                S.activation(router[:, :], ringv[:, ru % RING, KC * 384:KC * 400], ACT.Copy).then_inc(sem("router_in"), 1)
                gg = width(l) // P
                for t in range(NT):
                    act.wait_ge(sem(f"proj{l}"), n + 1)
                    last = S.activation(TM[:, t, TM_SV:TM_GG].rearrange("p (h v) -> p h v", v=HV)[:, :, 0:HD],
                                        v3(bank(n % 4, P), 2), ACT.Copy)
                    if t < gg:
                        last = S.activation(TM[:, t, TM_GG:TMW], bank(n % 4, 256, P), ACT.Copy)
                    last.then_inc(sem(f"proj_out{l}"), 1)
                    n += 1
                project_out(l, 3, fm_parts(l, 3))
                gla_keys(l)
                project_out(l, 4, fm_parts(l, 4))
                gla_queries(l)
                gla_gate(l)
                attend(l)
                gate_rows(l, "a")
                post(l, "a")
                norm_rows(l, "f")
                ffn(l)
                gate_rows(l, "f")
                post(l, "f")

        @block.vector
        def _(dve):
            link = Chain(dve, "dve_chain")
            dve.wait_ge(sem("c_in"), 16)
            dve.wait_ge(sem("c_exp"), 1)
            link(V.tensor_scalar(CTMP[:, 0:16], CTMP[:, 0:16], 1.0, None, ALU.add))
            link(V.reciprocal(CTMP[:, 0:16], CTMP[:, 0:16]))
            V.tensor_tensor(CS, CS, CTMP[:, 0:16], ALU.mult).then_inc(sem("silu_c"), 1)

            def mod_out(l):
                n = MOD_AT[l] + MOD_UNITS - 1
                dve.wait_ge(sem("param_in"), 16)
                dve.wait_ge(ring_used[n % RING], n // RING + 1)
                V.tensor_tensor(modc[:, l * 96:(l + 1) * 96], bank(7, 96, 128),
                                prm[:, l * PARAMS + P_BMOD:l * PARAMS + P_BMOD + 96], ALU.add).then_inc(sem(f"mod{l}_out"), 1)
                dve.wait_ge(sem(f"mod{l}_out"), 1)

            def mod_cols(l):
                for s in range(2):
                    gain = prm[:, l * PARAMS + P_GAIN + 16 * s:l * PARAMS + P_GAIN + 16 * s + KC]
                    for wch in range(2):
                        sh = modv[:, l, 24 * s:24 * s + 8, wch]
                        sc = modv[:, l, 24 * s + 8:24 * s + 16, wch]
                        V.scalar_tensor_tensor(colv[:, s, wch, 0, :], sc, 1.0, gain, ALU.add, ALU.mult)
                        link(V.tensor_copy(colv[:, s, wch, 1, :], sh))

            def h_out(l, half):
                s = 0 if half == "a" else 1
                ctx_too = half == "a" or l < DEPTH - 1
                for k in range(KC):
                    for wch, (t0, n) in enumerate([(0, LAT), (LAT, CTX)][:2 if ctx_too else 1]):
                        dve.wait_ge(sem(f"xT{l}{half}"), (2 if ctx_too else 1) * k + wch + 1)
                        V.tensor_scalar(hTv[:, k, t0:t0 + n], bank(2 * (k % 2) + wch, n), colv[:, s, wch, 0, k:k + 1],
                                        colv[:, s, wch, 1, k:k + 1], ALU.mult, ALU.add).then_inc(sem(f"h_t{l}{half}"), 1)

            def gla_decay(l):
                p0 = l * PARAMS
                for d in range(2):
                    dve.wait_ge(sem("z"), d + 1 + l * PER["z"])
                    bias = prm[:, p0 + P_AB + d:p0 + P_AB + d + 1]
                    V.tensor_scalar(E[d][:, 0:LAT], bank(4 + d), bias, None, ALU.add)
                    V.tensor_scalar(E[d][:, LAT:TOK], bank(6 + d, CTX), bias, None, ALU.add).then_inc(sem("z_out"), 1)
                for d in range(2):
                    dve.wait_ge(sem("softplus"), d + 1 + l * PER["softplus"])
                    link(V.tensor_scalar(E[d], E[d], 0.0, 1.0 / TAU, ALU.min, ALU.mult))
                    link(V.scalar_tensor_tensor(E[d], E[2 + d], -1.0 / TAU, E[d], ALU.mult, ALU.add))
                    for t in range(NT):
                        c = slice(t * P, (t + 1) * P)
                        V.tensor_tensor_scan(CUM[d][:, c], ones[:, :], E[d][:, c], 0.0, ALU.mult, ALU.add)\
                            .then_inc(sem("scan"), 1)
                    dve.wait_ge(sem("scan"), NT * (d + 1) + l * PER["scan"])
                c3 = [v3(CUM[d], NT) for d in range(2)]
                for d in range(2):
                    V.tensor_copy(v3(gss[:, 6 * d:6 * d + 6], NT), c3[d][:, :, P - 1:P]).then_inc(sem("totc"), 1)
                dve.wait_ge(sem("totc"), 2 + l * PER["totc"])
                tot_b = gss[:, 6:12].unsqueeze(2).broadcast_to([P, NT, P])
                link(V.tensor_tensor(c3[1], tot_b, c3[1], ALU.subtract))
                link(V.tensor_tensor(CUM[1], CUM[1], E[1], ALU.add))
                for d in range(2):
                    tot = gss[:, 6 * d:6 * d + 6].unsqueeze(2).broadcast_to([P, NT, P])
                    V.tensor_tensor(v3(E[d], NT), tot, c3[d], ALU.subtract).then_inc(sem("ke_arg"), 1)

            def gla_state(l):
                dve.wait_ge(sem(f"proj_out{l}"), 2)
                for d in range(2):
                    dve.wait_ge(sem("ke_exp"), d + 1 + l * PER["ke_exp"])
                    V.tensor_tensor(E[d], E[d], FM[:, GK, :], ALU.mult).then_inc(sem("ke"), 1)
                V.memset(STATE[0][:, F_ORD[0], :], 0.0)
                link(V.memset(STATE[1][:, B_ORD[0], :], 0.0))
                dve.wait_ge(sem("tot_exp"), 1 + l * PER["tot_exp"])
                hm = cst[:, C_HM:C_HM + GLA_H]
                for i in range(NT - 1):
                    dve.wait_ge(sem("dS"), i + 1 + l * PER["dS"])
                    hmb = hm.unsqueeze(2).broadcast_to([P, GLA_H, DV])
                    for d, order in enumerate((F_ORD, B_ORD)):
                        V.tensor_tensor(v3(bank(4 + i % 2, 256, 256 * d), GLA_H), v3(bank(4 + i % 2, 256, 256 * d), GLA_H), hmb,
                                        ALU.mult).then_inc(sem("dSm"), 1)
                    dve.wait_ge(sem("dSm"), 2 * i + 2 + l * PER["dSm"])
                    for d, order in enumerate((F_ORD, B_ORD)):
                        a, b = order[i], order[i + 1]
                        V.scalar_tensor_tensor(STATE[d][:, b, :], STATE[d][:, a, :], grs[:, 6 * d + a:6 * d + a + 1],
                                               bank(4 + i % 2, 256, 256 * d), ALU.mult, ALU.add).then_inc(sem("state"), 1)
                    dve.wait_ge(sem("state"), 2 * i + 2 + l * PER["state"])

            def rope(l):
                for i, b in enumerate([SK, SQ, SQ + 1, SQ + 2, SQ + 3]):
                    dve.wait_ge(sem("rot"), i + 1 + l * PER["rot"])
                    V.tensor_tensor(A_TMP, bank(6 + i % 2), cst[:, C_SIN:C_SIN + LAT], ALU.mult)
                    link(V.tensor_tensor(FM[:, b, 0:LAT], FM[:, b, 0:LAT], cst[:, C_COS:C_COS + LAT], ALU.mult))
                    V.tensor_tensor(FM[:, b, 0:LAT], FM[:, b, 0:LAT], A_TMP, ALU.add).then_inc(sem("rope"), 1)
                    dve.wait_ge(sem("rope"), i + 1 + l * PER["rope"])

            def gla_queries(l):
                n = width(l)
                nt = n // P
                dve.wait_ge(sem("keT"), 3 + l * PER["keT"])
                for d in range(2):
                    c3 = v3(CUM[d], NT)[:, 0:nt, :]
                    mid = c3[:, :, P // 2:P // 2 + 1].broadcast_to([P, nt, P])
                    link(V.tensor_tensor(v3(E[3 * d + 2][:, 0:n], nt), c3, mid, ALU.subtract))
                    V.tensor_scalar(E[3 * d][:, 0:n], E[3 * d + 2][:, 0:n], 80.0, None, ALU.min).then_inc(sem("q_arg"), 1)
                    V.tensor_scalar(E[3 * d + 1][:, 0:n], E[3 * d + 2][:, 0:n], -80.0, -1.0, ALU.max, ALU.mult)\
                        .then_inc(sem("q_arg"), 1)
                    dve.wait_ge(sem("q_arg"), 3 * d + 2 + l * PER["q_arg"])
                    V.tensor_copy(E[3 * d + 2][:, 0:n], CUM[d][:, 0:n]).then_inc(sem("q_arg"), 1)
                dve.wait_ge(sem("q_arg"), 6 + l * PER["q_arg"])
                q = FM[:, GQ, 0:n]
                for d in range(2):
                    for i in range(3):
                        dve.wait_ge(sem("q_exp"), 3 * d + i + 1 + l * PER["q_exp"])
                        src = FM[:, GK, 0:n] if i == 1 else q
                        V.scalar_tensor_tensor(E[3 * d + i][:, 0:n], E[3 * d + i][:, 0:n], 1.0 if i == 1 else DK ** -0.5,
                                               src, ALU.mult, ALU.mult).then_inc(sem("qk"), 1)
                dve.wait_ge(sem("qk"), 6 + l * PER["qk"])

            def gla_out(l):
                hmb = cst[:, C_HM:C_HM + GLA_H].unsqueeze(2).broadcast_to([P, GLA_H, P])
                ts = tiles(l)
                for i, t in enumerate(ts):
                    c = slice(t * P, (t + 1) * P)
                    if i:
                        dve.wait_ge(sem(f"scores{l}"), i)
                    for d in range(2):
                        V.tensor_tensor(v3(QBLK[d], GLA_H), E[3 * d][:, c].unsqueeze(1).broadcast_to([P, GLA_H, P]), hmb,
                                        ALU.mult).then_inc(sem(f"qblk{l}"), 1)
                    dve.wait_ge(sem(f"scores{l}"), i + 1)
                    if i:
                        dve.wait_ge(sem(f"o{l}"), i)
                    for d, (m, dst) in enumerate(((C_MF, A_SB), (C_MB, A_TMP))):
                        link(V.tensor_tensor(v3(dst, GLA_H), v3(bank(4 + d), GLA_H),
                                             cst[:, m:m + P].unsqueeze(1).broadcast_to([P, GLA_H, P]), ALU.mult))
                    V.tensor_tensor(A_SB, A_SB, A_TMP, ALU.add).then_inc(sem(f"A{l}"), 1)
                    dve.wait_ge(sem(f"o{l}"), i + 1)
                    V.tensor_copy(glao[:, t * 256:(t + 1) * 256], bank(6 + i % 2, 256)).then_inc(sem(f"o_out{l}"), 1)
                nt = len(ts)
                n = nt * 256
                dve.wait_ge(sem(f"o_out{l}"), nt)
                sq = w(2048, n)
                link(V.tensor_tensor(sq, glao[:, 0:n], glao[:, 0:n], ALU.mult))
                V.reduce_sum(gss[:, 0:4 * nt], v3(sq, 4 * nt), AX).then_inc(sem("gla_ms"), 1)
                dve.wait_ge(sem("gla_rs"), 1 + l * PER["gla_rs"])
                dve.wait_ge(sem("gate_exp"), 1 + l * PER["gate_exp"])
                link(V.tensor_scalar(w(0, n), w(0, n), 1.0, None, ALU.add))
                link(V.reciprocal(w(0, n), w(0, n)))
                link(V.tensor_tensor(v3(w(0, n), nt), v3(w(0, n), nt), TM[:, 0:nt, TM_GG:TMW], ALU.mult))
                g0 = l * PARAMS + P_GG
                link(V.tensor_tensor(v3(w(0, n), 4 * nt), v3(w(0, n), 4 * nt),
                                     prm[:, g0:g0 + DV].unsqueeze(1).broadcast_to([P, 4 * nt, DV]), ALU.mult))
                link(V.tensor_tensor(v3(glao[:, 0:n], 4 * nt), v3(glao[:, 0:n], 4 * nt),
                                     grs[:, 0:4 * nt].unsqueeze(2).broadcast_to([P, 4 * nt, DV]), ALU.mult))
                V.tensor_tensor(glao[:, 0:n], glao[:, 0:n], w(0, n), ALU.mult).then_inc(sem("gla_o"), 1)
                dve.wait_ge(sem("gla_o"), 1 + l * PER["gla_o"])

            def attend(l):
                us = units(l)
                nb = 0
                for u in range(len(us) + 2):
                    if u < len(us):
                        ti, t, kind, h = us[u]
                        k0, nl = local_keys(t, kind)
                        dve.wait_ge(sem(f"s{l}"), u + 1)
                        if u >= 2:
                            dve.wait_ge(sem(f"exp{l}"), u - 1)
                        st = AST[:, 8 * (u % 2):8 * (u % 2) + 8]
                        if nl:
                            if kind == "n":
                                dve.wait_ge(sem(f"bias{nb % 4}"), 16 * (nb // 4 + 1) + l * PER["bias"])
                                add = BIAS[nb % 4]
                                nb += 1
                            else:
                                off = C_BAND + (P if t == 0 else 0)
                                add = cst[:, off:off + nl]
                            V.reduce_max(st[:, 1:2], bank(2 * (u % 2) + 1, CTX), AX)
                            link(V.scalar_tensor_tensor(SC[u % 2][:, 0:nl], bank(2 * (u % 2), nl), SCALE, add[:, 0:nl], ALU.mult, ALU.add))
                            link(V.reduce_max(st[:, 0:1], SC[u % 2][:, 0:nl], AX))
                            link(V.tensor_scalar(st[:, 3:4], st[:, 1:2], SCALE, st[:, 0:1], ALU.mult, ALU.max))
                        else:
                            link(V.reduce_max(st[:, 1:2], bank(2 * (u % 2) + 1, CTX), AX))
                            link(V.tensor_scalar(st[:, 3:4], st[:, 1:2], SCALE, None, ALU.mult))
                        if kind == "s":
                            orig = h // 2 + 4 * (h % 2)
                            sink = prm[:, l * PARAMS + P_SINK + orig:l * PARAMS + P_SINK + orig + 1]
                            V.tensor_scalar(st[:, 2:3], st[:, 3:4], sink, -1.0, ALU.max, ALU.mult).then_inc(sem(f"max{l}"), 1)
                        else:
                            V.tensor_scalar(st[:, 2:3], st[:, 3:4], -1.0, None, ALU.mult).then_inc(sem(f"max{l}"), 1)
                    v = u - 2
                    if 0 <= v < len(us):
                        ti, t, kind, h = us[v]
                        dve.wait_ge(sem(f"pv{l}"), v + 1)
                        if v % UPT == 0 and ti >= 2:
                            dve.wait_ge(sem(f"mixT{l}"), ti - 1)
                        o = bank(6 + v % 2, HV)
                        dn = AST[:, 20:21]
                        if kind == "s":
                            link(V.tensor_tensor(dn, o[:, HD:HV], AST[:, 16 + v % 4:17 + v % 4], ALU.add))
                            link(V.reciprocal(AST[:, 21:22], dn))
                            c = 256 + 64 * (h // 2 + 4 * (h % 2))
                        else:
                            link(V.reciprocal(AST[:, 21:22], o[:, HD:HV]))
                            c = 64 * h
                        V.tensor_scalar(MIX[ti % 2][:, c:c + HD], o[:, 0:HD], AST[:, 21:22], None, ALU.mult).then_inc(sem(f"norm{l}"), 1)

            def gate_rows(l, half):
                s = 0 if half == "a" else 1
                if half == "a":
                    dve.wait_ge(sem(f"pv{l}"), len(units(l)))
                for wch in range(2 if l < DEPTH - 1 else 1):
                    g0 = l * PARAMS + P_GAIN + 16 * s + 8
                    link(V.tensor_tensor(gcol[:, 8 * wch:8 * wch + 8], modv[:, l, 24 * s + 16:24 * s + 24, wch], prm[:, g0:g0 + KC], ALU.mult))
                    V.tensor_tensor(v3(DIAG[wch], KC), ident.unsqueeze(1).broadcast_to([P, KC, P]),
                                    gcol[:, 8 * wch:8 * wch + 8].unsqueeze(2).broadcast_to([P, KC, P]), ALU.mult)\
                        .then_inc(sem("diag"), 1)

            def post(l, half):
                dve.wait_ge(sem("grow_out"), 1 + before("grow_out", l, half))
                for i, t in enumerate(tiles(l)):
                    dve.wait_ge(sem("prs"), i + 1 + before("prs", l, half))
                    src = ps[:, (i % 2) * D:(i % 2) * D + D] if half == "a" else ACC[:, t, :]
                    V.scalar_tensor_tensor(YT_, src, rs[:, t:t + 1], GROW[:, 0 if t < NLT else 1, :], ALU.mult, ALU.mult)\
                        .then_inc(sem("y_used"), 1)
                    dve.wait_ge(sem("y_used"), i + 1 + before("y_used", l, half))
                    if half == "a":
                        dve.wait_ge(sem(f"x_back{t}"), 16 * (l + 1 if t < NLT else 1))
                        name = f"x_mid{l}"
                    else:
                        name = f"x_ready{l + 1}" if t < NLT else f"xc_ready{l + 1}"
                    V.tensor_tensor(X[:, t, :], X[:, t, :], YT_, ALU.add).then_inc(sem(name), 1)
                    if half == "a":
                        dve.wait_ge(sem(name), i + 1)
                    else:
                        dve.wait_ge(sem(name), (t if t < NLT else t - NLT) + 1)

            def route(l):
                nt = len(tiles(l))
                ctx_too = l < DEPTH - 1
                dve.wait_ge(sem("logits"), 1 + l * PER["logits"])
                lg = v3(bank(6, NT * NE), NT)[:, 0:nt, :]
                st = AFM
                link(V.reduce_max(st[:, 0:nt], lg, AX))
                V.tensor_tensor(LOG[:, 0:nt, :], lg, st[:, 0:nt].unsqueeze(2).broadcast_to([P, nt, NE]), ALU.subtract)\
                    .then_inc(sem("logit_sub"), 1)
                link(V.memset(AFF, -1.0))
                dve.wait_ge(sem("logit_exp"), 1 + l * PER["logit_exp"])
                link(V.reduce_sum(st[:, 8:8 + nt], LOG[:, 0:nt, :], AX))
                link(V.reciprocal(st[:, 8:8 + nt], st[:, 8:8 + nt]))
                if ctx_too:
                    V.tensor_tensor(AFF[:, 0:NCT, 32:48], LOG[:, NLT:NT, :], st[:, 12:14].unsqueeze(2).broadcast_to([P, NCT, NE]), ALU.mult)
                V.tensor_tensor(AFF[:, :, 0:NE], LOG[:, 0:NLT, :], st[:, 8:12].unsqueeze(2).broadcast_to([P, NLT, NE]), ALU.mult)\
                    .then_inc(sem("aff"), 1)
                dve.wait_ge(sem("affT"), 1 + l * PER["affT"])
                a = [AFT0[0:48, 0:LAT], AFT1[0:48, 0:LAT]]
                link(V.tensor_copy(a[0], ps[0:48, 7 * 512:8 * 512]))
                for r in range(CAP_L // 8):
                    sl = slice(8 * r, 8 * r + 8)
                    src, dst = a[r % 2], a[(r + 1) % 2]
                    link(V.max(VALS[0:48, sl], src))
                    V.max_index(idxu[0:48, sl], VALS[0:48, sl], src)
                    link(V.match_replace(dst, VALS[0:48, sl], src, -1.0))
                V.tensor_copy(IDXF[0:48, :], idxu[0:48, :]).then_inc(sem("picked"), 1)

            def ffn(l):
                ctx_too = l < DEPTH - 1
                base = FFN_AT[l]
                nt = len(tiles(l))
                per = 2 * nt
                acc = sem(f"acc{l}")
                dve.sem_inc(acc, 4)
                dve.sem_inc(sem(f"hid{l}"), 2)
                dve.wait_ge(sem(f"pick_in{l}"), picks(l))
                dve.wait_ge(sem("iota"), 16 + l * PER["iota"])
                dve.wait_ge(sem(f"acc_zero{l}"), nt)
                with dve.Fori(0, PAIRS) as i:
                    for t in range(NLT):
                        last = V.tensor_scalar(SEL_L[:, t, :], IDXL[:, bass.ts(i, P)], cst[:, C_IOTA + t:C_IOTA + t + 1], None, ALU.is_equal)
                    if ctx_too:
                        for t in range(NCT):
                            last = V.tensor_scalar(SEL_C[:, t, :], IDXC[:, bass.ts(i, 64)], cst[:, C_IOTA + t:C_IOTA + t + 1], None, ALU.is_equal)
                    last.then_inc(sem("sel"), 1)
                    last = V.tensor_scalar(PT_L, IOTAR, IDXLC[:, bass.ds(i, 1)], VALLC[:, bass.ds(i, 1)], ALU.is_equal, ALU.mult)
                    if ctx_too:
                        last = V.tensor_scalar(PT_C[0:64, :], IOTAR[0:64, 0:CTX], IDXCC[0:64, bass.ds(i, 1)], VALCC[0:64, bass.ds(i, 1)],
                                               ALU.is_equal, ALU.mult)
                    last.then_inc(sem("ptok"), 1)
                    if ctx_too:
                        dve.wait_ge(sem(f"gather{l}"), i * 3 + 3)
                        for k in range(KC):
                            last = V.tensor_scalar(XST[:, k, :, CAP_L:CW], v3(bank(4, 64, k * 64), 2), colv[:, 1, 1, 0, k:k + 1],
                                                   colv[:, 1, 1, 1, k:k + 1], ALU.mult, ALU.add)
                        last.then_inc(sem(f"xsc{l}"), 1)
                    for e in range(2):
                        for h in range(2):
                            n = base + 6 * e + 2 * h + 1
                            dve.wait_ge(sem("silu"), i * 4 + (2 * e + h + 1) + l * PER["silu"])
                            dve.wait_ge(ring_used[n % RING], i * 3 + (n // RING + 1))
                            V.tensor_tensor(HID[:, e, 4 * h:4 * h + 4, 0:cw(l)], v3(SG[h], 4)[:, :, 0:cw(l)],
                                            v3(bank(2 * h + 1, 4 * CW), 4)[:, :, 0:cw(l)], ALU.mult).then_inc(sem(f"hid{l}"), 1)
                    dve.wait_ge(sem(f"yturn{l}"), i * (2 if ctx_too else 1) + 1)
                    V.tensor_copy(YL, ps[:, 6 * 512:8 * 512]).then_inc(sem("yl"), 1)
                    dve.wait_ge(acc, i * per + 4)
                    for c in range(per):
                        t, half = tiles(l)[c // 2], c % 2
                        dve.wait_ge(sem(f"comb{l}"), i * per + (c + 1))
                        d = ACC[:, t, half * 512:half * 512 + 512]
                        V.tensor_tensor(d, d, bank((6, 7, 2, 3)[c % 4]), ALU.add).then_inc(acc, 1)

            mod_out(0)
            for l in range(DEPTH):
                mod_cols(l)
                dve.wait_ge(sem("const_in"), 16)
                h_out(l, "a")
                gla_decay(l)
                gla_state(l)
                gla_queries(l)
                rope(l)
                gla_out(l)
                attend(l)
                if l == 0:
                    mod_out(1)
                gate_rows(l, "a")
                post(l, "a")
                h_out(l, "f")
                route(l)
                ffn(l)
                dve.wait_ge(sem(f"acc{l}"), acc_total(l))
                gate_rows(l, "f")
                post(l, "f")

        @block.tensor
        def _(pe):
            def arrived(n):
                pe.wait_ge(ring_full[n % RING], 16 * (n // RING + 1))
                return ringv[:, n % RING, :]

            def mod(l, k):
                n = MOD_AT[l] + k
                u = v3(arrived(n), KC)
                for j in range(4):
                    c = 128 + 2 * (4 * k + j)
                    for kc in range(KC):
                        last = T.matmul(bank(7, 2, c), u[:, kc, j * P:(j + 1) * P],
                                        CS[:, 2 * kc:2 * kc + 2],
                                        start=kc == 0, stop=kc == KC - 1)
                last.then_inc(ring_used[n % RING], 1)

            def turn_x(l, half):
                ctx_too = half == "a" or l < DEPTH - 1
                pe.wait_ge(sem("xn"), (NT if half == "a" else len(tiles(l))) + before("xn", l, half))
                per = 2 if ctx_too else 1
                for k in range(KC):
                    if k >= 2:
                        pe.wait_ge(sem(f"h_t{l}{half}"), per * (k - 1))
                    for wch in range(per):
                        t0 = NLT * wch
                        for t in range(NLT if wch == 0 else NCT):
                            last = T.transpose(bank(2 * (k % 2) + wch, P, t * P), XN[:, t0 + t, k * P:(k + 1) * P], ident)
                        last.then_inc(sem(f"xT{l}{half}"), 1)
                pe.wait_ge(sem(f"h_t{l}{half}"), per * KC)

            def project(l, unit):
                n = n_items(l, unit)
                g = IN_AT[l] + unit
                uw = arrived(g)

                def free(n):
                    if n >= 4:
                        pe.wait_ge(sem(f"proj_out{l}"), n - 3)

                if unit in (1, 2):
                    cols_ = 512 if unit == 1 else 384
                    v = v3(uw[:, 0:KC * cols_], KC)
                    for t in range(NT):
                        free(n)
                        k_ = P if unit == 2 and t * P >= width(l) else cols_
                        for kc in range(KC):
                            last = T.matmul(bank(n % 4, k_), hTv[:, kc, t * P:(t + 1) * P], v[:, kc, 0:k_], start=kc == 0, stop=kc == KC - 1)
                        last.then_inc(sem(f"proj{l}"), 1)
                        n += 1
                    if unit == 2:
                        pe.wait_ge(sem("router_in"), 1 + l * PER["router_in"])
                else:
                    for j, b, t0, tn in fm_items(l, unit):
                        free(n)
                        m = 48 if b == AL else P
                        for kc in range(KC):
                            last = T.matmul(bank(n % 4, tn)[0:m, :], uw[:, j * D + kc * P:j * D + kc * P + m], hTv[:, kc, t0:t0 + tn],
                                            start=kc == 0, stop=kc == KC - 1)
                        last.then_inc(sem(f"proj{l}"), 1)
                        n += 1
                pe.drain().then_inc(ring_used[g % RING], 1)

            def gla_z(l):
                pe.wait_ge(sem(f"proj_out{l}"), n_items(l, 1))
                aup = prm[:, l * PARAMS + P_AUP:l * PARAMS + P_AUP + P]
                for d in range(2):
                    r = slice(32 * d, 32 * d + 16)
                    T.matmul(bank(4 + d), aup[r, :], FM[r, AL, 0:LAT], start=True, stop=True)
                    T.matmul(bank(6 + d, CTX), aup[r, :], FM[r, AL, LAT:TOK], start=True, stop=True).then_inc(sem("z"), 1)

            def gla_keys(l):
                pe.wait_ge(sem("ke"), 2 + l * PER["ke"])
                for g in range(3):
                    for j in range(4):
                        n = 4 * g + j
                        last = T.transpose(bank(4 + g, P, j * P), E[n // NT][:, (n % NT) * P:(n % NT + 1) * P], ident)
                    last.then_inc(sem("keT"), 1)
                pe.wait_ge(sem("keT_out"), 1 + l * PER["keT_out"])
                for i in range(NT - 1):
                    if i >= 2:
                        pe.wait_ge(sem("state"), 2 * (i - 1) + l * PER["state"])
                    for d, order in enumerate((F_ORD, B_ORD)):
                        t = order[i]
                        last = T.matmul(bank(4 + i % 2, 256, 256 * d), KET[:, NT * d + t, :], TM[:, t, TM_GV:TM_GV + 256], start=True, stop=True)
                    last.then_inc(sem("dS"), 1)

            def rot(l):
                pe.wait_ge(sem(f"proj_out{l}"), n_items(l, 5))
                for i, b in enumerate([SK, SQ, SQ + 1, SQ + 2, SQ + 3]):
                    if i >= 2:
                        pe.wait_ge(sem("rope"), i - 1 + l * PER["rope"])
                    T.matmul(bank(6 + i % 2), cst[:, C_ROT:C_ROT + P], FM[:, b, 0:LAT], start=True, stop=True).then_inc(sem("rot"), 1)

            def gla_out(l):
                pe.wait_ge(sem("qk"), 6 + l * PER["qk"])
                pe.wait_ge(sem("rope"), 5 + l * PER["rope"])
                for i, t in enumerate(tiles(l)):
                    c = slice(t * P, (t + 1) * P)
                    pe.wait_ge(sem(f"qblk{l}"), 2 * i + 2)
                    for d in range(2):
                        last = T.matmul(bank(4 + d), E[3 * d + 1][:, c], QBLK[d], start=True, stop=True)
                    last.then_inc(sem(f"scores{l}"), 1)
                    if i >= 2:
                        pe.wait_ge(sem(f"o_out{l}"), i - 1)
                    for d in range(2):
                        T.matmul(bank(6 + i % 2, 256), E[3 * d + 2][:, c], STATE[d][:, t, :], start=d == 0, stop=False)
                    pe.wait_ge(sem(f"A{l}"), i + 1)
                    for h in range(GLA_H):
                        last = T.matmul(bank(6 + i % 2, DV, h * DV), A_SB[:, h * P:(h + 1) * P], TM[:, t, TM_GV + h * DV:TM_GV + (h + 1) * DV],
                                        start=False, stop=h == GLA_H - 1)
                    last.then_inc(sem(f"o{l}"), 1)

            def attend(l):
                us = units(l)
                pe.wait_ge(sem("gla_o"), 1 + l * PER["gla_o"])
                nmod = 0

                def scores(u):
                    ti, t, kind, h = us[u]
                    k0, nl = local_keys(t, kind)
                    r = slice(64 * (h % 2), 64 * (h % 2) + 64)
                    if kind == "n":
                        q, kb = FM[r, NQ + h // 2, t * P:(t + 1) * P], NK + h // 2
                    else:
                        q, kb = FM[r, SQ + h // 2, t * P:(t + 1) * P], SK
                    if u >= 2:
                        pe.wait_ge(sem(f"exp{l}"), u - 1)
                    if nl:
                        T.matmul(bank(2 * (u % 2), nl), q, FM[r, kb, k0:k0 + nl], start=True, stop=True)
                    T.matmul(bank(2 * (u % 2) + 1, CTX), q, FM[r, kb, LAT:TOK], start=True, stop=True).then_inc(sem(f"s{l}"), 1)

                def product(u):
                    ti, t, kind, h = us[u]
                    k0, nl = local_keys(t, kind)
                    pe.wait_ge(sem(f"pt_out{l}"), u + 1)
                    if u >= 2:
                        pe.wait_ge(sem(f"norm{l}"), u - 1)
                    kt = [k0 // P + j for j in range(nl // P)] + [NLT, NLT + 1]
                    c = TM_NV + h * HV if kind == "n" else TM_SV + (h % 2) * HV
                    for j, tk in enumerate(kt):
                        last = T.matmul(bank(6 + u % 2, HV), PT[u % 2][:, j, :], TM[:, tk, c:c + HV], start=j == 0, stop=j == len(kt) - 1)
                    last.then_inc(sem(f"pv{l}"), 1)

                scores(0)
                for u in range(len(us) + 2):
                    if u + 1 < len(us):
                        scores(u + 1)
                    if u < len(us):
                        nk = (local_keys(us[u][1], us[u][2])[1] + CTX) // P
                        pe.wait_ge(sem(f"exp{l}"), u + 1)
                        if u >= 1:
                            pe.wait_ge(sem(f"pt_out{l}"), u)
                        done = (u - 2) // UPT
                        if done > 0:
                            pe.wait_ge(sem(f"mixT_out{l}"), done)
                        for j in range(nk):
                            last = T.transpose(bank(4, P, j * P) if j < 4 else bank(5, P, (j - 4) * P), PR[u % 2][:, j * P:(j + 1) * P], ident)
                        last.then_inc(sem(f"T{l}"), 1)
                    if 0 <= u - 1 < len(us):
                        product(u - 1)
                    v = u - 2
                    if v >= 0 and v % UPT == UPT - 1:
                        ti, t = us[v][0], us[v][1]
                        pe.wait_ge(sem(f"norm{l}"), v + 1)
                        pe.wait_ge(sem(f"pt_out{l}"), min(u + 1, len(us)))
                        for k in range(KC):
                            src = glao[:, t * 256 + k * P:t * 256 + (k + 1) * P] if k < 2 else MIX[ti % 2][:, (k - 2) * P:(k - 1) * P]
                            last = T.transpose(bank(4 + k // 4, P, (k % 4) * P), src, ident)
                        last.then_inc(sem(f"mixT{l}"), 1)
                        if l == 0:
                            for _ in range(2):
                                mod(1, nmod)
                                nmod += 1

            def gate_rows(l, half):
                n = 2 if l < DEPTH - 1 else 1
                if half == "a":
                    pe.wait_ge(sem(f"mixT_out{l}"), len(tiles(l)))
                    if l == 0:
                        pe.wait_ge(sem("mod1_out"), 1)
                for wch in range(n):
                    pe.wait_ge(sem("diag"), wch + 1 + before("diag", l, half))
                    for j in range(2):
                        last = T.matmul(bank(4 + 2 * wch + j), ones[:, :], DIAG[wch][:, j * 512:(j + 1) * 512], start=True, stop=True)
                    last.then_inc(sem("grow"), 1)

            def w_out(l):
                u = [v3(arrived(OUT_AT[l] + j), KC) for j in range(2)]
                for i, t in enumerate(tiles(l)):
                    if i >= 2:
                        pe.wait_ge(sem("y_used"), i - 1 + before("y_used", l, "a"))
                    for j in range(2):
                        for kc in range(KC):
                            last = T.matmul(bank(2 * (i % 2) + j), hTv[:, kc, t * P:(t + 1) * P], u[j][:, kc, :], start=kc == 0, stop=kc == KC - 1)
                    last.then_inc(sem(f"wo{l}"), 1)
                pe.drain().then_inc(ring_used[OUT_AT[l] % RING], 1)
                pe.drain().then_inc(ring_used[(OUT_AT[l] + 1) % RING], 1)

            def route(l):
                ts = tiles(l)
                for t in sorted(ts):
                    for kc in range(KC):
                        last = T.matmul(bank(6, NE, t * NE), hTv[:, kc, t * P:(t + 1) * P], router[:, kc * NE:(kc + 1) * NE],
                                        start=kc == 0, stop=kc == KC - 1)
                last.then_inc(sem("logits"), 1)
                pe.wait_ge(sem("aff"), 1 + l * PER["aff"])
                for t in range(NLT):
                    last = T.transpose(ps[0:48, 7 * 512 + t * P:7 * 512 + (t + 1) * P], AFF[:, t, :], ident)
                last.then_inc(sem("affT"), 1)
                pe.wait_ge(sem("picked"), 1 + l * PER["picked"])

            def ffn(l):
                ctx_too = l < DEPTH - 1
                base = FFN_AT[l]
                nt = len(tiles(l))
                per = 2 * nt
                c_ = cw(l)
                pe.wait_ge(sem(f"acc{l}"), 4)
                with pe.Fori(0, PAIRS) as i:
                    def arrived_(n):
                        pe.wait_ge(ring_full[n % RING], i * 48 + 16 * (n // RING + 1))
                        return v3(ringv[:, n % RING, :], KC)

                    pe.wait_ge(sem("sel"), i + 1 + l * PER["sel"])
                    pe.wait_ge(sem(f"acc{l}"), i * per + 4)
                    for g in range(2):
                        for k in range(4):
                            c0 = (4 * g + k) * P
                            for t in range(NLT):
                                last = T.matmul(bank(6 + g, P, k * P), XN[:, t, c0:c0 + P], SEL_L[:, t, :], start=t == 0, stop=t == NLT - 1)
                        last.then_inc(sem(f"gather{l}"), 1)
                    if ctx_too:
                        for k in range(KC):
                            for t in range(NCT):
                                last = T.matmul(bank(4, 64, k * 64), XN[:, NLT + t, k * P:(k + 1) * P], SEL_C[:, t, :], start=t == 0, stop=t == NCT - 1)
                        last.then_inc(sem(f"gather{l}"), 1)
                    pe.wait_ge(sem("xs"), i + 1 + l * PER["xs"])
                    if ctx_too:
                        pe.wait_ge(sem(f"xsc{l}"), i + 1)
                    for e in range(2):
                        u0 = base + 6 * e
                        for h in range(2):
                            for m in range(2):
                                n = u0 + 2 * h + m
                                u = arrived_(n)
                                if m == 0:
                                    pe.wait_ge(sem(f"hid{l}"), i * 4 + (2 * e + h + 1))
                                for j in range(4):
                                    for kc in range(KC):
                                        last = T.matmul(bank(2 * h + m, c_, j * CW), u[:, kc, j * P:(j + 1) * P], XST[:, kc, e, 0:c_],
                                                        start=kc == 0, stop=kc == KC - 1)
                                last.then_inc(ring_used[n % RING], 1)
                        for d in range(2):
                            n = u0 + 4 + d
                            u = arrived_(n)
                            if d == 0:
                                pe.wait_ge(sem(f"hid{l}"), i * 4 + (2 * e + 4))
                            if e == 1:
                                pe.wait_ge(sem("yt"), i * 4 + d + 1 + l * PER["yt"])
                            for j in range(4):
                                for kc in range(KC):
                                    last = T.matmul(bank(4 + d, c_, j * CW), u[:, kc, j * P:(j + 1) * P], HID[:, e, kc, 0:c_],
                                                    start=kc == 0, stop=kc == KC - 1)
                            last.then_inc(ring_used[n % RING], 1)
                    pe.wait_ge(sem("yt"), i * 4 + 4 + l * PER["yt"])
                    for k in range(KC):
                        last = T.transpose(bank(6 + k // 4, P, (k % 4) * P), YTL[:, k, :], ident)
                    last.then_inc(sem(f"yturn{l}"), 1)
                    if ctx_too:
                        for k in range(KC):
                            last = T.transpose(ps[0:64, k * P:(k + 1) * P], YTC[:, k, :], ident)
                        last.then_inc(sem(f"yturn{l}"), 1)
                    pe.wait_ge(sem("yl"), i + 1 + l * PER["yl"])
                    pe.wait_ge(sem("ptok"), i + 1 + l * PER["ptok"])
                    for c in range(per):
                        t, half = tiles(l)[c // 2], c % 2
                        if c == 0 and ctx_too:
                            pe.wait_ge(sem(f"yc{l}"), i + 1)
                        if c >= 4:
                            pe.wait_ge(sem(f"acc{l}"), i * per + (c + 1))
                        ob = bank((6, 7, 2, 3)[c % 4])
                        if t < NLT:
                            last = T.matmul(ob, PT_L[:, t * P:(t + 1) * P], YL[:, half * 512:half * 512 + 512], start=True, stop=True)
                        else:
                            last = T.matmul(ob, PT_C[0:64, (t - NLT) * P:(t - NLT + 1) * P], YC[0:64, half * 512:half * 512 + 512], start=True, stop=True)
                        last.then_inc(sem(f"comb{l}"), 1)

            pe.wait_ge(sem("silu_c"), 1)
            for k in range(MOD_UNITS):
                mod(0, k)
            pe.wait_ge(sem("const_in"), 16)
            pe.wait_ge(sem("param_in"), 16)
            pe.wait_ge(sem("ones_set"), 1)
            for l in range(DEPTH):
                turn_x(l, "a")
                project(l, 0)
                project(l, 1)
                gla_z(l)
                project(l, 2)
                project(l, 3)
                gla_keys(l)
                project(l, 4)
                rot(l)
                gla_out(l)
                attend(l)
                gate_rows(l, "a")
                w_out(l)
                turn_x(l, "f")
                route(l)
                ffn(l)
                gate_rows(l, "f")


def _constants(np):
    c = np.zeros((P, CONSTS), np.float32)
    i = np.arange(P)
    c[:, C_ID:C_ID + P] = np.eye(P)
    c[:, C_MF:C_MF + P] = i[:, None] <= i[None, :]
    c[:, C_MB:C_MB + P] = i[:, None] >= i[None, :]
    band = np.arange(3 * P)[None, :] - P - i[:, None]
    c[:, C_BAND:C_BAND + 3 * P] = np.where(np.abs(band) <= WINDOW, 0.0, NEG)
    d, t = np.arange(P) % HD, np.arange(LAT)
    quarter = HD // 4
    freq = np.float32(10000.0) ** (-np.arange(quarter, dtype=np.float32) / np.float32(quarter))
    pos = np.where((d < HD // 2)[:, None], (t // GRID_W)[None, :], (t % GRID_W)[None, :]).astype(np.float32)
    ang = pos * freq[d % quarter][:, None].astype(np.float32)
    c[:, C_COS:C_COS + LAT] = np.cos(ang)
    c[:, C_SIN:C_SIN + LAT] = np.sin(ang)
    for m in range(P):
        if m % (2 * quarter) < quarter:
            c[m + quarter, C_ROT + m] = -1.0
        else:
            c[m - quarter, C_ROT + m] = 1.0
    c[:, C_HM:C_HM + GLA_H] = (i[:, None] // DK) == np.arange(GLA_H)[None, :]
    c[:, C_IOTA:C_IOTA + NLT] = i[:, None] + P * np.arange(NLT)[None, :]
    return c


def _layout(np, a):
    f = np.float32
    x_all = np.concatenate([a["x"][0], a["ctx"][0]], 0)
    cvec = np.stack([a["c"][0].reshape(KC, P).T, a["c_ctx"].reshape(KC, P).T], 2).reshape(P, 2 * KC)
    widths = (GLA_H * DK, GLA_H * DV, 16, 16, NAT_H * HD, NAT_H * HD, 2 * HD, 2 * HD, GLA_H * DK, GLA_H * DV, NAT_H * HD, SWA_H * HD)
    at = np.concatenate([[0], np.cumsum(widths)])
    sq_order = np.concatenate([np.arange(HD) + HD * (p // 2 + 4 * (p % 2)) for p in range(SWA_H)])

    def rows(w):
        return w.reshape(KC, P, -1).transpose(1, 0, 2)

    def blocks(w):
        return w.reshape(KC, P, 4, P).transpose(1, 2, 0, 3).reshape(P, UNIT)

    stream = np.zeros((N_UNITS, P, UNIT), f)
    params = np.zeros((DEPTH, P, PARAMS), f)
    for l in range(DEPTH):
        for k in range(MOD_UNITS):
            stream[MOD_AT[l] + k] = rows(a["w_mod"][l][:, 512 * k:512 * (k + 1)]).reshape(P, UNIT)
        gk, gv, gaf, gab, nk, nv, sk, sv, gq, gg, nq, sq = (a["w_in"][l][:, at[i]:at[i + 1]] for i in range(12))
        z16 = np.zeros((D, 16), f)
        al = np.concatenate([gaf, z16, gab, z16, z16, z16, z16, z16], 1)
        u = IN_AT[l]
        stream[u] = blocks(np.concatenate([gk, al, gq, sk], 1))
        stream[u + 1] = rows(np.concatenate([gv, nv], 1)).reshape(P, UNIT)
        stream[u + 2, :, 0:KC * 384] = rows(np.concatenate([sv, gg], 1)).reshape(P, -1)
        stream[u + 2, :, KC * 384:KC * 400] = rows(a["w_router"][l]).reshape(P, -1)
        stream[u + 3] = blocks(np.concatenate([nk, nq], 1))
        stream[u + 4] = blocks(sq[:, sq_order])
        for j in range(2):
            stream[OUT_AT[l] + j] = rows(a["w_out"][l][:, 512 * j:512 * (j + 1)]).reshape(P, UNIT)
        for e in range(NE):
            u = FFN_AT[l] + 6 * e
            for h in range(2):
                c = slice(512 * h, 512 * (h + 1))
                stream[u + 2 * h] = rows(a["w_gate"][l, e][:, c]).reshape(P, UNIT)
                stream[u + 2 * h + 1] = rows(a["w_up"][l, e][:, c]).reshape(P, UNIT)
                stream[u + 4 + h] = rows(a["w_down"][l, e][:, c]).reshape(P, UNIT)
        params[l, :, P_BMOD:P_BMOD + 96] = np.repeat(a["b_mod"][l].reshape(48, P).T[:, :, None], 2, 2).reshape(P, 96)
        params[l, :, P_GAIN:P_GAIN + 32] = a["norm_gains"][l].reshape(4, KC, P).transpose(2, 0, 1).reshape(P, 32)
        params[l, 0:16, P_AUP:P_AUP + P] = a["gla_a_up"][l, 0]
        params[l, 32:48, P_AUP:P_AUP + P] = a["gla_a_up"][l, 1]
        params[l, :, P_AB:P_AB + 2] = a["gla_a_bias"][l].T
        params[l, :, P_GG:P_GG + DV] = a["gla_norm"][l][None, :]
        params[l, :, P_SINK:P_SINK + SWA_H] = a["swa_sink"][l][None, :]
    t = np.arange(LAT)
    r, c = t // GRID_W, t % GRID_W
    start = np.clip(c - NAT_COLS // 2, 0, GRID_W - NAT_COLS)
    seen = (c[None, :] >= start[:, None]) & (c[None, :] < start[:, None] + NAT_COLS)
    ri = r[None, :] - r[:, None] + NAT_ROWS - 1
    ci = np.clip(c[None, :] - c[:, None] + NAT_COLS - 1, 0, 2 * NAT_COLS - 2)
    bias = np.where(seen, a["nat_rpb"][:, :, ri, ci], f(NEG)).astype(f)
    bias = bias.reshape(DEPTH, NAT_H, NLT, P, LAT).transpose(0, 2, 1, 3, 4)
    iotarow = np.broadcast_to(np.arange(LAT, dtype=f), (P, LAT))
    return {"x_all": x_all, "cvec": cvec, "consts": _constants(np), "iotarow": iotarow, "params": params,
            "nat_bias": bias, "wstream": stream}


def kernel(**inputs):
    import numpy as np
    import concourse.bacc as bacc
    from concourse import mybir as mb
    from concourse.bass_utils import run_bass_kernel_spmd as run

    nc = bacc.Bacc("TRN2", target_bir_lowering=False, num_devices=1)
    arrays, args = {}, []
    laid = _layout(np, {k: np.asarray(v) for k, v in inputs.items()})
    for name in ("x_all", "cvec", "consts", "iotarow", "params", "nat_bias", "wstream"):
        v = np.ascontiguousarray(laid[name])
        arrays[f"in_{name}"] = v
        args.append(nc.dram_tensor(f"in_{name}", v.shape, mb.dt.from_np(v.dtype), kind="ExternalInput").ap())
    args.append(nc.dram_tensor("x_kept", (LAT, D), mb.dt.float32).ap())
    args.append(nc.dram_tensor("picked", (DEPTH, 2, 2, NE * CAP_L), mb.dt.float32).ap())
    args.append(nc.dram_tensor("out_x", (LAT, D), mb.dt.float32, kind="ExternalOutput").ap())
    bass_hybrid_dit(nc, *args)
    r = run(nc, [arrays], core_ids=[0])
    return r.results[0]["out_x"].reshape(1, LAT, D)
```

```python
import concourse.bass as bass
from concourse import mybir
from contextlib import ExitStack

P = 128
D = 1024
KC = D // P
LAT, CTX = 512, 256
TOK = LAT + CTX
NLT, NCT = LAT // P, CTX // P
NT = NLT + NCT
DEPTH = 2
GRID_W = 64
NAT_H, SWA_H, GLA_H = 4, 8, 4
NAT_ROWS, NAT_COLS = 8, 16
WINDOW = 128
HD = 64
DK, DV = 32, 64
TAU = 16.0
NE = 16
PAIRS = NE // 2
CAP_L, CAP_C = 2 * LAT // NE, 2 * CTX // NE
EPS = 1e-6
NEG = -1e30
SCALE = HD ** -0.5
UNIT = 4096
RING = 4
MOD_UNITS, IN_UNITS, OUT_UNITS, FFN_UNITS = 12, 5, 2, 6 * NE
CW = CAP_L + CAP_C

SLOTS = 6
MOD_AT = [0, MOD_UNITS + IN_UNITS]
IN_AT = [MOD_UNITS, 2 * MOD_UNITS + IN_UNITS + OUT_UNITS + FFN_UNITS]
OUT_AT = [2 * MOD_UNITS + IN_UNITS, IN_AT[1] + IN_UNITS]
FFN_AT = [OUT_AT[0] + OUT_UNITS, OUT_AT[1] + OUT_UNITS]
N_UNITS = FFN_AT[1] + FFN_UNITS


def lap(n):
    n -= FFN_UNITS if n >= FFN_AT[0] else 0
    return n % RING, n // RING



GK, GQ, NQ, NK, SK, SQ, AL = 0, 1, 2, 4, 6, 7, 11
NFM = 12
TM_GV, TM_NV, TM_SV, TM_GG = 0, 256, 512, 640
TMW = TM_GG + 256

C_ID, C_MF, C_MB, C_BAND, C_COS, C_SIN, C_ROT, C_HM, C_IOTA, C_SUM = 0, 128, 256, 384, 768, 1280, 1792, 1920, 1924, 1928
CONSTS = C_SUM + 2
P_BMOD, P_GAIN, P_AUP, P_AB, P_GG, P_SINK = 0, 96, 128, 256, 258, 322
PARAMS = P_SINK + SWA_H


UPT = NAT_H + SWA_H

PER = {"z": 2, "z_out": 2, "softplus": 2, "scan": 12, "totc": 2, "ke_arg": 2, "ke_exp": 2, "ke": 2,
       "tot_exp": 1, "keT": 3, "keT_out": 1, "dSm": 10, "dS": 5, "state": 10, "rope": 5, "rot": 5,
       "q_arg": 6, "q_exp": 6, "qk": 6, "gla_ms": 1, "gla_rs": 1, "gate_exp": 1, "gla_o": 1, "router_in": 1,
       "logits": 1, "logit_sub": 1, "logit_exp": 1, "aff": 1, "affT": 1, "picked": 1, "iota": 16,
       "proj": 2 * NT + 28, "proj_out": 2 * NT + 28, "qblk": 2 * NT, "scores": NT, "A": NT, "o": NT, "o_out": NT,
       "s": UPT * NT, "max": UPT * NT, "exp": UPT * NT, "diagr": UPT * NT, "T": UPT * NT, "pt_out": UPT * NT,
       "pv": UPT * NT // 2, "mix": UPT * NT // 2, "bias": 16 * NAT_H * NLT // 4, "wo": NT, "x_mid": NT,
       "acc_zero": NT, "gather": 3 * PAIRS, "comb": PAIRS * 2 * NT,
       "acc": PAIRS * 2 * NT}


PASSES = {"xT": (2 * KC, 2 * KC, 2 * KC, KC),
          "h_t": (2 * KC, 2 * KC, 2 * KC, KC),
          "diag": (2, 2, 1, 1),
          "grow": (2, 2, 1, 1),
          "grow_out": (1, 1, 1, 1),
          "psq": (NT, NT, NLT, NLT),
          "prs": (NT, NT, NLT, NLT),
          "y_used": (NT, NT, NLT, NLT),
          "sq": (NT, NT, NT, NLT),
          "xn": (NT, NT, NT, NLT)}


def before(name, l, half):
    return sum(PASSES[name][:2 * l + (half == "f")])


def bass_hybrid_dit(nc, x_all, cvec, consts, iotarow_d, params_d, nat_bias, wstream, xkeep, pick_d, out):
    f32 = mybir.dt.float32
    u32 = mybir.dt.uint32
    ALU = mybir.AluOpType
    ACT = mybir.ActivationFunctionType
    AX = mybir.AxisListType.X
    V, S, T = nc.vector, nc.scalar, nc.tensor

    ctx = ExitStack()
    with ctx:
        def sb(name, n, dt=f32):
            return ctx.enter_context(nc.sbuf_tensor(name, [P, n], dt))

        ring = sb("ring", RING * UNIT)
        hT = sb("hT", KC * TOK)
        big = sb("big", NFM * TOK + NT * TMW)
        cst = sb("cst", CONSTS)
        prm = sb("prm", DEPTH * PARAMS)
        ones = sb("ones", P)
        modc = sb("modc", DEPTH * 96)
        cols = sb("cols", 2 * 2 * 2 * KC)
        gcol = sb("gcol", 2 * KC)
        router = sb("router", P)
        small = sb("small", 2 * 8 + 2 * 8 + 8 + 24 + 24)
        glao = sb("glao", NT * 256)
        work = sb("work", 10752)
        ps = ctx.enter_context(nc.psum_tensor("ps", [P, 8 * 512], f32))

        def bank(b, n=512, at=0):
            return ps[:, b * 512 + at:b * 512 + at + n]

        def v3(ap, a):
            return ap.rearrange("p (a b) -> p a b", a=a)

        ident = cst[:, C_ID:C_ID + P]
        X = v3(big[:, 0:NT * D], NT)
        GROW = v3(big[:, NT * D:NT * D + 2 * D], 2)
        XN = v3(big[:, 8 * D:8 * D + NT * D], NT)
        FM = v3(big[:, 0:NFM * TOK], NFM)
        TM = v3(big[:, NFM * TOK:], NT)
        hTv = v3(hT[:, :], KC)
        ACC = v3(hT[:, :], NT)
        ringv = v3(ring[:, :], RING)
        slot = [ringv[:, j, :] for j in range(RING)] + [big[:, j * UNIT:(j + 1) * UNIT] for j in range(2)]
        colv = cols[:, :].rearrange("p (s w m k) -> p s w m k", s=2, w=2, m=2)
        modv = modc[:, :].rearrange("p (l n w) -> p l n w", l=DEPTH, w=2)
        ss = small[:, 0:12]
        rs = small[:, 16:16 + 12]
        tmp8 = small[:, 32:40]
        gss = small[:, 40:64]
        grs = small[:, 64:88]

        def w(at, n):
            return work[:, at:at + n]

        CUM = [w(0, TOK), w(TOK, TOK)]
        E = [w((2 + i) * TOK, TOK) for i in range(6)]
        STATE = [v3(w(8 * TOK + d * NT * 256, NT * 256), NT) for d in range(2)]
        GX = 8 * TOK + 2 * NT * 256
        KET = v3(w(GX, 12 * P), 12)
        A_SB = w(GX, 512)
        A_TMP = w(GX + 512, 512)
        QBLK = [w(CUM_AT, 512) for CUM_AT in (0, 512)]
        KW = 5 * P
        SC = [w(384 * i, 384) for i in range(2)]
        PR = [w(768 + KW * i, KW) for i in range(2)]
        PT = [w(2048 + KW * i, KW) for i in range(4)]
        BIAS = [w(4608 + 384 * i, 384) for i in range(4)]
        RDIAG = [w(6144 + P * i, P) for i in range(2)]
        AST = w(6400, 96)
        MODROW = w(6656, 512)
        CS = w(0, 16)
        CTMP = w(16, 16)
        CS32 = v3(sb("silu_c", KC * 32)[:, :], KC)
        AFMX = sb("route_stats", 16)
        AFM = AFMX[:, :]
        DIAG = [w(0, D), w(D, D)]
        JUNK = w(2 * D, D)
        YT_ = w(3 * D, D)
        at = [0]

        def take(n):
            at[0] += n
            assert at[0] <= 10752
            return w(at[0] - n, n)

        SEL_L, SEL_C = v3(take(512), 4), v3(take(128), 2)
        PT_L, PT_C = [take(512) for _ in range(2)], [take(256) for _ in range(2)]
        XST = take(KC * 2 * CW).rearrange("p (k e c) -> p k e c", k=KC, e=2)
        HT = v3(take(KC * CW), KC)
        HIDL, HIDC = take(512), take(512)
        SGL, SGC = glao[:, 0:512], glao[:, 512:1024]
        YL, YC = [take(512) for _ in range(2)], [take(512) for _ in range(2)]
        IDXL, IDXC = take(NE * CAP_L), take(NE * CAP_C)
        COLS_L, COLS_C = v3(take(4 * PAIRS), 4), v3(take(4 * PAIRS), 4)
        IOTAR = take(LAT)
        AFF = v3(take(NLT * 48), NLT)
        LOG = v3(take(NT * NE), NT)
        VALS, IDXF = take(CAP_L), take(CAP_L)
        AFT0, AFT1 = HIDL, HIDC
        idxu = sb("idxu", CAP_L, u32)

        sems = {}

        def sem(name):
            if name not in sems:
                sems[name] = ctx.enter_context(nc.semaphore(name))
            return sems[name]

        ring_full = [sem(f"ring_full{i}") for i in range(RING)]
        ring_used = [sem(f"ring_used{i}") for i in range(RING)]
        ffn_full = [sem(f"ffn_full{i}") for i in range(SLOTS)]
        ffn_used = [sem(f"ffn_used{i}") for i in range(SLOTS)]

        class Chain:

            def __init__(self, eng, name):
                self.eng, self.sem, self.n = eng, sem(name), 0

            def __call__(self, ins):
                self.n += 1
                ins.then_inc(self.sem, 1)
                self.eng.wait_ge(self.sem, self.n)

        def width(l):
            return TOK if l < DEPTH - 1 else LAT

        def tiles(l):
            return [4, 5, 0, 1, 2, 3] if l < DEPTH - 1 else [0, 1, 2, 3]

        def token_parts(l, kv):
            return [(0, LAT)] + ([(LAT, CTX)] if kv or l < DEPTH - 1 else [])

        def fm_items(l, unit):
            blocks = {0: [GK, AL, GQ, SK], 3: [NK, NK + 1, NQ, NQ + 1], 4: [SQ, SQ + 1, SQ + 2, SQ + 3]}[unit]
            return [(j, b, t0, n) for j, b in enumerate(blocks)
                    for t0, n in token_parts(l, b in (GK, AL, SK, NK, NK + 1))]

        def n_items(l, upto):
            return sum({1: NT + 4, 2: NT}[u] if u in (1, 2) else len(fm_items(l, u)) for u in range(upto))

        def units(l):
            out_ = []
            for ti, t in enumerate(tiles(l)):
                for kind, h in [("n", h) for h in range(NAT_H)] + [("s", h) for h in range(SWA_H)]:
                    out_.append((ti, t, kind, h))
            return out_

        def by_column(ap, packed):
            if packed:
                return ap.rearrange("p (c r) -> p c r", r=LAT // GRID_W)
            return ap.rearrange("p (r c) -> p c r", c=GRID_W)

        def local_keys(t):
            if t >= NLT:
                return 0, 0
            a, b = max(t - 1, 0), min(t + 2, NLT)
            return a * P, (b - a) * P

        KEY_COPY = [(NK, GK), (NK + 1, GQ), (SK, AL)]

        F_ORD, B_ORD = [4, 5, 0, 1, 2, 3], [5, 4, 3, 2, 1, 0]

        def cw(l):
            return CW if l < DEPTH - 1 else CAP_L

        def acc_total(l):
            return (l * NT + len(tiles(l))) * 2 * PAIRS

        COMB_BANKS = (7, 0, 1)

        block = ctx.enter_context(nc.Block())

        @block.sync
        def _(sp):
            def load(n):
                p, before_ = lap(n)
                sp.dma_start(ringv[:, p, :], wstream[n, :, :]).then_inc(ring_full[p], 16)

            def ring_load(a, b):
                p0, g0 = lap(a)
                laps = (b - a) // RING
                if laps:
                    with sp.Fori(0, laps) as g:
                        for j in range(RING):
                            p = (p0 + j) % RING
                            sp.wait_ge(ring_used[p], g + lap(a + j)[1])
                            sp.dma_start(ringv[:, p, :], wstream[g * RING + (a + j), :, :]).then_inc(ring_full[p], 16)
                for n in range(a + laps * RING, b):
                    sp.wait_ge(ring_used[lap(n)[0]], lap(n)[1])
                    load(n)

            for n in range(RING):
                load(n)
            ring_load(RING, FFN_AT[0])
            for l in range(DEPTH):
                last = FFN_AT[l] - 1
                for j in range(SLOTS):
                    if j < RING:
                        n = max(n for n in range(last - RING + 1, last + 1) if lap(n)[0] == j)
                        sp.wait_ge(ring_used[j], lap(n)[1] + 1)
                    elif j == RING:
                        sp.wait_ge(sem("x_saved"), 16 * [NT, NT + NLT][l])
                    sp.dma_start(slot[j], wstream[FFN_AT[l] + j, :, :]).then_inc(ffn_full[j], 16)
                with sp.Fori(1, NE) as e:
                    for j in range(SLOTS):
                        sp.wait_ge(ffn_used[j], e + l * NE)
                        sp.dma_start(slot[j], wstream[e * SLOTS + (FFN_AT[l] + j), :, :]).then_inc(ffn_full[j], 16)
                if l == 0:
                    for n in range(IN_AT[1], FFN_AT[1]):
                        if n < IN_AT[1] + RING:
                            sp.wait_ge(ffn_used[lap(n)[0]], NE)
                        sp.wait_ge(ring_used[lap(n)[0]], lap(n)[1])
                        load(n)

        @block.gpsimd
        def _(pool):
            pool.dma_start(cst[:, :], consts).then_inc(sem("const_in"), 16)
            pool.dma_start(v3(prm[:, :], DEPTH), params_d.rearrange("l p c -> p l c")).then_inc(sem("param_in"), 16)
            pool.dma_start(CS, cvec).then_inc(sem("c_in"), 16)
            pool.memset(CS32, 0.0).then_inc(sem("c_zero"), 1)
            pool.dma_start(X, x_all.rearrange("(t p) d -> p t d", p=P)).then_inc(sem("x_in"), 16)
            pool.memset(ones[:, :], 1.0).then_inc(sem("ones_set"), 1)
            for l in range(DEPTH):
                us = units(l)
                if l:
                    for t in range(NLT):
                        pool.wait_ge(sem("x_ready"), t + 1)
                        pool.dma_start(xkeep[t * P:(t + 1) * P, :], X[:, t, :]).then_inc(sem("x_kept"), 16)
                    pool.wait_ge(sem("x_kept"), 16 * NLT)
                pool.wait_ge(sem("qk"), (l + 1) * PER["qk"])
                pool.wait_ge(sem("rope"), (l + 1) * PER["rope"])
                pool.wait_ge(sem("proj_out"), n_items(l, 5) + l * PER["proj_out"])
                for i, (b, other) in enumerate(KEY_COPY):
                    pool.tensor_copy(FM[64:P, other, :], FM[64:P, b, :]).then_inc(sem("key_copy"), 1)
                    pool.memset(FM[0:64, other, :], 0.0).then_inc(sem("keys"), 1)
                    pool.wait_ge(sem("key_copy"), 3 * l + i + 1)
                    pool.memset(FM[64:P, b, :], 0.0).then_inc(sem("keys"), 1)
                n = 0
                pool.wait_ge(sem("gla_o"), 1 + l * PER["gla_o"])
                stts = [u for u, x in enumerate(us) if x[2] == "n" and x[1] < NLT]
                for n, u in enumerate(stts):
                    if n >= 4:
                        pool.wait_ge(sem("max"), stts[n - 4] + 1 + l * PER["max"])
                    nl = local_keys(us[u][1])[1]
                    pool.dma_start(BIAS[n % 4][:, 0:nl], nat_bias[l, us[u][1], us[u][3], :, 0:nl]).then_inc(sem(f"bias{n % 4}"), 16)
                pool.wait_ge(sem("pv"), len(us) // 2 + l * PER["pv"])
                for t in tiles(l):
                    src = x_all if l == 0 else xkeep
                    pool.dma_start(X[:, t, :], src[t * P:(t + 1) * P, :]).then_inc(sem(f"x_back{t}"), 16)
                for i, t in enumerate(tiles(l)):
                    pool.wait_ge(sem("x_mid"), i + 1 + l * PER["x_mid"])
                    pool.wait_ge(sem("xn"), i + 1 + before("xn", l, "f"))
                    pool.dma_start(xkeep[t * P:(t + 1) * P, :], X[:, t, :]).then_inc(sem("x_saved"), 16)
                pool.wait_ge(sem("logits"), 1 + l * PER["logits"])
                for t in tiles(l):
                    pool.memset(ACC[:, t, :], 0.0).then_inc(sem("acc_zero"), 1)
                pool.dma_start(IOTAR, iotarow_d).then_inc(sem("iota"), 16)
                ctx_too = l < DEPTH - 1
                pool.wait_ge(sem("picked"), 1 + l * PER["picked"])
                pool.dma_start(pick_d[l, 1, 0, :].rearrange("(e r) -> e r", r=CAP_L), VALS[0:NE, :]).then_inc(sem("val_out"), 16)
                if ctx_too:
                    pool.dma_start(pick_d[l, 1, 1, 0:NE * CAP_C].rearrange("(e r) -> e r", r=CAP_C),
                                   VALS[32:32 + NE, 0:CAP_C]).then_inc(sem("val_out"), 16)
                pool.wait_ge(sem("idx_out"), l * 32 + (32 if ctx_too else 16))
                pool.wait_ge(sem("val_out"), l * 32 + (32 if ctx_too else 16))
                with nc.allow_non_contiguous_dma(reason="slot columns"):
                    for i in range(2):
                        for e in range(2):
                            src = pick_d[l, i, 0, :].rearrange("(a e p) -> e p a", e=2, p=CAP_L)[e]
                            for sw in range(2):
                                p = 64 * (e ^ sw)
                                pool.dma_start(COLS_L[p:p + 64, 2 * i + sw, :], src).then_inc(sem("cols_in"), 16)
                            if ctx_too:
                                src = pick_d[l, i, 1, 0:NE * CAP_C].rearrange("(a e p) -> e p a", e=2, p=CAP_C)[e]
                                for sw in range(2):
                                    for part in range(2):
                                        p = 64 * (e ^ sw) + 32 * part
                                        pool.dma_start(COLS_C[p:p + 32, 2 * i + sw, :], src).then_inc(sem("cols_in"), 16)
                for j in range(RING, SLOTS):
                    pool.wait_ge(ffn_used[j], (l + 1) * NE)
                for t in tiles(l):
                    pool.dma_start(X[:, t, :], xkeep[t * P:(t + 1) * P, :]).then_inc(sem(f"x_again{t}"), 16)
            for t in range(NLT):
                pool.wait_ge(sem("x_ready"), t + 1 + (DEPTH - 1) * NLT)
                pool.dma_start(out[t * P:(t + 1) * P, :], X[:, t, :]).then_inc(sem("stored"), 16)
            pool.wait_ge(sem("stored"), 16 * NLT)

        def picks(l):
            return 16 * (24 if l < DEPTH - 1 else 8)

        @block.scalar
        def _(act):
            chain = Chain(act, "act_chain")
            act.wait_ge(sem("c_in"), 16)
            S.activation(CTMP[:, 0:16], CS, ACT.Exp, scale=-1.0).then_inc(sem("c_exp"), 1)

            def norm_rows(l, half):
                ts = range(NT) if half == "a" else tiles(l)
                for i, t in enumerate(ts):
                    if half == "a":
                        if l == 0:
                            act.wait_ge(sem("x_in"), 16)
                        elif t < NLT:
                            act.wait_ge(sem("x_ready"), t + 1)
                        else:
                            act.wait_ge(sem("xc_ready"), t - NLT + 1)
                    else:
                        act.wait_ge(sem("x_mid"), i + 1 + l * PER["x_mid"])
                    S.activation(XN[:, t, :], X[:, t, :], ACT.Square, accum_out=ss[:, t:t + 1])\
                        .then_inc(sem("sq"), 1)
                    act.wait_ge(sem("sq"), i + 1 + before("sq", l, half))
                    chain(S.activation(rs[:, t:t + 1], ss[:, t:t + 1], ACT.Ln, scale=1.0 / D, bias=EPS))
                    chain(S.activation(rs[:, t:t + 1], rs[:, t:t + 1], ACT.Exp, scale=-0.5))
                    S.activation(XN[:, t, :], X[:, t, :], ACT.Copy, scale=rs[:, t:t + 1]).then_inc(sem("xn"), 1)

            def project_out(l, unit, parts):
                n = n_items(l, unit)
                for dst, b, k, shape in parts:
                    act.wait_ge(sem("proj"), n + 1 + l * PER["proj"])
                    S.activation(dst, shape(bank(n % 4, k)), ACT.Copy).then_inc(sem("proj_out"), 1)
                    n += 1

            def fm_parts(l, unit):
                parts = []
                for j, b, t0, n in fm_items(l, unit):
                    m = 48 if b == AL else P
                    if NQ <= b < SK and t0 == 0:
                        parts.append((by_column(FM[:, b, 0:LAT], True), b, n, lambda ap: by_column(ap, False)))
                    else:
                        parts.append((FM[0:m, b, t0:t0 + n], b, n, lambda ap, m=m: ap[0:m, :]))
                return parts

            def gla_exps(l):
                for d in range(2):
                    act.wait_ge(sem("z_out"), d + 1 + l * PER["z_out"])
                    chain(S.activation(E[2 + d], E[d], ACT.Abs))
                    chain(S.activation(E[2 + d], E[2 + d], ACT.Exp, scale=-1.0))
                    S.activation(E[2 + d], E[2 + d], ACT.Ln, bias=1.0).then_inc(sem("softplus"), 1)

            def gla_keys(l):
                for d in range(2):
                    act.wait_ge(sem("ke_arg"), d + 1 + l * PER["ke_arg"])
                    S.activation(E[d], E[d], ACT.Exp).then_inc(sem("ke_exp"), 1)
                act.wait_ge(sem("totc"), 2 + l * PER["totc"])
                S.activation(grs[:, 0:12], gss[:, 0:12], ACT.Exp).then_inc(sem("tot_exp"), 1)
                act.wait_ge(sem("keT"), 3 + l * PER["keT"])
                S.activation(w(GX, 12 * P), ps[:, 4 * 512:4 * 512 + 12 * P], ACT.Copy).then_inc(sem("keT_out"), 1)

            def gla_queries(l):
                n = width(l)
                for d in range(2):
                    for i in range(3):
                        act.wait_ge(sem("q_arg"), 3 * d + i + 1 + l * PER["q_arg"])
                        S.activation(E[3 * d + i][:, 0:n], E[3 * d + i][:, 0:n], ACT.Exp).then_inc(sem("q_exp"), 1)

            def gla_gate(l):
                n = width(l) // P
                act.wait_ge(sem("gla_ms"), 1 + l * PER["gla_ms"])
                chain(S.activation(grs[:, 0:4 * n], gss[:, 0:4 * n], ACT.Ln, scale=1.0 / DV, bias=EPS))
                S.activation(grs[:, 0:4 * n], grs[:, 0:4 * n], ACT.Exp, scale=-0.5).then_inc(sem("gla_rs"), 1)
                act.wait_ge(sem("proj_out"), n_items(l, 3) + l * PER["proj_out"])
                S.activation(v3(w(0, n * 256), n), TM[:, 0:n, TM_GG:TM_GG + 256], ACT.Exp, scale=-1.0)\
                    .then_inc(sem("gate_exp"), 1)

            def modrow(k):
                act.wait_ge(sem("modrow"), k + 1 + MOD_UNITS)
                S.activation(MODROW, bank(7), ACT.Copy).then_inc(sem("modrow_out"), 1)

            def attend(l):
                us = units(l)
                nt = width(l) // P
                act.wait_ge(sem("glaT"), l + 1)
                S.activation(hTv[:, 0:2, 0:nt * P], v3(ps[:, 4 * 512:4 * 512 + 2 * TOK], 2)[:, :, 0:nt * P], ACT.Copy)\
                    .then_inc(sem("glaT_out"), 1)
                for u in range(len(us) + 2):
                    if u < len(us):
                        ti, t, kind, h = us[u]
                        k0, nl = local_keys(t)
                        act.wait_ge(sem("max"), u + 1 + l * PER["max"])
                        if u >= 2:
                            act.wait_ge(sem("T"), u - 1 + l * PER["T"])
                        st = AST[:, 8 * (u % 4):8 * (u % 4) + 8]
                        if nl:
                            S.activation(PR[u % 2][:, 0:nl], SC[u % 2][:, 0:nl], ACT.Exp, bias=st[:, 2:3], accum_out=st[:, 4:5])
                        if kind == "s":
                            orig = h // 2 + 4 * (h % 2)
                            S.activation(st[:, 6:7], prm[:, l * PARAMS + P_SINK + orig:l * PARAMS + P_SINK + orig + 1], ACT.Exp,
                                         bias=st[:, 2:3])
                        S.activation(PR[u % 2][:, nl:nl + CTX], bank(2 * (u % 2) + 1, CTX), ACT.Exp, bias=st[:, 2:3],
                                     scale=SCALE, accum_out=st[:, 5:6]).then_inc(sem("exp"), 1)
                    v = u - 1
                    if 0 <= v < len(us):
                        n = local_keys(us[v][1])[1] + CTX
                        act.wait_ge(sem("T"), v + 1 + l * PER["T"])
                        if v >= 4:
                            act.wait_ge(sem("pv"), v // 2 - 1 + l * PER["pv"])
                        S.activation(PT[v % 4][:, 0:n], ps[:, 4 * 512:4 * 512 + n], ACT.Copy).then_inc(sem("pt_out"), 1)
                        if l == 0 and v % UPT in (7, 11):
                            modrow(2 * (v // UPT) + v % UPT // 11)

            def gate_rows(l, half):
                ctx_too = l < DEPTH - 1
                act.wait_ge(sem("grow"), (2 if ctx_too else 1) + before("grow", l, half))
                n = 2 if ctx_too else 1
                S.activation(big[:, NT * D:NT * D + n * D], ps[:, 4 * 512:4 * 512 + n * D], ACT.Copy)\
                    .then_inc(sem("grow_out"), 1)

            def post(l, half):
                for i, t in enumerate(tiles(l)):
                    if half == "a":
                        act.wait_ge(sem("wo"), i + 1 + l * PER["wo"])
                        src = ps[:, (i % 2) * D:(i % 2) * D + D]
                    else:
                        act.wait_ge(sem("acc"), acc_total(l))
                        src = ACC[:, t, :]
                    S.activation(JUNK, src, ACT.Square, accum_out=ss[:, t:t + 1]).then_inc(sem("psq"), 1)
                    act.wait_ge(sem("psq"), i + 1 + before("psq", l, half))
                    chain(S.activation(rs[:, t:t + 1], ss[:, t:t + 1], ACT.Ln, scale=1.0 / D, bias=EPS))
                    S.activation(rs[:, t:t + 1], rs[:, t:t + 1], ACT.Exp, scale=-0.5).then_inc(sem("prs"), 1)

            def ffn(l):
                ctx_too = l < DEPTH - 1
                base = FFN_AT[l]
                nt = len(tiles(l))
                act.wait_ge(sem("logit_sub"), 1 + l * PER["logit_sub"])
                S.activation(LOG[:, 0:nt, :], LOG[:, 0:nt, :], ACT.Exp).then_inc(sem("logit_exp"), 1)
                act.wait_ge(sem("picked"), 1 + l * PER["picked"])
                act.dma_start(pick_d[l, 0, 0, :].rearrange("(e r) -> e r", r=CAP_L), IDXF[0:NE, :]).then_inc(sem("idx_out"), 16)
                if ctx_too:
                    act.dma_start(pick_d[l, 0, 1, 0:NE * CAP_C].rearrange("(e r) -> e r", r=CAP_C), IDXF[32:32 + NE, 0:CAP_C])\
                        .then_inc(sem("idx_out"), 16)
                act.wait_ge(sem("idx_out"), l * 32 + (32 if ctx_too else 16))
                act.dma_start(IDXL, pick_d[l, 0, 0, :].partition_broadcast(P)).then_inc(sem("idx_in"), 16)
                if ctx_too:
                    act.dma_start(IDXC, pick_d[l, 0, 1, 0:NE * CAP_C].partition_broadcast(P)).then_inc(sem("idx_in"), 16)
                def picked(i, g):
                    act.wait_ge(sem("gather"), i * (3 if ctx_too else 2) + (g + 1 + l * PER["gather"]))
                    for k in range(4):
                        last = S.activation(XST[:, 4 * g + k, :, 0:CAP_L], v3(bank((7, 0)[g], P, k * P), 2), ACT.Identity,
                                            scale=colv[:, 1, 0, 0, 4 * g + k:4 * g + k + 1],
                                            bias=colv[:, 1, 0, 1, 4 * g + k:4 * g + k + 1])
                    if g:
                        last.then_inc(sem("xs"), 1)

                def expert(i, e, last_pair):
                    act.wait_ge(ffn_used[3], i * 2 + (e + 1 + l * NE))
                    S.activation(SGL, bank(0), ACT.Silu).then_inc(sem("silu"), 1)
                    if ctx_too:
                        S.activation(SGC[64:P, :], bank(2)[0:64, :], ACT.Silu).then_inc(sem("silu_ctx"), 1)
                    if e and not last_pair:
                        picked(i + 1, 0)
                    act.wait_ge(sem("hidT"), i * 2 + (e + 1 + l * NE))
                    S.activation(HT.rearrange("p (h j) c -> p h j c", h=2)[:, :, :, 0:CAP_L],
                                 bank(5).rearrange("p (j h c) -> p h j c", j=4, h=2), ACT.Copy).then_inc(sem("ht"), 1)
                    if ctx_too:
                        act.wait_ge(sem("hidT_c"), i * 2 + (e + 1))
                        S.activation(HT.rearrange("p (h j) c -> p h j c", h=2)[:, :, :, CAP_L:CW],
                                     bank(6).rearrange("p (j z h c) -> p z h j c", j=4, z=2, h=2)[:, 1], ACT.Copy).then_inc(sem("ht_c"), 1)
                    if e and not last_pair:
                        picked(i + 1, 1)
                    act.wait_ge(ffn_used[5], i * 2 + (e + 1 + l * NE))
                    S.activation(YL[e][0:64, :], bank(3)[0:64, :], ACT.Copy)
                    last = S.activation(YL[1 - e][64:P, :], bank(3)[64:P, :], ACT.Copy)
                    if ctx_too:
                        S.activation(YC[e][0:64, :], bank(4)[0:64, :], ACT.Copy)
                        last = S.activation(YC[1 - e][64:P, :], bank(4)[64:P, :], ACT.Copy)
                    last.then_inc(sem("yev"), 1)

                picked(0, 0)
                picked(0, 1)
                with act.Fori(0, PAIRS - 1) as i:
                    for e in range(2):
                        expert(i, e, False)
                for e in range(2):
                    expert(PAIRS - 1, e, True)

            norm_rows(0, "a")
            for k in range(MOD_UNITS):
                act.wait_ge(sem("modrow"), k + 1)
                if k >= 2:
                    act.wait_ge(sem("modcol"), k - 1)
                S.activation(w(512 + 512 * (k % 2), 512), bank(k % 2), ACT.Copy).then_inc(sem("modrow_out"), 1)
            for l in range(DEPTH):
                if l:
                    norm_rows(l, "a")
                if l:
                    act.wait_ge(sem("x_kept"), 16 * NLT)
                project_out(l, 0, fm_parts(l, 0))
                n = n_items(l, 1)
                for b in range(2):
                    act.wait_ge(sem("proj"), n + 1 + l * PER["proj"])
                    S.activation(by_column(FM[:, NQ + b, 0:LAT], True), by_column(bank(n % 4), False), ACT.Copy)\
                        .then_inc(sem("proj_out"), 1)
                    n += 1
                for t in range(NT):
                    act.wait_ge(sem("proj"), n + 1 + l * PER["proj"])
                    m = 256 if t < NLT else 512
                    S.activation(TM[:, t, TM_GV:TM_GV + m], bank(n % 4, m), ACT.Copy).then_inc(sem("proj_out"), 1)
                    n += 1
                for j in range(2):
                    act.wait_ge(sem("proj"), n + 1 + l * PER["proj"])
                    S.activation(TM[:, 2 * j:2 * j + 2, TM_NV:TM_SV], v3(bank(n % 4), 2), ACT.Copy).then_inc(sem("proj_out"), 1)
                    n += 1
                gla_exps(l)
                ru = IN_AT[l] + 2
                act.wait_ge(ring_full[lap(ru)[0]], 16 * (lap(ru)[1] + 1))
                S.activation(router[:, :], ringv[:, lap(ru)[0], KC * 384:KC * 400], ACT.Copy).then_inc(sem("router_in"), 1)
                gg = width(l) // P
                for t in range(NT):
                    act.wait_ge(sem("proj"), n + 1 + l * PER["proj"])
                    m = 384 if t < gg else P
                    S.activation(TM[:, t, TM_SV:TM_SV + m], bank(n % 4, m), ACT.Copy).then_inc(sem("proj_out"), 1)
                    n += 1
                project_out(l, 3, fm_parts(l, 3))
                gla_keys(l)
                project_out(l, 4, fm_parts(l, 4))
                gla_queries(l)
                gla_gate(l)
                attend(l)
                gate_rows(l, "a")
                post(l, "a")
                norm_rows(l, "f")
                ffn(l)
                gate_rows(l, "f")
                post(l, "f")

        @block.vector
        def _(dve):
            link = Chain(dve, "dve_chain")
            dve.wait_ge(sem("c_in"), 16)
            dve.wait_ge(sem("c_exp"), 1)
            link(V.tensor_scalar(CTMP[:, 0:16], CTMP[:, 0:16], 1.0, None, ALU.add))
            link(V.reciprocal(CTMP[:, 0:16], CTMP[:, 0:16]))
            dve.wait_ge(sem("c_zero"), 1)
            V.tensor_tensor(CS32[:, :, 0:2], CS.rearrange("p (k w) -> p k w", w=2), CTMP.rearrange("p (k w) -> p k w", w=2), ALU.mult)\
                .then_inc(sem("silu_c"), 1)

            def mod_out(l):
                dve.wait_ge(sem("param_in"), 16)
                dve.wait_ge(sem("modcol"), (l + 1) * MOD_UNITS)
                V.tensor_tensor(modc[:, l * 96:(l + 1) * 96], bank(6, 96, 384),
                                prm[:, l * PARAMS + P_BMOD:l * PARAMS + P_BMOD + 96], ALU.add).then_inc(sem("mod_out"), 1)
                dve.wait_ge(sem("mod_out"), l + 1)

            def mod_cols(l):
                for s in range(2):
                    gain = prm[:, l * PARAMS + P_GAIN + 16 * s:l * PARAMS + P_GAIN + 16 * s + KC]
                    for wch in range(2):
                        sh = modv[:, l, 24 * s:24 * s + 8, wch]
                        sc = modv[:, l, 24 * s + 8:24 * s + 16, wch]
                        V.scalar_tensor_tensor(colv[:, s, wch, 0, :], sc, 1.0, gain, ALU.add, ALU.mult)
                        link(V.tensor_copy(colv[:, s, wch, 1, :], sh))

            def h_out(l, half):
                s = 0 if half == "a" else 1
                ctx_too = half == "a" or l < DEPTH - 1
                for k in range(KC):
                    for wch, (t0, n) in enumerate([(0, LAT), (LAT, CTX)][:2 if ctx_too else 1]):
                        dve.wait_ge(sem("xT"), (2 if ctx_too else 1) * k + wch + 1 + before("xT", l, half))
                        V.tensor_scalar(hTv[:, k, t0:t0 + n], bank(2 * (k % 2) + wch, n), colv[:, s, wch, 0, k:k + 1],
                                        colv[:, s, wch, 1, k:k + 1], ALU.mult, ALU.add).then_inc(sem("h_t"), 1)

            def gla_decay(l):
                p0 = l * PARAMS
                for d in range(2):
                    dve.wait_ge(sem("z"), d + 1 + l * PER["z"])
                    bias = prm[:, p0 + P_AB + d:p0 + P_AB + d + 1]
                    V.tensor_scalar(E[d][:, 0:LAT], bank(4 + d), bias, None, ALU.add)
                    V.tensor_scalar(E[d][:, LAT:TOK], bank(6 + d, CTX), bias, None, ALU.add).then_inc(sem("z_out"), 1)
                for d in range(2):
                    dve.wait_ge(sem("softplus"), d + 1 + l * PER["softplus"])
                    link(V.tensor_scalar(E[d], E[d], 0.0, 1.0 / TAU, ALU.min, ALU.mult))
                    link(V.scalar_tensor_tensor(E[d], E[2 + d], -1.0 / TAU, E[d], ALU.mult, ALU.add))
                    for t in range(NT):
                        c = slice(t * P, (t + 1) * P)
                        V.tensor_tensor_scan(CUM[d][:, c], ones[:, :], E[d][:, c], 0.0, ALU.mult, ALU.add)\
                            .then_inc(sem("scan"), 1)
                    dve.wait_ge(sem("scan"), NT * (d + 1) + l * PER["scan"])
                c3 = [v3(CUM[d], NT) for d in range(2)]
                for d in range(2):
                    V.tensor_copy(v3(gss[:, 6 * d:6 * d + 6], NT), c3[d][:, :, P - 1:P]).then_inc(sem("totc"), 1)
                dve.wait_ge(sem("totc"), 2 + l * PER["totc"])
                tot_b = gss[:, 6:12].unsqueeze(2).broadcast_to([P, NT, P])
                link(V.tensor_tensor(c3[1], tot_b, c3[1], ALU.subtract))
                link(V.tensor_tensor(CUM[1], CUM[1], E[1], ALU.add))
                for d in range(2):
                    tot = gss[:, 6 * d:6 * d + 6].unsqueeze(2).broadcast_to([P, NT, P])
                    V.tensor_tensor(v3(E[d], NT), tot, c3[d], ALU.subtract).then_inc(sem("ke_arg"), 1)

            def gla_state(l):
                dve.wait_ge(sem("proj_out"), 2 + l * PER["proj_out"])
                for d in range(2):
                    dve.wait_ge(sem("ke_exp"), d + 1 + l * PER["ke_exp"])
                    V.tensor_tensor(E[d], E[d], FM[:, GK, :], ALU.mult).then_inc(sem("ke"), 1)
                V.memset(STATE[0][:, F_ORD[0], :], 0.0)
                link(V.memset(STATE[1][:, B_ORD[0], :], 0.0))
                dve.wait_ge(sem("tot_exp"), 1 + l * PER["tot_exp"])
                hm = cst[:, C_HM:C_HM + GLA_H]
                for i in range(NT - 1):
                    dve.wait_ge(sem("dS"), i + 1 + l * PER["dS"])
                    hmb = hm.unsqueeze(2).broadcast_to([P, GLA_H, DV])
                    for d, order in enumerate((F_ORD, B_ORD)):
                        V.tensor_tensor(v3(bank(4 + i % 2, 256, 256 * d), GLA_H), v3(bank(4 + i % 2, 256, 256 * d), GLA_H), hmb,
                                        ALU.mult).then_inc(sem("dSm"), 1)
                    dve.wait_ge(sem("dSm"), 2 * i + 2 + l * PER["dSm"])
                    for d, order in enumerate((F_ORD, B_ORD)):
                        a, b = order[i], order[i + 1]
                        V.scalar_tensor_tensor(STATE[d][:, b, :], STATE[d][:, a, :], grs[:, 6 * d + a:6 * d + a + 1],
                                               bank(4 + i % 2, 256, 256 * d), ALU.mult, ALU.add).then_inc(sem("state"), 1)
                    dve.wait_ge(sem("state"), 2 * i + 2 + l * PER["state"])

            def rope(l):
                for i, b in enumerate([SK, SQ, SQ + 1, SQ + 2, SQ + 3]):
                    dve.wait_ge(sem("rot"), i + 1 + l * PER["rot"])
                    V.tensor_tensor(A_TMP, bank(6 + i % 2), cst[:, C_SIN:C_SIN + LAT], ALU.mult)
                    link(V.tensor_tensor(FM[:, b, 0:LAT], FM[:, b, 0:LAT], cst[:, C_COS:C_COS + LAT], ALU.mult))
                    V.tensor_tensor(FM[:, b, 0:LAT], FM[:, b, 0:LAT], A_TMP, ALU.add).then_inc(sem("rope"), 1)
                    dve.wait_ge(sem("rope"), i + 1 + l * PER["rope"])

            def gla_queries(l):
                n = width(l)
                nt = n // P
                dve.wait_ge(sem("keT"), 3 + l * PER["keT"])
                for d in range(2):
                    c3 = v3(CUM[d], NT)[:, 0:nt, :]
                    mid = c3[:, :, P // 2:P // 2 + 1].broadcast_to([P, nt, P])
                    link(V.tensor_tensor(v3(E[3 * d + 2][:, 0:n], nt), c3, mid, ALU.subtract))
                    V.tensor_scalar(E[3 * d][:, 0:n], E[3 * d + 2][:, 0:n], 80.0, None, ALU.min).then_inc(sem("q_arg"), 1)
                    V.tensor_scalar(E[3 * d + 1][:, 0:n], E[3 * d + 2][:, 0:n], -80.0, -1.0, ALU.max, ALU.mult)\
                        .then_inc(sem("q_arg"), 1)
                    dve.wait_ge(sem("q_arg"), 3 * d + 2 + l * PER["q_arg"])
                    V.tensor_copy(E[3 * d + 2][:, 0:n], CUM[d][:, 0:n]).then_inc(sem("q_arg"), 1)
                dve.wait_ge(sem("q_arg"), 6 + l * PER["q_arg"])
                q = FM[:, GQ, 0:n]
                for d in range(2):
                    for i in range(3):
                        dve.wait_ge(sem("q_exp"), 3 * d + i + 1 + l * PER["q_exp"])
                        src = FM[:, GK, 0:n] if i == 1 else q
                        V.scalar_tensor_tensor(E[3 * d + i][:, 0:n], E[3 * d + i][:, 0:n], 1.0 if i == 1 else DK ** -0.5,
                                               src, ALU.mult, ALU.mult).then_inc(sem("qk"), 1)
                dve.wait_ge(sem("qk"), 6 + l * PER["qk"])

            def gla_out(l):
                hmb = cst[:, C_HM:C_HM + GLA_H].unsqueeze(2).broadcast_to([P, GLA_H, P])
                ts = tiles(l)
                for i, t in enumerate(ts):
                    c = slice(t * P, (t + 1) * P)
                    if i:
                        dve.wait_ge(sem("scores"), i + l * PER["scores"])
                    for d in range(2):
                        V.tensor_tensor(v3(QBLK[d], GLA_H), E[3 * d][:, c].unsqueeze(1).broadcast_to([P, GLA_H, P]), hmb,
                                        ALU.mult).then_inc(sem("qblk"), 1)
                    dve.wait_ge(sem("scores"), i + 1 + l * PER["scores"])
                    if i:
                        dve.wait_ge(sem("o"), i + l * PER["o"])
                    for d, (m, dst) in enumerate(((C_MF, A_SB), (C_MB, A_TMP))):
                        link(V.tensor_tensor(v3(dst, GLA_H), v3(bank(4 + d), GLA_H),
                                             cst[:, m:m + P].unsqueeze(1).broadcast_to([P, GLA_H, P]), ALU.mult))
                    V.tensor_tensor(A_SB, A_SB, A_TMP, ALU.add).then_inc(sem("A"), 1)
                    dve.wait_ge(sem("o"), i + 1 + l * PER["o"])
                    V.tensor_copy(glao[:, t * 256:(t + 1) * 256], bank(6 + i % 2, 256)).then_inc(sem("o_out"), 1)
                nt = len(ts)
                n = nt * 256
                dve.wait_ge(sem("o_out"), nt + l * PER["o_out"])
                sq = w(2048, n)
                link(V.tensor_tensor(sq, glao[:, 0:n], glao[:, 0:n], ALU.mult))
                V.reduce_sum(gss[:, 0:4 * nt], v3(sq, 4 * nt), AX).then_inc(sem("gla_ms"), 1)
                dve.wait_ge(sem("gla_rs"), 1 + l * PER["gla_rs"])
                dve.wait_ge(sem("gate_exp"), 1 + l * PER["gate_exp"])
                link(V.tensor_scalar(w(0, n), w(0, n), 1.0, None, ALU.add))
                link(V.reciprocal(w(0, n), w(0, n)))
                link(V.tensor_tensor(v3(w(0, n), nt), v3(w(0, n), nt), TM[:, 0:nt, TM_GG:TMW], ALU.mult))
                g0 = l * PARAMS + P_GG
                link(V.tensor_tensor(v3(w(0, n), 4 * nt), v3(w(0, n), 4 * nt),
                                     prm[:, g0:g0 + DV].unsqueeze(1).broadcast_to([P, 4 * nt, DV]), ALU.mult))
                link(V.tensor_tensor(v3(glao[:, 0:n], 4 * nt), v3(glao[:, 0:n], 4 * nt),
                                     grs[:, 0:4 * nt].unsqueeze(2).broadcast_to([P, 4 * nt, DV]), ALU.mult))
                V.tensor_tensor(glao[:, 0:n], glao[:, 0:n], w(0, n), ALU.mult).then_inc(sem("gla_o"), 1)
                dve.wait_ge(sem("gla_o"), 1 + l * PER["gla_o"])

            def attend(l):
                us = units(l)
                nb = 0
                for u in range(len(us) + 3):
                    if u < len(us):
                        ti, t, kind, h = us[u]
                        k0, nl = local_keys(t)
                        dve.wait_ge(sem("s"), u + 1 + l * PER["s"])
                        if u >= 2:
                            dve.wait_ge(sem("exp"), u - 1 + l * PER["exp"])
                        st = AST[:, 8 * (u % 4):8 * (u % 4) + 8]
                        if nl:
                            if kind == "n":
                                dve.wait_ge(sem(f"bias{nb % 4}"), 16 * (nb // 4 + 1) + l * PER["bias"])
                                add = BIAS[nb % 4]
                                nb += 1
                            else:
                                off = C_BAND + (P if t == 0 else 0)
                                add = cst[:, off:off + nl]
                            V.reduce_max(st[:, 1:2], bank(2 * (u % 2) + 1, CTX), AX)
                            link(V.scalar_tensor_tensor(SC[u % 2][:, 0:nl], bank(2 * (u % 2), nl), SCALE, add[:, 0:nl], ALU.mult, ALU.add))
                            link(V.reduce_max(st[:, 0:1], SC[u % 2][:, 0:nl], AX))
                            link(V.tensor_scalar(st[:, 3:4], st[:, 1:2], SCALE, st[:, 0:1], ALU.mult, ALU.max))
                        else:
                            link(V.reduce_max(st[:, 1:2], bank(2 * (u % 2) + 1, CTX), AX))
                            link(V.tensor_scalar(st[:, 3:4], st[:, 1:2], SCALE, None, ALU.mult))
                        if kind == "s":
                            orig = h // 2 + 4 * (h % 2)
                            sink = prm[:, l * PARAMS + P_SINK + orig:l * PARAMS + P_SINK + orig + 1]
                            V.tensor_scalar(st[:, 2:3], st[:, 3:4], sink, -1.0, ALU.max, ALU.mult).then_inc(sem("max"), 1)
                        else:
                            V.tensor_scalar(st[:, 2:3], st[:, 3:4], -1.0, None, ALU.mult).then_inc(sem("max"), 1)
                    v = u - 1
                    if 0 <= v < len(us):
                        ti, t, kind, h = us[v]
                        dve.wait_ge(sem("exp"), v + 1 + l * PER["exp"])
                        if v >= 2:
                            dve.wait_ge(sem("T"), v - 1 + l * PER["T"])
                        st = AST[:, 8 * (v % 4):8 * (v % 4) + 8]
                        terms = ([4] if t < NLT else []) + [5] + ([6] if kind == "s" else [])
                        den = st[:, 5:6]
                        if len(terms) == 3:
                            den = st[:, 7:8]
                            link(V.tensor_scalar(den, st[:, 4:5], st[:, 5:6], st[:, 6:7], ALU.add, ALU.add))
                        elif len(terms) == 2:
                            den = st[:, 7:8]
                            link(V.tensor_tensor(den, st[:, terms[0]:terms[0] + 1], st[:, terms[1]:terms[1] + 1], ALU.add))
                        link(V.reciprocal(st[:, 3:4], den))
                        V.tensor_scalar(RDIAG[v % 2], ident, st[:, 3:4], None, ALU.mult).then_inc(sem("diagr"), 1)
                    v = u - 3
                    if v >= 0 and v % 2:
                        ti, t, kind, h = us[v]
                        dve.wait_ge(sem("pv"), v // 2 + 1 + l * PER["pv"])
                        o = bank(6, P)
                        if kind == "n" and t < NLT:
                            dst = by_column(hTv[:, 2 + h // 2, 0:LAT], False)[:, 16 * t:16 * (t + 1), :]
                            V.tensor_copy(dst, by_column(o, True)).then_inc(sem("mix"), 1)
                        else:
                            k = 2 + h // 2 if kind == "n" else 4 + h // 2
                            V.tensor_copy(hTv[:, k, t * P:(t + 1) * P], o).then_inc(sem("mix"), 1)

            def gate_rows(l, half):
                s = 0 if half == "a" else 1
                if half == "a":
                    dve.wait_ge(sem("pv"), len(units(l)) // 2 + l * PER["pv"])
                for wch in range(2 if l < DEPTH - 1 else 1):
                    g0 = l * PARAMS + P_GAIN + 16 * s + 8
                    link(V.tensor_tensor(gcol[:, 8 * wch:8 * wch + 8], modv[:, l, 24 * s + 16:24 * s + 24, wch], prm[:, g0:g0 + KC], ALU.mult))
                    V.tensor_tensor(v3(DIAG[wch], KC), ident.unsqueeze(1).broadcast_to([P, KC, P]),
                                    gcol[:, 8 * wch:8 * wch + 8].unsqueeze(2).broadcast_to([P, KC, P]), ALU.mult)\
                        .then_inc(sem("diag"), 1)

            def post(l, half):
                dve.wait_ge(sem("grow_out"), 1 + before("grow_out", l, half))
                for i, t in enumerate(tiles(l)):
                    dve.wait_ge(sem("prs"), i + 1 + before("prs", l, half))
                    src = ps[:, (i % 2) * D:(i % 2) * D + D] if half == "a" else ACC[:, t, :]
                    V.scalar_tensor_tensor(YT_, src, rs[:, t:t + 1], GROW[:, 0 if t < NLT else 1, :], ALU.mult, ALU.mult)\
                        .then_inc(sem("y_used"), 1)
                    dve.wait_ge(sem("y_used"), i + 1 + before("y_used", l, half))
                    if half == "a":
                        dve.wait_ge(sem(f"x_back{t}"), 16 * (l + 1 if t < NLT else 1))
                        done, n = "x_mid", i + 1 + l * PER["x_mid"]
                    else:
                        dve.wait_ge(sem(f"x_again{t}"), 16 * (l + 1 if t < NLT else 1))
                        done, n = ("x_ready", t + 1 + l * NLT) if t < NLT else ("xc_ready", t - NLT + 1)
                    V.tensor_tensor(X[:, t, :], X[:, t, :], YT_, ALU.add).then_inc(sem(done), 1)
                    dve.wait_ge(sem(done), n)

            def route(l):
                nt = len(tiles(l))
                ctx_too = l < DEPTH - 1
                dve.wait_ge(sem("logits"), 1 + l * PER["logits"])
                lg = v3(bank(6, NT * NE), NT)[:, 0:nt, :]
                st = AFM
                link(V.reduce_max(st[:, 0:nt], lg, AX))
                V.tensor_tensor(LOG[:, 0:nt, :], lg, st[:, 0:nt].unsqueeze(2).broadcast_to([P, nt, NE]), ALU.subtract)\
                    .then_inc(sem("logit_sub"), 1)
                link(V.memset(AFF, -1.0))
                dve.wait_ge(sem("logit_exp"), 1 + l * PER["logit_exp"])
                link(V.reduce_sum(st[:, 8:8 + nt], LOG[:, 0:nt, :], AX))
                link(V.reciprocal(st[:, 8:8 + nt], st[:, 8:8 + nt]))
                if ctx_too:
                    V.tensor_tensor(AFF[:, 0:NCT, 32:48], LOG[:, NLT:NT, :], st[:, 12:14].unsqueeze(2).broadcast_to([P, NCT, NE]), ALU.mult)
                V.tensor_tensor(AFF[:, :, 0:NE], LOG[:, 0:NLT, :], st[:, 8:12].unsqueeze(2).broadcast_to([P, NLT, NE]), ALU.mult)\
                    .then_inc(sem("aff"), 1)
                dve.wait_ge(sem("affT"), 1 + l * PER["affT"])
                a = [AFT0[0:48, 0:LAT], AFT1[0:48, 0:LAT]]
                link(V.tensor_copy(a[0], ps[0:48, 7 * 512:8 * 512]))
                for r in range(CAP_L // 8):
                    sl = slice(8 * r, 8 * r + 8)
                    src, dst = a[r % 2], a[(r + 1) % 2]
                    link(V.max(VALS[0:48, sl], src))
                    V.max_index(idxu[0:48, sl], VALS[0:48, sl], src)
                    link(V.match_replace(dst, VALS[0:48, sl], src, -1.0))
                V.tensor_copy(IDXF[0:48, :], idxu[0:48, :]).then_inc(sem("picked"), 1)

            def ffn(l):
                ctx_too = l < DEPTH - 1
                base = FFN_AT[l]
                nt = len(tiles(l))
                per = 2 * nt
                dve.wait_ge(sem("idx_in"), l * 32 + (32 if ctx_too else 16))
                dve.wait_ge(sem("acc_zero"), nt + l * PER["acc_zero"])
                if ctx_too:
                    link(V.memset(HIDC[0:64, :], 0.0))

                def select(i):
                    for t in range(NLT):
                        last = V.tensor_scalar(SEL_L[:, t, :], IDXL[:, bass.ts(i, P)], cst[:, C_IOTA + t:C_IOTA + t + 1], None, ALU.is_equal)
                    if ctx_too:
                        for t in range(NCT):
                            last = V.tensor_scalar(SEL_C[:, t, :], IDXC[:, bass.ts(i, 64)], cst[:, C_IOTA + t:C_IOTA + t + 1], None, ALU.is_equal)
                    last.then_inc(sem("sel"), 1)

                def slots(i):
                    for sw in range(2):
                        last = V.tensor_scalar(PT_L[sw], IOTAR, COLS_L[:, sw, bass.ds(i, 1)], COLS_L[:, 2 + sw, bass.ds(i, 1)],
                                               ALU.is_equal, ALU.mult)
                        if ctx_too:
                            last = V.tensor_scalar(PT_C[sw], IOTAR[:, 0:CTX], COLS_C[:, sw, bass.ds(i, 1)], COLS_C[:, 2 + sw, bass.ds(i, 1)],
                                                   ALU.is_equal, ALU.mult)
                    last.then_inc(sem("ptok"), 1)

                def picked_ctx(i):
                    dve.wait_ge(sem("gather"), i * 3 + 3)
                    for k in range(KC):
                        last = V.tensor_scalar(XST[:, k, :, CAP_L:CW], v3(bank(1, 64, k * 64), 2), colv[:, 1, 1, 0, k:k + 1],
                                               colv[:, 1, 1, 1, k:k + 1], ALU.mult, ALU.add)
                    last.then_inc(sem("xs_ctx"), 1)

                def add(i):
                    for c in range(per):
                        t, half = tiles(l)[c // 2], c % 2
                        dve.wait_ge(sem("comb"), i * per + (c + 1 + l * PER["comb"]))
                        d = ACC[:, t, half * 512:half * 512 + 512]
                        V.tensor_tensor(d, d, bank(COMB_BANKS[c % 3]), ALU.add).then_inc(sem("acc"), 1)

                def expert(i, e, first, last_pair):
                    dve.wait_ge(sem("silu"), i * 2 + (e + 1 + l * NE))
                    V.tensor_tensor(HIDL, SGL, bank(1), ALU.mult).then_inc(sem("hid"), 1)
                    if ctx_too:
                        dve.wait_ge(sem("silu_ctx"), i * 2 + (e + 1))
                        V.tensor_tensor(HIDC[64:P, :], SGC[64:P, :], bank(2)[64:P, :], ALU.mult).then_inc(sem("hid_c"), 1)
                    if e == 0 and not first:
                        add(i - 1)
                    if e == 0:
                        if first:
                            dve.wait_ge(sem("cols_in"), picks(l) + l * picks(0))
                            dve.wait_ge(sem("iota"), 16 + l * PER["iota"])
                        slots(i)
                        if not last_pair:
                            select(i + 1)
                    elif ctx_too and not last_pair:
                        picked_ctx(i + 1)

                select(0)
                if ctx_too:
                    picked_ctx(0)
                for e in range(2):
                    expert(0, e, True, False)
                with dve.Fori(1, PAIRS - 1) as i:
                    for e in range(2):
                        expert(i, e, False, False)
                for e in range(2):
                    expert(PAIRS - 1, e, False, True)
                dve.wait_ge(sem("acc"), (PAIRS - 1) * per + l * PER["acc"])
                add(PAIRS - 1)

            mod_out(0)
            for l in range(DEPTH):
                mod_cols(l)
                dve.wait_ge(sem("const_in"), 16)
                h_out(l, "a")
                gla_decay(l)
                gla_state(l)
                gla_queries(l)
                rope(l)
                gla_out(l)
                attend(l)
                if l == 0:
                    mod_out(1)
                gate_rows(l, "a")
                post(l, "a")
                h_out(l, "f")
                route(l)
                ffn(l)
                dve.wait_ge(sem("acc"), acc_total(l))
                gate_rows(l, "f")
                post(l, "f")

        @block.tensor
        def _(pe):
            def arrived(n):
                pe.wait_ge(ring_full[lap(n)[0]], 16 * (lap(n)[1] + 1))
                return ringv[:, lap(n)[0], :]

            def mod_rows(l, k, ob):
                n = MOD_AT[l] + k
                u = v3(arrived(n), KC)
                for kc in range(KC):
                    j = kc % 4
                    last = T.matmul(ob[32 * j:32 * j + 32, :], CS32[:, kc, :], u[:, kc, :], start=kc < 4, stop=kc >= 4)
                last.then_inc(sem("modrow"), 1)
                pe.drain().then_inc(ring_used[lap(n)[0]], 1)

            def mod_cols(l, k, row):
                pe.wait_ge(sem("modrow_out"), k + 1 + l * MOD_UNITS)
                for j in range(4):
                    last = T.matmul(bank(6, 2, 384 + 2 * (4 * k + j)), row[:, j * P:(j + 1) * P], cst[:, C_SUM:C_SUM + 2], start=True, stop=True)
                last.then_inc(sem("modcol"), 1)

            def turn_x(l, half):
                ctx_too = half == "a" or l < DEPTH - 1
                pe.wait_ge(sem("xn"), (NT if half == "a" else len(tiles(l))) + before("xn", l, half))
                per = 2 if ctx_too else 1
                for k in range(KC):
                    if k >= 2:
                        pe.wait_ge(sem("h_t"), per * (k - 1) + before("h_t", l, half))
                    for wch in range(per):
                        t0 = NLT * wch
                        for t in range(NLT if wch == 0 else NCT):
                            last = T.transpose(bank(2 * (k % 2) + wch, P, t * P), XN[:, t0 + t, k * P:(k + 1) * P], ident)
                        last.then_inc(sem("xT"), 1)
                pe.wait_ge(sem("h_t"), per * KC + before("h_t", l, half))

            def project(l, unit):
                n = n_items(l, unit)
                g = IN_AT[l] + unit
                uw = arrived(g)

                def free(n):
                    if n >= 4:
                        pe.wait_ge(sem("proj_out"), n - 3 + l * PER["proj_out"])

                if unit in (1, 2):
                    cols_ = 512 if unit == 1 else 384
                    v = v3(uw[:, 0:KC * cols_], KC)
                    if unit == 1:
                        for b in range(2):
                            free(n)
                            for kc in range(KC):
                                last = T.matmul(bank(n % 4), v[:, kc, 256 + b * P:256 + (b + 1) * P], hTv[:, kc, 0:LAT],
                                                start=kc == 0, stop=kc == KC - 1)
                            last.then_inc(sem("proj"), 1)
                            n += 1
                    for t in range(NT):
                        free(n)
                        k_ = 256 if unit == 1 and t < NLT else P if unit == 2 and t * P >= width(l) else cols_
                        for kc in range(KC):
                            last = T.matmul(bank(n % 4, k_), hTv[:, kc, t * P:(t + 1) * P], v[:, kc, 0:k_], start=kc == 0, stop=kc == KC - 1)
                        last.then_inc(sem("proj"), 1)
                        n += 1
                    if unit == 1:
                        for j in range(2):
                            free(n)
                            for i in range(4):
                                t, b = 2 * j + i // 2, i % 2
                                last = T.transpose(bank(n % 4, P, i * P), FM[:, NQ + b, t * P:(t + 1) * P], ident)
                            last.then_inc(sem("proj"), 1)
                            n += 1
                    if unit == 2:
                        pe.wait_ge(sem("router_in"), 1 + l * PER["router_in"])
                else:
                    for j, b, t0, tn in fm_items(l, unit):
                        free(n)
                        m = 48 if b == AL else P
                        for kc in range(KC):
                            last = T.matmul(bank(n % 4, tn)[0:m, :], uw[:, j * D + kc * P:j * D + kc * P + m], hTv[:, kc, t0:t0 + tn],
                                            start=kc == 0, stop=kc == KC - 1)
                        last.then_inc(sem("proj"), 1)
                        n += 1
                pe.drain().then_inc(ring_used[lap(g)[0]], 1)

            def gla_z(l):
                pe.wait_ge(sem("proj_out"), n_items(l, 1) + l * PER["proj_out"])
                aup = prm[:, l * PARAMS + P_AUP:l * PARAMS + P_AUP + P]
                for d in range(2):
                    r = slice(32 * d, 32 * d + 16)
                    T.matmul(bank(4 + d), aup[r, :], FM[r, AL, 0:LAT], start=True, stop=True)
                    T.matmul(bank(6 + d, CTX), aup[r, :], FM[r, AL, LAT:TOK], start=True, stop=True).then_inc(sem("z"), 1)

            def gla_keys(l):
                pe.wait_ge(sem("ke"), 2 + l * PER["ke"])
                for g in range(3):
                    for j in range(4):
                        n = 4 * g + j
                        last = T.transpose(bank(4 + g, P, j * P), E[n // NT][:, (n % NT) * P:(n % NT + 1) * P], ident)
                    last.then_inc(sem("keT"), 1)
                pe.wait_ge(sem("keT_out"), 1 + l * PER["keT_out"])
                for i in range(NT - 1):
                    if i >= 2:
                        pe.wait_ge(sem("state"), 2 * (i - 1) + l * PER["state"])
                    for d, order in enumerate((F_ORD, B_ORD)):
                        t = order[i]
                        last = T.matmul(bank(4 + i % 2, 256, 256 * d), KET[:, NT * d + t, :], TM[:, t, TM_GV:TM_GV + 256], start=True, stop=True)
                    last.then_inc(sem("dS"), 1)

            def rot(l):
                pe.wait_ge(sem("proj_out"), n_items(l, 5) + l * PER["proj_out"])
                for i, b in enumerate([SK, SQ, SQ + 1, SQ + 2, SQ + 3]):
                    if i >= 2:
                        pe.wait_ge(sem("rope"), i - 1 + l * PER["rope"])
                    T.matmul(bank(6 + i % 2), cst[:, C_ROT:C_ROT + P], FM[:, b, 0:LAT], start=True, stop=True).then_inc(sem("rot"), 1)

            def gla_out(l):
                pe.wait_ge(sem("qk"), 6 + l * PER["qk"])
                pe.wait_ge(sem("rope"), 5 + l * PER["rope"])
                for i, t in enumerate(tiles(l)):
                    c = slice(t * P, (t + 1) * P)
                    pe.wait_ge(sem("qblk"), 2 * i + 2 + l * PER["qblk"])
                    for d in range(2):
                        last = T.matmul(bank(4 + d), E[3 * d + 1][:, c], QBLK[d], start=True, stop=True)
                    last.then_inc(sem("scores"), 1)
                    if i >= 2:
                        pe.wait_ge(sem("o_out"), i - 1 + l * PER["o_out"])
                    for d in range(2):
                        T.matmul(bank(6 + i % 2, 256), E[3 * d + 2][:, c], STATE[d][:, t, :], start=d == 0, stop=False)
                    pe.wait_ge(sem("A"), i + 1 + l * PER["A"])
                    for h in range(GLA_H):
                        last = T.matmul(bank(6 + i % 2, DV, h * DV), A_SB[:, h * P:(h + 1) * P], TM[:, t, TM_GV + h * DV:TM_GV + (h + 1) * DV],
                                        start=False, stop=h == GLA_H - 1)
                    last.then_inc(sem("o"), 1)

            def attend(l):
                us = units(l)
                nt = width(l) // P
                pe.wait_ge(sem("gla_o"), (l + 1) * PER["gla_o"])
                for k in range(2):
                    for t in range(nt):
                        last = T.transpose(ps[:, 4 * 512 + k * TOK + t * P:4 * 512 + k * TOK + (t + 1) * P],
                                           glao[:, t * 256 + k * P:t * 256 + (k + 1) * P], ident)
                last.then_inc(sem("glaT"), 1)
                pe.wait_ge(sem("keys"), 6 * (l + 1))

                def scores(u):
                    ti, t, kind, h = us[u]
                    k0, nl = local_keys(t)
                    qb, kb = (NQ + h // 2, NK + h // 2) if kind == "n" else (SQ + h // 2, SK)
                    if h % 2:
                        kb = dict(KEY_COPY)[kb]
                    q = FM[:, qb, t * P:(t + 1) * P]
                    if u >= 2:
                        pe.wait_ge(sem("exp"), u - 1 + l * PER["exp"])
                    if nl:
                        T.matmul(bank(2 * (u % 2), nl), q, FM[:, kb, k0:k0 + nl], start=True, stop=True)
                    T.matmul(bank(2 * (u % 2) + 1, CTX), q, FM[:, kb, LAT:TOK], start=True, stop=True).then_inc(sem("s"), 1)

                def mod_unit(u):
                    return 2 * (u // UPT) + u % UPT // 6 if u % UPT in (4, 10) else None

                def products(u):
                    if u == 0:
                        pe.wait_ge(sem("glaT_out"), l + 1)
                    pe.wait_ge(sem("pt_out"), u + 2 + l * PER["pt_out"])
                    if u >= 2:
                        pe.wait_ge(sem("mix"), u // 2 + l * PER["mix"])
                    k = mod_unit(u)
                    if l == 0 and k:
                        mod_cols(1, k - 1, MODROW)
                    t = us[u][1]
                    k0, nl = local_keys(t)
                    kt = [k0 // P + j for j in range(nl // P)] + [NLT, NLT + 1]
                    for j, tk in enumerate(kt):
                        for v in (u, u + 1):
                            kind, h = us[v][2:]
                            c = TM_NV + h * HD if kind == "n" else TM_SV + (h % 2) * HD
                            r_ = 64 * (v % 2)
                            last = T.matmul(bank(6, P)[r_:r_ + 64, :], TM[:, tk, c:c + HD], PT[v % 4][:, j * P:(j + 1) * P],
                                            start=j == 0, stop=j == len(kt) - 1)
                    last.then_inc(sem("pv"), 1)

                scores(0)
                for u in range(len(us) + 3):
                    if u + 1 < len(us):
                        scores(u + 1)
                    v = u - 1
                    if 0 <= v < len(us):
                        nk = (local_keys(us[v][1])[1] + CTX) // P
                        pe.wait_ge(sem("diagr"), v + 1 + l * PER["diagr"])
                        if v == 0:
                            pe.wait_ge(sem("glaT_out"), l + 1)
                        if v >= 1:
                            pe.wait_ge(sem("pt_out"), v + l * PER["pt_out"])
                        for j in range(nk):
                            last = T.matmul(ps[:, 4 * 512 + j * P:4 * 512 + (j + 1) * P], PR[v % 2][:, j * P:(j + 1) * P], RDIAG[v % 2],
                                            start=True, stop=True)
                        last.then_inc(sem("T"), 1)
                    v = u - 3
                    if v >= 0 and v % 2 == 0:
                        products(v)
                        if l == 0 and mod_unit(v) is not None:
                            mod_rows(1, mod_unit(v), bank(7))
                if l == 0:
                    pe.wait_ge(sem("mix"), len(us) // 2)
                    mod_cols(1, MOD_UNITS - 1, MODROW)

            def gate_rows(l, half):
                n = 2 if l < DEPTH - 1 else 1
                if half == "a":
                    pe.wait_ge(sem("mix"), len(units(l)) // 2 + l * PER["mix"])
                    if l == 0:
                        pe.wait_ge(sem("mod_out"), 2)
                for wch in range(n):
                    pe.wait_ge(sem("diag"), wch + 1 + before("diag", l, half))
                    for j in range(2):
                        last = T.matmul(bank(4 + 2 * wch + j), ones[:, :], DIAG[wch][:, j * 512:(j + 1) * 512], start=True, stop=True)
                    last.then_inc(sem("grow"), 1)

            def w_out(l):
                u = [v3(arrived(OUT_AT[l] + j), KC) for j in range(2)]
                for i, t in enumerate(tiles(l)):
                    if i >= 2:
                        pe.wait_ge(sem("y_used"), i - 1 + before("y_used", l, "a"))
                    for j in range(2):
                        for kc in range(KC):
                            last = T.matmul(bank(2 * (i % 2) + j), hTv[:, kc, t * P:(t + 1) * P], u[j][:, kc, :], start=kc == 0, stop=kc == KC - 1)
                    last.then_inc(sem("wo"), 1)
                for j in range(OUT_UNITS):
                    pe.drain().then_inc(ring_used[lap(OUT_AT[l] + j)[0]], 1)

            def route(l):
                ts = tiles(l)
                for t in sorted(ts):
                    for kc in range(KC):
                        last = T.matmul(bank(6, NE, t * NE), hTv[:, kc, t * P:(t + 1) * P], router[:, kc * NE:(kc + 1) * NE],
                                        start=kc == 0, stop=kc == KC - 1)
                last.then_inc(sem("logits"), 1)
                pe.wait_ge(sem("aff"), 1 + l * PER["aff"])
                for t in range(NLT):
                    last = T.transpose(ps[0:48, 7 * 512 + t * P:7 * 512 + (t + 1) * P], AFF[:, t, :], ident)
                last.then_inc(sem("affT"), 1)
                pe.wait_ge(sem("picked"), 1 + l * PER["picked"])

            def ffn(l):
                ctx_too = l < DEPTH - 1
                base = FFN_AT[l]
                nt = len(tiles(l))
                per = 2 * nt
                gate_up = [v3(slot[j], 2) for j in range(4)]
                down = [v3(slot[4 + j], 4) for j in range(2)]

                def gather(i, g):
                    for k in range(4):
                        c0 = (4 * g + k) * P
                        for t in range(NLT):
                            last = T.matmul(bank((7, 0)[g], P, k * P), XN[:, t, c0:c0 + P], SEL_L[:, t, :], start=t == 0, stop=t == NLT - 1)
                    last.then_inc(sem("gather"), 1)

                def gather_ctx(i):
                    for k in range(KC):
                        for t in range(NCT):
                            last = T.matmul(bank(1, 64, k * 64), XN[:, NLT + t, k * P:(k + 1) * P], SEL_C[:, t, :], start=t == 0, stop=t == NCT - 1)
                    last.then_inc(sem("gather"), 1)

                def combine(i, cs, wait_hid=None):
                    for c in cs:
                        t, half = tiles(l)[c // 2], c % 2
                        if c >= 3:
                            pe.wait_ge(sem("acc"), i * per + (c - 2 + l * PER["acc"]))
                        elif c == 1 and wait_hid is not None:
                            pe.wait_ge(sem("hid"), wait_hid)
                        ob = bank(COMB_BANKS[c % 3])
                        if t < NLT:
                            last = T.matmul(ob, PT_L[half][:, t * P:(t + 1) * P], YL[half], start=True, stop=True)
                        else:
                            last = T.matmul(ob, PT_C[half][:, (t - NLT) * P:(t - NLT + 1) * P], YC[half], start=True, stop=True)
                        last.then_inc(sem("comb"), 1)

                def turn_hidden(i, e):
                    pe.wait_ge(sem("hid"), i * 2 + (e + 1 + l * NE))
                    for j in range(4):
                        last = T.transpose(bank(5, P, j * P), HIDL[:, j * P:(j + 1) * P], ident)
                    last.then_inc(sem("hidT"), 1)

                def turn_hidden_ctx(i, e):
                    pe.wait_ge(sem("hid_c"), i * 2 + (e + 1))
                    for j in range(4):
                        last = T.transpose(bank(6, P, j * P), HIDC[:, j * P:(j + 1) * P], ident)
                    last.then_inc(sem("hidT_c"), 1)

                def turn_all(i, e):
                    turn_hidden(i, e)
                    if ctx_too:
                        turn_hidden_ctx(i, e)

                def expert(i, e, first, last_pair):
                    if e == 0:
                        pe.wait_ge(sem("xs"), i + (1 + l * PAIRS))
                        if ctx_too:
                            pe.wait_ge(sem("xs_ctx"), i + 1)
                    elif not first:
                        pe.wait_ge(sem("acc"), i * per + l * PER["acc"])
                    for j in range(4):
                        pe.wait_ge(ffn_full[j], i * 32 + 16 * (e + 1 + l * NE))
                        for kk in range(2):
                            kc = 2 * j + kk
                            for m in range(2):
                                for h in range(2):
                                    last = T.matmul(bank(m)[64 * h:64 * h + 64, :], XST[:, kc, e, 0:CAP_L],
                                                    gate_up[j][:, kk, m * D + h * 512:m * D + (h + 1) * 512], start=kc == 0, stop=kc == KC - 1)
                            if ctx_too:
                                for g in range(4):
                                    last = T.matmul(bank(2)[32 * g:32 * g + 32, :], XST[:, kc, e, CAP_L:CW],
                                                    gate_up[j][:, kk, g * 512:(g + 1) * 512], start=kc == 0, stop=kc == KC - 1)
                        last.then_inc(ffn_used[j], 1)
                    if e == 0 and not first:
                        pe.wait_ge(sem("yev"), i * 2 + l * NE)
                        pe.wait_ge(sem("ptok"), i + l * PAIRS)
                        combine(i - 1, range(per // 2), i * 2 + (e + 1 + l * NE))
                        turn_all(i, e)
                        combine(i - 1, range(per // 2, per))
                    elif e and not last_pair:
                        pe.wait_ge(sem("sel"), i + (2 + l * PAIRS))
                        gather(i + 1, 0)
                        turn_all(i, e)
                        gather(i + 1, 1)
                        if ctx_too:
                            gather_ctx(i + 1)
                    else:
                        turn_all(i, e)
                    pe.wait_ge(sem("ht"), i * 2 + (e + 1 + l * NE))
                    if ctx_too:
                        pe.wait_ge(sem("ht_c"), i * 2 + (e + 1))
                    if e or l or not first:
                        pe.wait_ge(sem("yev"), i * 2 + (e + l * NE))
                    for kc in range(KC):
                        if kc % 4 == 0:
                            pe.wait_ge(ffn_full[4 + kc // 4], i * 32 + 16 * (e + 1 + l * NE))
                        for g in range(2):
                            h = g ^ e
                            last = T.matmul(bank(3)[64 * g:64 * g + 64, :], HT[:, kc, 0:CAP_L],
                                            down[kc // 4][:, kc % 4, h * 512:(h + 1) * 512], start=kc == 0, stop=kc == KC - 1)
                        if ctx_too and kc % 2:
                            for g in range(4):
                                h, k = (g // 2) ^ e, kc - 1 + g % 2
                                last = T.matmul(bank(4)[32 * g:32 * g + 32, :], HT[:, k, CAP_L:CW],
                                                down[k // 4][:, k % 4, h * 512:(h + 1) * 512], start=kc == 1, stop=kc == KC - 1)
                        if kc % 4 == 3:
                            last.then_inc(ffn_used[4 + kc // 4], 1)

                pe.wait_ge(sem("sel"), 1 + l * PAIRS)
                gather(0, 0)
                gather(0, 1)
                if ctx_too:
                    gather_ctx(0)
                for e in range(2):
                    expert(0, e, True, False)
                with pe.Fori(1, PAIRS - 1) as i:
                    for e in range(2):
                        expert(i, e, False, False)
                for e in range(2):
                    expert(PAIRS - 1, e, False, True)
                pe.wait_ge(sem("yev"), NE + l * NE)
                pe.wait_ge(sem("ptok"), (l + 1) * PAIRS)
                combine(PAIRS - 1, range(per))

            pe.wait_ge(sem("silu_c"), 1)
            pe.wait_ge(sem("const_in"), 16)
            for k in range(MOD_UNITS + 1):
                if k < MOD_UNITS:
                    if k >= 2:
                        pe.wait_ge(sem("modrow_out"), k - 1)
                    mod_rows(0, k, bank(k % 2))
                if k:
                    mod_cols(0, k - 1, w(512 + 512 * ((k - 1) % 2), 512))
            pe.wait_ge(sem("param_in"), 16)
            pe.wait_ge(sem("ones_set"), 1)
            for l in range(DEPTH):
                turn_x(l, "a")
                project(l, 0)
                project(l, 1)
                gla_z(l)
                project(l, 2)
                project(l, 3)
                gla_keys(l)
                project(l, 4)
                rot(l)
                gla_out(l)
                attend(l)
                gate_rows(l, "a")
                w_out(l)
                turn_x(l, "f")
                route(l)
                ffn(l)
                gate_rows(l, "f")


def _constants(np):
    c = np.zeros((P, CONSTS), np.float32)
    i = np.arange(P)
    c[:, C_ID:C_ID + P] = np.eye(P)
    c[:, C_MF:C_MF + P] = i[:, None] <= i[None, :]
    c[:, C_MB:C_MB + P] = i[:, None] >= i[None, :]
    band = np.arange(3 * P)[None, :] - P - i[:, None]
    c[:, C_BAND:C_BAND + 3 * P] = np.where(np.abs(band) <= WINDOW, 0.0, NEG)
    d, t = np.arange(P) % HD, np.arange(LAT)
    quarter = HD // 4
    freq = np.float32(10000.0) ** (-np.arange(quarter, dtype=np.float32) / np.float32(quarter))
    pos = np.where((d < HD // 2)[:, None], (t // GRID_W)[None, :], (t % GRID_W)[None, :]).astype(np.float32)
    ang = pos * freq[d % quarter][:, None].astype(np.float32)
    c[:, C_COS:C_COS + LAT] = np.cos(ang)
    c[:, C_SIN:C_SIN + LAT] = np.sin(ang)
    for m in range(P):
        if m % (2 * quarter) < quarter:
            c[m + quarter, C_ROT + m] = -1.0
        else:
            c[m - quarter, C_ROT + m] = 1.0
    c[:, C_HM:C_HM + GLA_H] = (i[:, None] // DK) == np.arange(GLA_H)[None, :]
    c[:, C_IOTA:C_IOTA + NLT] = i[:, None] + P * np.arange(NLT)[None, :]
    c[:, C_SUM:C_SUM + 2] = (i[:, None] % 32) == np.arange(2)[None, :]
    return c


def _layout(np, a):
    f = np.float32
    x_all = np.concatenate([a["x"][0], a["ctx"][0]], 0)
    cvec = np.stack([a["c"][0].reshape(KC, P).T, a["c_ctx"].reshape(KC, P).T], 2).reshape(P, 2 * KC)
    widths = (GLA_H * DK, GLA_H * DV, 16, 16, NAT_H * HD, NAT_H * HD, 2 * HD, 2 * HD, GLA_H * DK, GLA_H * DV, NAT_H * HD, SWA_H * HD)
    at = np.concatenate([[0], np.cumsum(widths)])
    sq_order = np.concatenate([np.arange(HD) + HD * (p // 2 + 4 * (p % 2)) for p in range(SWA_H)])

    def rows(w):
        return w.reshape(KC, P, -1).transpose(1, 0, 2)

    def blocks(w):
        return w.reshape(KC, P, 4, P).transpose(1, 2, 0, 3).reshape(P, UNIT)

    stream = np.zeros((N_UNITS, P, UNIT), f)
    params = np.zeros((DEPTH, P, PARAMS), f)
    for l in range(DEPTH):
        for k in range(MOD_UNITS):
            stream[MOD_AT[l] + k] = rows(a["w_mod"][l][:, 512 * k:512 * (k + 1)]).reshape(P, UNIT)
        gk, gv, gaf, gab, nk, nv, sk, sv, gq, gg, nq, sq = (a["w_in"][l][:, at[i]:at[i + 1]] for i in range(12))
        z16 = np.zeros((D, 16), f)
        al = np.concatenate([gaf, z16, gab, z16, z16, z16, z16, z16], 1)
        u = IN_AT[l]
        stream[u] = blocks(np.concatenate([gk, al, gq, sk], 1))
        stream[u + 1] = rows(np.concatenate([gv, nv], 1)).reshape(P, UNIT)
        stream[u + 2, :, 0:KC * 384] = rows(np.concatenate([sv, gg], 1)).reshape(P, -1)
        stream[u + 2, :, KC * 384:KC * 400] = rows(a["w_router"][l]).reshape(P, -1)
        stream[u + 3] = blocks(np.concatenate([nk, nq], 1))
        stream[u + 4] = blocks(sq[:, sq_order])
        for j in range(2):
            wo = np.concatenate([a["w_out"][l][0:512], a["w_out"][l][512:][sq_order]], 0)
            stream[OUT_AT[l] + j] = rows(wo[:, 512 * j:512 * (j + 1)]).reshape(P, UNIT)
        for e in range(NE):
            u = FFN_AT[l] + 6 * e
            gu = np.concatenate([rows(a["w_gate"][l, e]), rows(a["w_up"][l, e])], 2)
            stream[u:u + 4] = gu.reshape(P, 4, UNIT).transpose(1, 0, 2)
            stream[u + 4:u + 6] = rows(a["w_down"][l, e]).reshape(P, 2, UNIT).transpose(1, 0, 2)
        params[l, :, P_BMOD:P_BMOD + 96] = np.repeat(a["b_mod"][l].reshape(48, P).T[:, :, None], 2, 2).reshape(P, 96)
        params[l, :, P_GAIN:P_GAIN + 32] = a["norm_gains"][l].reshape(4, KC, P).transpose(2, 0, 1).reshape(P, 32)
        params[l, 0:16, P_AUP:P_AUP + P] = a["gla_a_up"][l, 0]
        params[l, 32:48, P_AUP:P_AUP + P] = a["gla_a_up"][l, 1]
        params[l, :, P_AB:P_AB + 2] = a["gla_a_bias"][l].T
        params[l, :, P_GG:P_GG + DV] = a["gla_norm"][l][None, :]
        params[l, :, P_SINK:P_SINK + SWA_H] = a["swa_sink"][l][None, :]
    t = np.arange(LAT)
    c, r = t // NAT_ROWS, t % NAT_ROWS
    start = np.clip(c - NAT_COLS // 2, 0, GRID_W - NAT_COLS)
    seen = (c[None, :] >= start[:, None]) & (c[None, :] < start[:, None] + NAT_COLS)
    ri = r[None, :] - r[:, None] + NAT_ROWS - 1
    ci = np.clip(c[None, :] - c[:, None] + NAT_COLS - 1, 0, 2 * NAT_COLS - 2)
    full = np.where(seen, a["nat_rpb"][:, :, ri, ci], f(NEG)).astype(f)
    bias = np.full((DEPTH, NLT, NAT_H, P, 3 * P), NEG, f)
    for j in range(NLT):
        k0, k1 = max(j - 1, 0) * P, min(j + 2, NLT) * P
        assert not seen[j * P:(j + 1) * P, :k0].any() and not seen[j * P:(j + 1) * P, k1:].any()
        bias[:, j, :, :, 0:k1 - k0] = full[:, :, j * P:(j + 1) * P, k0:k1]
    iotarow = np.broadcast_to(np.arange(LAT, dtype=f), (P, LAT))
    return {"x_all": x_all, "cvec": cvec, "consts": _constants(np), "iotarow": iotarow, "params": params,
            "nat_bias": bias, "wstream": stream}


def kernel(**inputs):
    import numpy as np
    import concourse.bacc as bacc
    from concourse import mybir as mb
    from concourse.bass_utils import run_bass_kernel_spmd as run

    nc = bacc.Bacc("TRN2", target_bir_lowering=False, num_devices=1)
    arrays, args = {}, []
    laid = _layout(np, {k: np.asarray(v) for k, v in inputs.items()})
    for name in ("x_all", "cvec", "consts", "iotarow", "params", "nat_bias", "wstream"):
        v = np.ascontiguousarray(laid[name])
        arrays[f"in_{name}"] = v
        args.append(nc.dram_tensor(f"in_{name}", v.shape, mb.dt.from_np(v.dtype), kind="ExternalInput").ap())
    args.append(nc.dram_tensor("x_kept", (TOK, D), mb.dt.float32).ap())
    args.append(nc.dram_tensor("picked", (DEPTH, 2, 2, NE * CAP_L), mb.dt.float32).ap())
    args.append(nc.dram_tensor("out_x", (LAT, D), mb.dt.float32, kind="ExternalOutput").ap())
    bass_hybrid_dit(nc, *args)
    r = run(nc, [arrays], core_ids=[0])
    return r.results[0]["out_x"].reshape(1, LAT, D)
```

```python
import concourse.bass as bass
from concourse import mybir
from contextlib import ExitStack

P = 128
D = 1024
KC = D // P
LAT, CTX = 512, 256
TOK = LAT + CTX
NLT, NCT = LAT // P, CTX // P
NT = NLT + NCT
DEPTH = 2
GRID_W = 64
NAT_H, SWA_H, GLA_H = 4, 8, 4
NAT_ROWS, NAT_COLS = 8, 16
WINDOW = 128
HD = 64
DK, DV = 32, 64
TAU = 16.0
NE = 16
PAIRS = NE // 2
CAP_L, CAP_C = 2 * LAT // NE, 2 * CTX // NE
EPS = 1e-6
NEG = -1e30
SCALE = HD ** -0.5
UNIT = 4096
RING = 4
MOD_UNITS, IN_UNITS, OUT_UNITS, FFN_UNITS = 12, 5, 2, 6 * NE
CW = CAP_L + CAP_C

SLOTS = 6
MOD_EARLY = 4
IN_AT = [MOD_EARLY, 2 * MOD_UNITS + IN_UNITS + OUT_UNITS + FFN_UNITS]
OUT_AT = [2 * MOD_UNITS + IN_UNITS, IN_AT[1] + IN_UNITS]
FFN_AT = [OUT_AT[0] + OUT_UNITS, OUT_AT[1] + OUT_UNITS]
N_UNITS = FFN_AT[1] + FFN_UNITS


def mod_at(n):
    return n + (IN_UNITS if n >= MOD_EARLY else 0)


MOD_SLOT = {1 + j * 7 // 4: MOD_EARLY + j for j in range(2 * MOD_UNITS - MOD_EARLY)}


def lap(n):
    n -= FFN_UNITS if n >= FFN_AT[0] else 0
    return n % RING, n // RING



GK, GQ, NQ, NK, SK, SQ, AL = 0, 1, 2, 4, 6, 7, 11
NFM = 12
TM_GV, TM_NV, TM_SV, TM_GG = 0, 256, 512, 640
TMW = TM_GG + 256

C_ID, C_MF, C_MB, C_COS, C_SIN, C_ROT, C_HM, C_IOTA, C_SUM = 0, 128, 256, 384, 896, 1408, 1536, 1540, 1544
CONSTS = C_SUM + NE
P_BMOD, P_GAIN, P_AUP, P_AB, P_GG, P_SINK = 0, 96, 128, 256, 258, 322
PARAMS = P_SINK + SWA_H


UPT = NAT_H + SWA_H

PER = {"z": 2, "z_out": 2, "softplus": 2, "scan": 12, "totc": 2, "ke_arg": 2, "ke_exp": 2, "ke": 2,
       "tot_exp": 1, "keT": 3, "keT_out": 1, "dSm": 10, "dS": 5, "state": 10, "rope": 5, "rot": 5,
       "q_arg": 6, "q_exp": 6, "qk": 6, "gla_ms": 1, "gla_rms": 1, "gate_silu": 1, "gate_gain": 1,
       "gla_o": 1, "router_in": 1, "router_parts": 1, "router_sb": 1,
       "logits": 1, "logit_sub": 1, "logit_exp": 1, "aff": 1, "affT": 1, "picked": 1, "iota": 16,
       "proj": 2 * NT + 28, "proj_out": 2 * NT + 28, "qblk": 2 * NT, "scores": NT, "A": NT, "o": NT, "o_out": NT,
       "s": UPT * NT, "max": UPT * NT, "exp": UPT * NT, "diagr": UPT * NT, "T": UPT * NT, "pt_out": UPT * NT,
       "pv": UPT * NT // 2, "mix": UPT * NT // 2, "bias": 16 * NAT_H * NLT // 4, "wo": NT, "x_mid": NT,
       "acc_zero": NT, "gather": 3 * PAIRS, "comb": PAIRS * 2 * NT, "acc": PAIRS * 2 * NT}


PASSES = {"xT": (2 * KC, 2 * KC, 2 * KC, KC),
          "h_t": (KC, KC, KC, KC),
          "h_ctx": (KC, KC, KC, 0),
          "diag": (2, 2, 1, 1),
          "grow": (2, 2, 1, 1),
          "grow_out": (1, 1, 1, 1),
          "psq": (NT, NT, NLT, NLT),
          "rms": (NT, NT, NT, NLT),
          "y_used": (NT, NT, NLT, NLT),
          "sq": (NT, NT, NT, NLT),
          "xn": (NT, NT, NT, NLT)}


def before(name, l, half):
    return sum(PASSES[name][:2 * l + (half == "f")])


def bass_hybrid_dit(nc, x_all, cvec, consts, band_d, iotarow_d, params_d, nat_bias, wstream, xkeep, pick_d, out):
    f32 = mybir.dt.float32
    u32 = mybir.dt.uint32
    ALU = mybir.AluOpType
    ACT = mybir.ActivationFunctionType
    AX = mybir.AxisListType.X
    V, S, T = nc.vector, nc.scalar, nc.tensor

    ctx = ExitStack()
    with ctx:
        def sb(name, n, dt=f32):
            return ctx.enter_context(nc.sbuf_tensor(name, [P, n], dt))

        ring = sb("ring", RING * UNIT)
        hT = sb("hT", KC * TOK)
        big = sb("big", NFM * TOK + NT * TMW)
        cst = sb("cst", CONSTS)
        prm = sb("prm", DEPTH * PARAMS)
        ones = sb("ones", P)
        modc = sb("modc", DEPTH * 96)
        cols = sb("cols", 2 * 2 * 2 * KC)
        gcol = sb("gcol", 2 * KC)
        router = sb("router", KC * 32)[:, :].rearrange("p (a b) -> p a b", a=KC)
        small = sb("small", 2 * 8 + 2 * 8 + 8 + 24 + 24)
        glao = sb("glao", NT * 256)
        work = sb("work", 10752)
        ps = ctx.enter_context(nc.psum_tensor("ps", [P, 8 * 512], f32))

        def bank(b, n=512, at=0):
            return ps[:, b * 512 + at:b * 512 + at + n]

        def v3(ap, a):
            return ap.rearrange("p (a b) -> p a b", a=a)

        ident = cst[:, C_ID:C_ID + P]
        X = v3(big[:, 0:NT * D], NT)
        GROW = v3(big[:, NT * D:NT * D + 2 * D], 2)
        XN = v3(big[:, 8 * D:8 * D + NT * D], NT)
        FM = v3(big[:, 0:NFM * TOK], NFM)
        TM = v3(big[:, NFM * TOK:], NT)
        hTv = v3(hT[:, :], KC)
        ACC = v3(hT[:, :], NT)
        ringv = v3(ring[:, :], RING)
        slot = [ringv[:, j, :] for j in range(RING)] + [big[:, j * UNIT:(j + 1) * UNIT] for j in range(2)]
        colv = cols[:, :].rearrange("p (s w m k) -> p s w m k", s=2, w=2, m=2)
        modv = modc[:, :].rearrange("p (l n w) -> p l n w", l=DEPTH, w=2)
        ss = small[:, 0:12]
        rs = small[:, 16:16 + 12]
        gss = small[:, 40:64]
        grs = small[:, 64:88]

        def w(at, n):
            return work[:, at:at + n]

        CUM = [w(0, TOK), w(TOK, TOK)]
        E = [w((2 + i) * TOK, TOK) for i in range(6)]
        STATE = [v3(w(8 * TOK + d * NT * 256, NT * 256), NT) for d in range(2)]
        GX = 8 * TOK + 2 * NT * 256
        KET = v3(w(GX, 12 * P), 12)
        A_SB = w(GX, 512)
        A_TMP = w(GX + 512, 512)
        QBLK = [w(q, 512) for q in (0, 512, 1024, GX + 1024)]
        KW = 5 * P
        SC = [w(384 * i, 384) for i in range(2)]
        PR = [w(768 + KW * i, KW) for i in range(2)]
        PT = [w(2048 + KW * i, KW) for i in range(4)]
        BIAS = [w(4608 + 384 * i, 384) for i in range(4)]
        RDIAG = [w(6144 + P * i, P) for i in range(2)]
        AST = w(6400, 96)
        MODROW = w(6656, 512)
        BAND = w(4096, 3 * P)
        CS = w(0, 16)
        CTMP = w(16, 16)
        CS32 = v3(sb("silu_c", KC * 32)[:, :], KC)
        nsink = sb("nsink", DEPTH * SWA_H)[:, :]
        masks = sb("masks", 4 * P, mybir.dt.bfloat16)
        band_lo, ident_lo = masks[:, 0:3 * P], masks[:, 3 * P:4 * P]
        AFM = sb("route_stats", 16)[:, :]
        at = [0]

        def take(n):
            at[0] += n
            assert at[0] <= 10752
            return w(at[0] - n, n)

        SEL_L, SEL_C = v3(take(512), 4), v3(take(128), 2)
        PT_L, PT_C = [take(512) for _ in range(2)], [take(256) for _ in range(2)]
        tokens_at = at[0]
        XST = take(KC * 2 * CW).rearrange("p (k e c) -> p k e c", k=KC, e=2)
        HT = v3(take(KC * CW), KC)
        HIDL, HIDC = take(512), take(512)
        SGL, SGC = glao[:, 0:512], glao[:, 512:1024]
        YL, YC = [take(512) for _ in range(2)], [take(512) for _ in range(2)]
        picked_at = at[0]
        IDXL, IDXC = take(NE * CAP_L), take(NE * CAP_C)
        SQUARES, GAIN_X = w(tokens_at, D), w(tokens_at + D, D)
        DIAG = [w(picked_at, D), w(picked_at + D, D)]
        RPART = IDXL[:, 0:TOK]
        COLS_L, COLS_C = v3(take(4 * PAIRS), 4), v3(take(4 * PAIRS), 4)
        IOTAR = take(LAT)
        AFF = v3(take(NLT * 48), NLT)
        LOG = v3(take(NT * NE), NT)
        VALS, IDXF = take(CAP_L), take(CAP_L)
        AFT0, AFT1 = HIDL, HIDC
        idxu = sb("idxu", CAP_L, u32)

        sems = {}

        def sem(name):
            if name not in sems:
                sems[name] = ctx.enter_context(nc.semaphore(name))
            return sems[name]

        ring_full = [sem(f"ring_full{i}") for i in range(RING)]
        ring_used = [sem(f"ring_used{i}") for i in range(RING)]
        ffn_full = [sem(f"ffn_full{i}") for i in range(SLOTS)]
        ffn_used = [sem(f"ffn_used{i}") for i in range(SLOTS)]

        class Chain:

            def __init__(self, eng, name):
                self.eng, self.sem, self.n = eng, sem(name), 0

            def __call__(self, ins):
                self.n += 1
                ins.then_inc(self.sem, 1)
                self.eng.wait_ge(self.sem, self.n)

        def width(l):
            return TOK if l < DEPTH - 1 else LAT

        def tiles(l):
            return [4, 5, 0, 1, 2, 3] if l < DEPTH - 1 else [0, 1, 2, 3]

        def token_parts(l, kv):
            return [(0, LAT)] + ([(LAT, CTX)] if kv or l < DEPTH - 1 else [])

        def fm_items(l, unit):
            blocks = {0: [GK, AL, GQ, SK], 3: [SQ, SQ + 1, SQ + 2, SQ + 3], 4: [NK, NK + 1, NQ, NQ + 1]}[unit]
            return [(j, b, t0, n) for j, b in enumerate(blocks)
                    for t0, n in token_parts(l, b in (GK, AL, SK, NK, NK + 1))]

        def n_items(l, upto):
            return sum({1: NT + 4, 2: NT}[u] if u in (1, 2) else len(fm_items(l, u)) for u in range(upto))

        def units(l):
            out_ = []
            for ti, t in enumerate(tiles(l)):
                for kind, h in [("n", h) for h in range(NAT_H)] + [("s", h) for h in range(SWA_H)]:
                    out_.append((ti, t, kind, h))
            return out_

        def by_column(ap, packed):
            if packed:
                return ap.rearrange("p (c r) -> p c r", r=LAT // GRID_W)
            return ap.rearrange("p (r c) -> p c r", c=GRID_W)

        def local_keys(t):
            if t >= NLT:
                return 0, 0
            a, b = max(t - 1, 0), min(t + 2, NLT)
            return a * P, (b - a) * P

        def score_place(u, nl):
            at_ = (2 * (u % 2) + 1) * 512
            return ps[:, at_ - nl:at_], ps[:, at_:at_ + CTX], ps[:, at_ - nl:at_ + CTX]

        KEY_COPY = [(NK, GK), (NK + 1, GQ), (SK, AL)]

        F_ORD, B_ORD = [4, 5, 0, 1, 2, 3], [5, 4, 3, 2, 1, 0]

        def acc_total(l):
            return (l * NT + len(tiles(l))) * 2 * PAIRS

        COMB_BANKS, LAST_BANKS = (7, 0, 1), (0, 1, 2)

        block = ctx.enter_context(nc.Block())

        @block.sync
        def _(sp):
            def load(n):
                p = lap(n)[0]
                sp.dma_start(ringv[:, p, :], wstream[n, :, :]).then_inc(ring_full[p], 16)

            def ring_load(a, b):
                p0, g0 = lap(a)
                laps = (b - a) // RING
                if laps:
                    with sp.Fori(0, laps) as g:
                        for j in range(RING):
                            p = (p0 + j) % RING
                            sp.wait_ge(ring_used[p], g + lap(a + j)[1])
                            sp.dma_start(ringv[:, p, :], wstream[g * RING + (a + j), :, :]).then_inc(ring_full[p], 16)
                for n in range(a + laps * RING, b):
                    sp.wait_ge(ring_used[lap(n)[0]], lap(n)[1])
                    load(n)

            sp.dma_start(X, x_all.rearrange("(t p) d -> p t d", p=P)).then_inc(sem("x_in"), 16)
            sp.dma_start(cst[:, :], consts).then_inc(sem("const_in"), 16)
            for n in range(RING):
                load(n)
            ring_load(RING, FFN_AT[0])
            for l in range(DEPTH):
                last = FFN_AT[l] - 1
                for j in range(SLOTS):
                    if j < RING:
                        n = max(n for n in range(last - RING + 1, last + 1) if lap(n)[0] == j)
                        sp.wait_ge(ring_used[j], lap(n)[1] + 1)
                    elif j == RING:
                        sp.wait_ge(sem("x_saved"), 16 * [NT, NT + NLT][l])
                    sp.dma_start(slot[j], wstream[FFN_AT[l] + j, :, :]).then_inc(ffn_full[j], 16)
                with sp.Fori(1, NE) as e:
                    for j in range(SLOTS):
                        sp.wait_ge(ffn_used[j], e + l * NE)
                        sp.dma_start(slot[j], wstream[e * SLOTS + (FFN_AT[l] + j), :, :]).then_inc(ffn_full[j], 16)
                if l == 0:
                    for n in range(IN_AT[1], FFN_AT[1]):
                        if n < IN_AT[1] + RING:
                            sp.wait_ge(ffn_used[lap(n)[0]], NE)
                        sp.wait_ge(ring_used[lap(n)[0]], lap(n)[1])
                        load(n)

        @block.gpsimd
        def _(pool):
            pool.memset(CS32, 0.0).then_inc(sem("c_zero"), 1)
            pool.dma_start(BAND, band_d).then_inc(sem("band_in"), 16)
            pool.wait_ge(sem("const_in"), 16)
            pool.wait_ge(sem("band_in"), 16)
            pool.tensor_copy(band_lo, BAND)
            pool.tensor_copy(ident_lo, ident).then_inc(sem("band_lo"), 1)
            pool.dma_start(v3(prm[:, :], DEPTH), params_d.rearrange("l p c -> p l c")).then_inc(sem("param_in"), 16)
            pool.memset(router, 0.0).then_inc(sem("router_zero"), 1)
            pool.memset(ones[:, :], 1.0).then_inc(sem("ones_set"), 1)
            for l in range(DEPTH):
                us = units(l)
                if l:
                    for t in range(NLT):
                        pool.wait_ge(sem("x_ready"), t + 1)
                        pool.dma_start(xkeep[t * P:(t + 1) * P, :], X[:, t, :]).then_inc(sem("x_kept"), 16)
                    pool.wait_ge(sem("x_kept"), 16 * NLT)
                pool.wait_ge(sem("gate_silu"), 1 + l * PER["gate_silu"])
                pool.wait_ge(sem("param_in"), 16)
                g0, n = l * PARAMS + P_GG, width(l) // P
                gates = TM[:, 0:n, TM_GG:TMW].rearrange("p t (h v) -> p t h v", h=GLA_H)
                pool.tensor_tensor(gates, gates, prm[:, g0:g0 + DV].unsqueeze(1).unsqueeze(1).broadcast_to([P, n, GLA_H, DV]), ALU.mult)\
                    .then_inc(sem("gate_gain"), 1)
                pool.wait_ge(sem("gate_gain"), 1 + l * PER["gate_gain"])
                pool.wait_ge(sem("qk"), (l + 1) * PER["qk"])
                pool.wait_ge(sem("rope"), (l + 1) * PER["rope"])
                pool.wait_ge(sem("proj_out"), n_items(l, 5) + l * PER["proj_out"])
                for i, (b, other) in enumerate(KEY_COPY):
                    pool.tensor_copy(FM[64:P, other, :], FM[64:P, b, :]).then_inc(sem("key_copy"), 1)
                    pool.memset(FM[0:64, other, :], 0.0).then_inc(sem("keys"), 1)
                    pool.wait_ge(sem("key_copy"), 3 * l + i + 1)
                    pool.memset(FM[64:P, b, :], 0.0).then_inc(sem("keys"), 1)
                n = 0
                pool.wait_ge(sem("gla_o"), 1 + l * PER["gla_o"])
                stts = [u for u, x in enumerate(us) if x[2] == "n" and x[1] < NLT]
                for n, u in enumerate(stts):
                    if n >= 4:
                        pool.wait_ge(sem("max"), stts[n - 4] + 1 + l * PER["max"])
                    nl = local_keys(us[u][1])[1]
                    pool.dma_start(BIAS[n % 4][:, 0:nl], nat_bias[l, us[u][1], us[u][3], :, 0:nl]).then_inc(sem(f"bias{n % 4}"), 16)
                pool.wait_ge(sem("pv"), len(us) // 2 + l * PER["pv"])
                for t in tiles(l):
                    src = x_all if l == 0 else xkeep
                    pool.dma_start(X[:, t, :], src[t * P:(t + 1) * P, :]).then_inc(sem(f"x_back{t}"), 16)
                for i, t in enumerate(tiles(l)):
                    pool.wait_ge(sem("x_mid"), i + 1 + l * PER["x_mid"])
                    pool.wait_ge(sem("xn"), i + 1 + before("xn", l, "f"))
                    pool.dma_start(xkeep[t * P:(t + 1) * P, :], X[:, t, :]).then_inc(sem("x_saved"), 16)
                pool.wait_ge(sem("logits"), 1 + l * PER["logits"])
                for t in tiles(l):
                    pool.memset(ACC[:, t, :], 0.0).then_inc(sem("acc_zero"), 1)
                pool.dma_start(IOTAR, iotarow_d).then_inc(sem("iota"), 16)
                ctx_too = l < DEPTH - 1
                pool.wait_ge(sem("picked"), 1 + l * PER["picked"])
                pool.dma_start(pick_d[l, 1, 0, :].rearrange("(e r) -> e r", r=CAP_L), VALS[0:NE, :]).then_inc(sem("val_out"), 16)
                if ctx_too:
                    pool.dma_start(pick_d[l, 1, 1, 0:NE * CAP_C].rearrange("(e r) -> e r", r=CAP_C),
                                   VALS[32:32 + NE, 0:CAP_C]).then_inc(sem("val_out"), 16)
                pool.wait_ge(sem("idx_out"), l * 32 + (32 if ctx_too else 16))
                pool.wait_ge(sem("val_out"), l * 32 + (32 if ctx_too else 16))
                with nc.allow_non_contiguous_dma(reason="slot columns"):
                    for i in range(2):
                        for e in range(2):
                            src = pick_d[l, i, 0, :].rearrange("(a e p) -> e p a", e=2, p=CAP_L)[e]
                            for sw in range(2):
                                p = 64 * (e ^ sw)
                                pool.dma_start(COLS_L[p:p + 64, 2 * i + sw, :], src).then_inc(sem("cols_in"), 16)
                            if ctx_too:
                                src = pick_d[l, i, 1, 0:NE * CAP_C].rearrange("(a e p) -> e p a", e=2, p=CAP_C)[e]
                                for sw in range(2):
                                    for part in range(2):
                                        p = 64 * (e ^ sw) + 32 * part
                                        pool.dma_start(COLS_C[p:p + 32, 2 * i + sw, :], src).then_inc(sem("cols_in"), 16)
                for j in range(RING, SLOTS):
                    pool.wait_ge(ffn_used[j], (l + 1) * NE)
                for t in tiles(l):
                    pool.dma_start(X[:, t, :], xkeep[t * P:(t + 1) * P, :]).then_inc(sem(f"x_again{t}"), 16)
            for t in range(NLT):
                pool.wait_ge(sem("x_ready"), t + 1 + (DEPTH - 1) * NLT)
                pool.dma_start(out[t * P:(t + 1) * P, :], X[:, t, :]).then_inc(sem("stored"), 16)
            pool.wait_ge(sem("stored"), 16 * NLT)

        def picks(l):
            return 16 * (24 if l < DEPTH - 1 else 8)

        @block.scalar
        def _(act):
            chain = Chain(act, "act_chain")
            act.dma_start(CS, cvec).then_inc(sem("c_in"), 16)
            act.wait_ge(sem("c_in"), 16)
            S.activation(CTMP[:, 0:16], CS, ACT.Exp, scale=-1.0).then_inc(sem("c_exp"), 1)

            def square(x, junk, out_, done):
                chain(S.activation(junk, x, ACT.Square, scale=D ** -0.5, accum_out=out_))
                S.activation(out_, out_, ACT.Sqrt, bias=EPS).then_inc(sem(done), 1)

            def norm_square(l, half, i, t):
                if l and half == "a":
                    if t < NLT:
                        act.wait_ge(sem("x_ready"), t + 1 + (l - 1) * NLT)
                    else:
                        act.wait_ge(sem("xc_ready"), t - NLT + 1)
                elif half == "f":
                    act.wait_ge(sem("x_mid"), i + 1 + l * PER["x_mid"])
                square(X[:, t, :], XN[:, t, :], ss[:, NT + t:NT + t + 1], "sq")

            def norm_scale(l, half, i, t):
                act.wait_ge(sem("rms"), i + 1 + before("rms", l, half))
                S.activation(XN[:, t, :], X[:, t, :], ACT.Copy, scale=rs[:, NT + t:NT + t + 1]).then_inc(sem("xn"), 1)

            def h_ctx(l, half):
                s = 0 if half == "a" else 1
                act.wait_ge(sem("cols"), 2 * (2 * l + s) + 2)
                for k in range(KC):
                    act.wait_ge(sem("xT"), 2 * k + 2 + before("xT", l, half))
                    S.activation(hTv[:, k, LAT:TOK], bank(2 * (k % 2) + 1, CTX), ACT.Identity, scale=colv[:, s, 1, 0, k:k + 1],
                                 bias=colv[:, s, 1, 1, k:k + 1]).then_inc(sem("h_ctx"), 1)

            def project_out(l, unit, parts):
                n = n_items(l, unit)
                for dst, b, k, shape in parts:
                    act.wait_ge(sem("proj"), n + 1 + l * PER["proj"])
                    S.activation(dst, shape(bank(n % 4, k)), ACT.Copy).then_inc(sem("proj_out"), 1)
                    n += 1
                    if unit == 4:
                        gla_queries(l, 6 - (n_items(l, 5) - n) - 1)

            def fm_parts(l, unit):
                parts = []
                for j, b, t0, n in fm_items(l, unit):
                    m = 48 if b == AL else P
                    if NQ <= b < SK and t0 == 0:
                        parts.append((by_column(FM[:, b, 0:LAT], True), b, n, lambda ap: by_column(ap, False)))
                    else:
                        parts.append((FM[0:m, b, t0:t0 + n], b, n, lambda ap, m=m: ap[0:m, :]))
                return parts

            def gla_exps(l):
                for d in range(2):
                    act.wait_ge(sem("z_out"), d + 1 + l * PER["z_out"])
                    chain(S.activation(E[2 + d], E[d], ACT.Abs))
                    chain(S.activation(E[2 + d], E[2 + d], ACT.Exp, scale=-1.0))
                    S.activation(E[2 + d], E[2 + d], ACT.Ln, bias=1.0).then_inc(sem("softplus"), 1)

            def gla_keys(l):
                for d in range(2):
                    act.wait_ge(sem("ke_arg"), d + 1 + l * PER["ke_arg"])
                    S.activation(E[d], E[d], ACT.Exp).then_inc(sem("ke_exp"), 1)
                act.wait_ge(sem("totc"), 2 + l * PER["totc"])
                S.activation(grs[:, 0:12], gss[:, 0:12], ACT.Exp).then_inc(sem("tot_exp"), 1)
                act.wait_ge(sem("keT"), 3 + l * PER["keT"])
                S.activation(w(GX, 12 * P), ps[:, 4 * 512:4 * 512 + 12 * P], ACT.Copy).then_inc(sem("keT_out"), 1)

            def gla_queries(l, j):
                if j >= 0:
                    e = E[j][:, 0:width(l)]
                    act.wait_ge(sem("q_arg"), j + 1 + l * PER["q_arg"])
                    S.activation(e, e, ACT.Exp).then_inc(sem("q_exp"), 1)

            def gla_gate(l):
                act.wait_ge(sem("proj_out"), n_items(l, 3) + l * PER["proj_out"])
                n = width(l) // P
                S.activation(TM[:, 0:n, TM_GG:TMW], TM[:, 0:n, TM_GG:TMW], ACT.Silu).then_inc(sem("gate_silu"), 1)

            def gla_rms(l):
                n = width(l) // P
                act.wait_ge(sem("gla_ms"), 1 + l * PER["gla_ms"])
                S.activation(grs[:, 0:4 * n], gss[:, 0:4 * n], ACT.Sqrt, scale=1.0 / DV, bias=EPS).then_inc(sem("gla_rms"), 1)

            def modrow(n):
                act.wait_ge(sem("modrow"), n + 1)
                S.activation(MODROW, bank(7), ACT.Copy).then_inc(sem("modrow_out"), 1)

            def attend(l):
                us = units(l)
                nt = width(l) // P
                act.wait_ge(sem("glaT"), l + 1)
                S.activation(hTv[:, 0:2, 0:nt * P], v3(ps[:, 4 * 512:4 * 512 + 2 * TOK], 2)[:, :, 0:nt * P], ACT.Copy)\
                    .then_inc(sem("glaT_out"), 1)
                for u in range(len(us) + 2):
                    if u < len(us):
                        ti, t, kind, h = us[u]
                        k0, nl = local_keys(t)
                        act.wait_ge(sem("max"), u + 1 + l * PER["max"])
                        if u >= 2:
                            act.wait_ge(sem("T"), u - 1 + l * PER["T"])
                        st = AST[:, 8 * (u % 4):8 * (u % 4) + 8]
                        local, context, both = score_place(u, nl)
                        if kind == "s":
                            context = both
                        elif nl:
                            S.activation(PR[u % 2][:, 0:nl], SC[u % 2][:, 0:nl], ACT.Exp, bias=st[:, 2:3], accum_out=st[:, 4:5])
                        if kind == "s":
                            orig = h // 2 + 4 * (h % 2)
                            S.activation(st[:, 6:7], prm[:, l * PARAMS + P_SINK + orig:l * PARAMS + P_SINK + orig + 1], ACT.Exp,
                                         bias=st[:, 2:3])
                        first = 0 if kind == "s" else nl
                        S.activation(PR[u % 2][:, first:nl + CTX], context, ACT.Exp, bias=st[:, 2:3],
                                     scale=SCALE, accum_out=st[:, 5:6]).then_inc(sem("exp"), 1)
                    v = u - 1
                    if 0 <= v < len(us):
                        n = local_keys(us[v][1])[1] + CTX
                        act.wait_ge(sem("T"), v + 1 + l * PER["T"])
                        if v >= 4:
                            act.wait_ge(sem("pv"), v // 2 - 1 + l * PER["pv"])
                        S.activation(PT[v % 4][:, 0:n], ps[:, 4 * 512:4 * 512 + n], ACT.Copy).then_inc(sem("pt_out"), 1)
                        if l == 0 and v % 2 == 0 and v // 2 - 1 in MOD_SLOT:
                            modrow(MOD_SLOT[v // 2 - 1])

            def gate_rows(l, half):
                ctx_too = l < DEPTH - 1
                act.wait_ge(sem("grow"), (2 if ctx_too else 1) + before("grow", l, half))
                n = 2 if ctx_too else 1
                S.activation(big[:, NT * D:NT * D + n * D], ps[:, 4 * 512:4 * 512 + n * D], ACT.Copy)\
                    .then_inc(sem("grow_out"), 1)

            def post(l, half):
                ts = tiles(l)
                nxt = (l, "f") if half == "a" else (l + 1, "a")
                for i in range(len(ts) + 2):
                    if i < len(ts):
                        if half == "a":
                            act.wait_ge(sem("wo"), i + 1 + l * PER["wo"])
                            src = ps[:, (i % 2) * D:(i % 2) * D + D]
                        else:
                            act.wait_ge(sem("acc"), acc_total(l) - 2 * (len(ts) - i - 1))
                            src = ACC[:, ts[i], :]
                        square(src, SQUARES, ss[:, ts[i]:ts[i] + 1], "psq")
                    if nxt[0] < DEPTH:
                        if 1 <= i <= len(ts):
                            norm_square(*nxt, i - 1, ts[i - 1])
                        if i >= 2:
                            norm_scale(*nxt, i - 2, ts[i - 2])

            def ffn(l):
                ctx_too = l < DEPTH - 1
                nt = len(tiles(l))
                if ctx_too:
                    h_ctx(l, "f")
                act.wait_ge(sem("router_parts"), 1 + l * PER["router_parts"])
                if ctx_too:
                    S.activation(RPART[:, LAT:TOK], bank(7, CTX), ACT.Copy)
                S.activation(RPART[:, 0:LAT], bank(6), ACT.Copy).then_inc(sem("router_sb"), 1)
                act.wait_ge(sem("logit_sub"), 1 + l * PER["logit_sub"])
                S.activation(LOG[:, 0:nt, :], LOG[:, 0:nt, :], ACT.Exp).then_inc(sem("logit_exp"), 1)
                act.wait_ge(sem("picked"), 1 + l * PER["picked"])
                act.dma_start(pick_d[l, 0, 0, :].rearrange("(e r) -> e r", r=CAP_L), IDXF[0:NE, :]).then_inc(sem("idx_out"), 16)
                if ctx_too:
                    act.dma_start(pick_d[l, 0, 1, 0:NE * CAP_C].rearrange("(e r) -> e r", r=CAP_C), IDXF[32:32 + NE, 0:CAP_C])\
                        .then_inc(sem("idx_out"), 16)
                act.wait_ge(sem("idx_out"), l * 32 + (32 if ctx_too else 16))
                act.dma_start(IDXL, pick_d[l, 0, 0, :].partition_broadcast(P)).then_inc(sem("idx_in"), 16)
                if ctx_too:
                    act.dma_start(IDXC, pick_d[l, 0, 1, 0:NE * CAP_C].partition_broadcast(P)).then_inc(sem("idx_in"), 16)
                def picked(i, g):
                    act.wait_ge(sem("gather"), i * (3 if ctx_too else 2) + (g + 1 + l * PER["gather"]))
                    for k in range(4):
                        last = S.activation(XST[:, 4 * g + k, :, 0:CAP_L], v3(bank((7, 0)[g], P, k * P), 2), ACT.Identity,
                                            scale=colv[:, 1, 0, 0, 4 * g + k:4 * g + k + 1],
                                            bias=colv[:, 1, 0, 1, 4 * g + k:4 * g + k + 1])
                    if g:
                        last.then_inc(sem("xs"), 1)

                def expert(i, e, last_pair):
                    act.wait_ge(ffn_used[3], i * 2 + (e + 1 + l * NE))
                    S.activation(SGL, bank(0), ACT.Silu).then_inc(sem("silu"), 1)
                    if ctx_too:
                        S.activation(SGC[64:P, :], bank(2)[0:64, :], ACT.Silu).then_inc(sem("silu_ctx"), 1)
                    if e and not last_pair:
                        picked(i + 1, 0)
                    act.wait_ge(sem("hidT"), i * 2 + (e + 1 + l * NE))
                    S.activation(HT.rearrange("p (h j) c -> p h j c", h=2)[:, :, :, 0:CAP_L],
                                 bank(5).rearrange("p (j h c) -> p h j c", j=4, h=2), ACT.Copy).then_inc(sem("ht"), 1)
                    if ctx_too:
                        act.wait_ge(sem("hidT_c"), i * 2 + (e + 1))
                        S.activation(HT.rearrange("p (h j) c -> p h j c", h=2)[:, :, :, CAP_L:CW],
                                     bank(6).rearrange("p (j z h c) -> p z h j c", j=4, z=2, h=2)[:, 1], ACT.Copy).then_inc(sem("ht_c"), 1)
                    if e and not last_pair:
                        picked(i + 1, 1)
                    act.wait_ge(ffn_used[5], i * 2 + (e + 1 + l * NE))
                    S.activation(YL[e][0:64, :], bank(3)[0:64, :], ACT.Copy)
                    last = S.activation(YL[1 - e][64:P, :], bank(3)[64:P, :], ACT.Copy)
                    if ctx_too:
                        S.activation(YC[e][0:64, :], bank(4)[0:64, :], ACT.Copy)
                        last = S.activation(YC[1 - e][64:P, :], bank(4)[64:P, :], ACT.Copy)
                    last.then_inc(sem("yev"), 1)

                picked(0, 0)
                picked(0, 1)
                with act.Fori(0, PAIRS - 1) as i:
                    for e in range(2):
                        expert(i, e, False)
                for e in range(2):
                    expert(PAIRS - 1, e, True)

            act.wait_ge(sem("x_in"), 16)
            for t in range(NT):
                norm_square(0, "a", t, t)
            for t in range(NT):
                norm_scale(0, "a", t, t)
            for k in range(MOD_EARLY):
                act.wait_ge(sem("modrow"), k + 1)
                if k >= 2:
                    act.wait_ge(sem("modcol"), k - 1)
                S.activation(w(512 + 512 * (k % 2), 512), bank(k % 2), ACT.Copy).then_inc(sem("modrow_out"), 1)
            for l in range(DEPTH):
                h_ctx(l, "a")
                if l:
                    act.wait_ge(sem("x_kept"), 16 * NLT)
                project_out(l, 0, fm_parts(l, 0))
                n = n_items(l, 1)
                for b in range(2):
                    act.wait_ge(sem("proj"), n + 1 + l * PER["proj"])
                    S.activation(by_column(FM[:, NQ + b, 0:LAT], True), by_column(bank(n % 4), False), ACT.Copy)\
                        .then_inc(sem("proj_out"), 1)
                    n += 1
                for t in range(NT):
                    act.wait_ge(sem("proj"), n + 1 + l * PER["proj"])
                    m = 256 if t < NLT else 512
                    S.activation(TM[:, t, TM_GV:TM_GV + m], bank(n % 4, m), ACT.Copy).then_inc(sem("proj_out"), 1)
                    n += 1
                for j in range(2):
                    act.wait_ge(sem("proj"), n + 1 + l * PER["proj"])
                    S.activation(TM[:, 2 * j:2 * j + 2, TM_NV:TM_SV], v3(bank(n % 4), 2), ACT.Copy).then_inc(sem("proj_out"), 1)
                    n += 1
                gla_exps(l)
                ru = IN_AT[l] + 2
                act.wait_ge(ring_full[lap(ru)[0]], 16 * (lap(ru)[1] + 1))
                act.wait_ge(sem("router_zero"), 1)
                S.activation(router[:, :, 0:NE], v3(ringv[:, lap(ru)[0], KC * 384:KC * 400], KC), ACT.Copy).then_inc(sem("router_in"), 1)
                gg = width(l) // P
                for t in range(NT):
                    act.wait_ge(sem("proj"), n + 1 + l * PER["proj"])
                    m = 384 if t < gg else P
                    S.activation(TM[:, t, TM_SV:TM_SV + m], bank(n % 4, m), ACT.Copy).then_inc(sem("proj_out"), 1)
                    n += 1
                gla_gate(l)
                project_out(l, 3, fm_parts(l, 3))
                gla_keys(l)
                project_out(l, 4, fm_parts(l, 4))
                gla_rms(l)
                attend(l)
                gate_rows(l, "a")
                post(l, "a")
                ffn(l)
                gate_rows(l, "f")
                post(l, "f")

        @block.vector
        def _(dve):
            link = Chain(dve, "dve_chain")
            dve.wait_ge(sem("param_in"), 16)
            for l in range(DEPTH):
                V.tensor_scalar(nsink[:, l * SWA_H:(l + 1) * SWA_H], prm[:, l * PARAMS + P_SINK:l * PARAMS + P_SINK + SWA_H], -1.0, None, ALU.mult)
            dve.wait_ge(sem("band_lo"), 1)
            dve.wait_ge(sem("c_in"), 16)
            dve.wait_ge(sem("c_exp"), 1)
            link(V.tensor_scalar(CTMP[:, 0:16], CTMP[:, 0:16], 1.0, None, ALU.add))
            link(V.reciprocal(CTMP[:, 0:16], CTMP[:, 0:16]))
            dve.wait_ge(sem("c_zero"), 1)
            V.tensor_tensor(CS32[:, :, 0:2], CS.rearrange("p (k w) -> p k w", w=2), CTMP.rearrange("p (k w) -> p k w", w=2), ALU.mult)\
                .then_inc(sem("silu_c"), 1)

            def rms(l, half, i, t):
                dve.wait_ge(sem("sq"), i + 1 + before("sq", l, half))
                V.reciprocal(rs[:, NT + t:NT + t + 1], ss[:, NT + t:NT + t + 1]).then_inc(sem("rms"), 1)

            def mod_out(n0, n1):
                l, a, n = n0 // MOD_UNITS, 8 * (n0 % MOD_UNITS), 8 * (n1 - n0)
                dve.wait_ge(sem("param_in"), 16)
                dve.wait_ge(sem("modcol"), n1)
                V.tensor_tensor(modc[:, l * 96 + a:l * 96 + a + n], bank(6, n, 384 + a),
                                prm[:, l * PARAMS + P_BMOD + a:l * PARAMS + P_BMOD + a + n], ALU.add).then_inc(sem("mod_out"), 1)
                dve.wait_ge(sem("mod_out"), (MOD_EARLY, MOD_UNITS, 2 * MOD_UNITS).index(n1) + 1)

            def mod_cols(l, s):
                gain = prm[:, l * PARAMS + P_GAIN + 16 * s:l * PARAMS + P_GAIN + 16 * s + KC]
                for wch in range(2):
                    sh = modv[:, l, 24 * s:24 * s + 8, wch]
                    sc = modv[:, l, 24 * s + 8:24 * s + 16, wch]
                    V.scalar_tensor_tensor(colv[:, s, wch, 0, :], sc, 1.0, gain, ALU.add, ALU.mult)
                    V.tensor_copy(colv[:, s, wch, 1, :], sh).then_inc(sem("cols"), 1)
                dve.wait_ge(sem("cols"), 2 * (2 * l + s) + 2)

            def h_out(l, half):
                s = 0 if half == "a" else 1
                per = 2 if half == "a" or l < DEPTH - 1 else 1
                for k in range(KC):
                    dve.wait_ge(sem("xT"), per * k + 1 + before("xT", l, half))
                    V.tensor_scalar(hTv[:, k, 0:LAT], bank(2 * (k % 2)), colv[:, s, 0, 0, k:k + 1], colv[:, s, 0, 1, k:k + 1],
                                    ALU.mult, ALU.add).then_inc(sem("h_t"), 1)

            def gla_decay(l):
                p0 = l * PARAMS
                for d in range(2):
                    dve.wait_ge(sem("z"), d + 1 + l * PER["z"])
                    bias = prm[:, p0 + P_AB + d:p0 + P_AB + d + 1]
                    V.tensor_scalar(E[d][:, 0:LAT], bank(4 + d), bias, None, ALU.add)
                    V.tensor_scalar(E[d][:, LAT:TOK], bank(6 + d, CTX), bias, None, ALU.add).then_inc(sem("z_out"), 1)
                for d in range(2):
                    dve.wait_ge(sem("softplus"), d + 1 + l * PER["softplus"])
                    link(V.tensor_scalar(E[d], E[d], 0.0, 1.0 / TAU, ALU.min, ALU.mult))
                    link(V.scalar_tensor_tensor(E[d], E[2 + d], -1.0 / TAU, E[d], ALU.mult, ALU.add))
                    for t in range(NT):
                        c = slice(t * P, (t + 1) * P)
                        V.tensor_tensor_scan(CUM[d][:, c], ones[:, :], E[d][:, c], 0.0, ALU.mult, ALU.add)\
                            .then_inc(sem("scan"), 1)
                    dve.wait_ge(sem("scan"), NT * (d + 1) + l * PER["scan"])
                c3 = [v3(CUM[d], NT) for d in range(2)]
                for d in range(2):
                    V.tensor_copy(v3(gss[:, 6 * d:6 * d + 6], NT), c3[d][:, :, P - 1:P]).then_inc(sem("totc"), 1)
                dve.wait_ge(sem("totc"), 2 + l * PER["totc"])
                tot_b = gss[:, 6:12].unsqueeze(2).broadcast_to([P, NT, P])
                link(V.tensor_tensor(c3[1], tot_b, c3[1], ALU.subtract))
                link(V.tensor_tensor(CUM[1], CUM[1], E[1], ALU.add))
                for d in range(2):
                    tot = gss[:, 6 * d:6 * d + 6].unsqueeze(2).broadcast_to([P, NT, P])
                    V.tensor_tensor(v3(E[d], NT), tot, c3[d], ALU.subtract).then_inc(sem("ke_arg"), 1)

            def gla_state(l):
                dve.wait_ge(sem("proj_out"), 2 + l * PER["proj_out"])
                for d in range(2):
                    dve.wait_ge(sem("ke_exp"), d + 1 + l * PER["ke_exp"])
                    V.tensor_tensor(E[d], E[d], FM[:, GK, :], ALU.mult).then_inc(sem("ke"), 1)
                V.memset(STATE[0][:, F_ORD[0], :], 0.0)
                link(V.memset(STATE[1][:, B_ORD[0], :], 0.0))
                dve.wait_ge(sem("tot_exp"), 1 + l * PER["tot_exp"])
                hm = cst[:, C_HM:C_HM + GLA_H]
                for i in range(NT - 1):
                    dve.wait_ge(sem("dS"), i + 1 + l * PER["dS"])
                    hmb = hm.unsqueeze(2).broadcast_to([P, GLA_H, DV])
                    for d, order in enumerate((F_ORD, B_ORD)):
                        V.tensor_tensor(v3(bank(4 + i % 2, 256, 256 * d), GLA_H), v3(bank(4 + i % 2, 256, 256 * d), GLA_H), hmb,
                                        ALU.mult).then_inc(sem("dSm"), 1)
                    dve.wait_ge(sem("dSm"), 2 * i + 2 + l * PER["dSm"])
                    for d, order in enumerate((F_ORD, B_ORD)):
                        a, b = order[i], order[i + 1]
                        V.scalar_tensor_tensor(STATE[d][:, b, :], STATE[d][:, a, :], grs[:, 6 * d + a:6 * d + a + 1],
                                               bank(4 + i % 2, 256, 256 * d), ALU.mult, ALU.add).then_inc(sem("state"), 1)
                    dve.wait_ge(sem("state"), 2 * i + 2 + l * PER["state"])

            def rope(l):
                for i, b in enumerate([SK, SQ, SQ + 1, SQ + 2, SQ + 3]):
                    dve.wait_ge(sem("rot"), i + 1 + l * PER["rot"])
                    V.tensor_tensor(A_TMP, bank(6 + i % 2), cst[:, C_SIN:C_SIN + LAT], ALU.mult)
                    link(V.tensor_tensor(FM[:, b, 0:LAT], FM[:, b, 0:LAT], cst[:, C_COS:C_COS + LAT], ALU.mult))
                    V.tensor_tensor(FM[:, b, 0:LAT], FM[:, b, 0:LAT], A_TMP, ALU.add).then_inc(sem("rope"), 1)
                    dve.wait_ge(sem("rope"), i + 1 + l * PER["rope"])

            def gla_queries(l):
                n = width(l)
                nt = n // P
                dve.wait_ge(sem("keT"), 3 + l * PER["keT"])
                for d in range(2):
                    c3 = v3(CUM[d], NT)[:, 0:nt, :]
                    mid = c3[:, :, P // 2:P // 2 + 1].broadcast_to([P, nt, P])
                    link(V.tensor_tensor(v3(E[3 * d + 2][:, 0:n], nt), c3, mid, ALU.subtract))
                    V.tensor_scalar(E[3 * d][:, 0:n], E[3 * d + 2][:, 0:n], 80.0, None, ALU.min).then_inc(sem("q_arg"), 1)
                    V.tensor_scalar(E[3 * d + 1][:, 0:n], E[3 * d + 2][:, 0:n], -80.0, -1.0, ALU.max, ALU.mult)\
                        .then_inc(sem("q_arg"), 1)
                    dve.wait_ge(sem("q_arg"), 3 * d + 2 + l * PER["q_arg"])
                    V.tensor_copy(E[3 * d + 2][:, 0:n], CUM[d][:, 0:n]).then_inc(sem("q_arg"), 1)
                dve.wait_ge(sem("q_arg"), 6 + l * PER["q_arg"])
                rope(l)
                q = FM[:, GQ, 0:n]
                for d in range(2):
                    for i in range(3):
                        dve.wait_ge(sem("q_exp"), 3 * d + i + 1 + l * PER["q_exp"])
                        src = FM[:, GK, 0:n] if i == 1 else q
                        V.scalar_tensor_tensor(E[3 * d + i][:, 0:n], E[3 * d + i][:, 0:n], 1.0 if i == 1 else DK ** -0.5,
                                               src, ALU.mult, ALU.mult).then_inc(sem("qk"), 1)
                dve.wait_ge(sem("qk"), 6 + l * PER["qk"])

            def gla_out(l):
                hmb = cst[:, C_HM:C_HM + GLA_H].unsqueeze(2).broadcast_to([P, GLA_H, P])
                ts = tiles(l)
                def queries(i):
                    c = slice(ts[i] * P, (ts[i] + 1) * P)
                    for d in range(2):
                        V.tensor_tensor(v3(QBLK[2 * (i % 2) + d], GLA_H), E[3 * d][:, c].unsqueeze(1).broadcast_to([P, GLA_H, P]), hmb,
                                        ALU.mult).then_inc(sem("qblk"), 1)

                def output(i):
                    dve.wait_ge(sem("o"), i + 1 + l * PER["o"])
                    V.tensor_copy(glao[:, ts[i] * 256:(ts[i] + 1) * 256], bank(6 + i % 2, 256)).then_inc(sem("o_out"), 1)

                queries(0)
                for i in range(len(ts)):
                    if i + 1 < len(ts):
                        if i:
                            dve.wait_ge(sem("scores"), i + l * PER["scores"])
                        queries(i + 1)
                    dve.wait_ge(sem("scores"), i + 1 + l * PER["scores"])
                    if i:
                        output(i - 1)
                    for d, (m, dst) in enumerate(((C_MF, A_SB), (C_MB, A_TMP))):
                        link(V.tensor_tensor(v3(dst, GLA_H), v3(bank((4, 0)[i % 2] + d), GLA_H),
                                             cst[:, m:m + P].unsqueeze(1).broadcast_to([P, GLA_H, P]), ALU.mult))
                    V.tensor_tensor(A_SB, A_SB, A_TMP, ALU.add).then_inc(sem("A"), 1)
                output(len(ts) - 1)
                nt = len(ts)
                n = nt * 256
                dve.wait_ge(sem("o_out"), nt + l * PER["o_out"])
                sq = w(2048, n)
                link(V.tensor_tensor(sq, glao[:, 0:n], glao[:, 0:n], ALU.mult))
                V.reduce_sum(gss[:, 0:4 * nt], v3(sq, 4 * nt), AX).then_inc(sem("gla_ms"), 1)
                dve.wait_ge(sem("gla_rms"), 1 + l * PER["gla_rms"])
                link(V.reciprocal(grs[:, 0:4 * nt], grs[:, 0:4 * nt]))
                link(V.tensor_tensor(v3(glao[:, 0:n], 4 * nt), v3(glao[:, 0:n], 4 * nt),
                                     grs[:, 0:4 * nt].unsqueeze(2).broadcast_to([P, 4 * nt, DV]), ALU.mult))
                dve.wait_ge(sem("gate_gain"), 1 + l * PER["gate_gain"])
                V.tensor_tensor(v3(glao[:, 0:n], nt), v3(glao[:, 0:n], nt), TM[:, 0:nt, TM_GG:TMW], ALU.mult)\
                    .then_inc(sem("gla_o"), 1)
                dve.wait_ge(sem("gla_o"), 1 + l * PER["gla_o"])

            def attend(l):
                us = units(l)
                nb = 0
                for u in range(len(us) + 3):
                    if u < len(us):
                        ti, t, kind, h = us[u]
                        k0, nl = local_keys(t)
                        dve.wait_ge(sem("s"), u + 1 + l * PER["s"])
                        if u >= 2:
                            dve.wait_ge(sem("exp"), u - 1 + l * PER["exp"])
                        st = AST[:, 8 * (u % 4):8 * (u % 4) + 8]
                        local, context, both = score_place(u, nl)
                        if kind == "s":
                            orig = h // 2 + 4 * (h % 2)
                            link(V.reduce_max(st[:, 1:2], both, AX))
                            V.tensor_scalar(st[:, 2:3], st[:, 1:2], -SCALE, nsink[:, l * SWA_H + orig:l * SWA_H + orig + 1],
                                            ALU.mult, ALU.min).then_inc(sem("max"), 1)
                        elif nl:
                            dve.wait_ge(sem(f"bias{nb % 4}"), 16 * (nb // 4 + 1) + l * PER["bias"])
                            V.reduce_max(st[:, 1:2], context, AX)
                            link(V.scalar_tensor_tensor(SC[u % 2][:, 0:nl], local, SCALE, BIAS[nb % 4][:, 0:nl], ALU.mult, ALU.add))
                            link(V.reduce_max(st[:, 0:1], SC[u % 2][:, 0:nl], AX))
                            link(V.tensor_scalar(st[:, 3:4], st[:, 1:2], SCALE, st[:, 0:1], ALU.mult, ALU.max))
                            V.tensor_scalar(st[:, 2:3], st[:, 3:4], -1.0, None, ALU.mult).then_inc(sem("max"), 1)
                            nb += 1
                        else:
                            link(V.reduce_max(st[:, 1:2], context, AX))
                            V.tensor_scalar(st[:, 2:3], st[:, 1:2], -SCALE, None, ALU.mult).then_inc(sem("max"), 1)
                    v = u - 1
                    if 0 <= v < len(us):
                        ti, t, kind, h = us[v]
                        dve.wait_ge(sem("exp"), v + 1 + l * PER["exp"])
                        if v >= 2:
                            dve.wait_ge(sem("T"), v - 1 + l * PER["T"])
                        st = AST[:, 8 * (v % 4):8 * (v % 4) + 8]
                        terms = [5] + ([6] if kind == "s" else [4] if t < NLT else [])
                        den = st[:, 5:6]
                        if len(terms) == 2:
                            den = st[:, 7:8]
                            link(V.tensor_tensor(den, st[:, terms[0]:terms[0] + 1], st[:, terms[1]:terms[1] + 1], ALU.add))
                        link(V.reciprocal(st[:, 3:4], den))
                        V.tensor_scalar(RDIAG[v % 2], ident, st[:, 3:4], None, ALU.mult).then_inc(sem("diagr"), 1)
                    v = u - 3
                    if v >= 0 and v % 2:
                        ti, t, kind, h = us[v]
                        dve.wait_ge(sem("pv"), v // 2 + 1 + l * PER["pv"])
                        if l == 0 and MOD_SLOT.get(v // 2) == MOD_UNITS:
                            mod_out(MOD_EARLY, MOD_UNITS)
                        o = bank(6, P)
                        if kind == "n" and t < NLT:
                            dst = by_column(hTv[:, 2 + h // 2, 0:LAT], False)[:, 16 * t:16 * (t + 1), :]
                            V.tensor_copy(dst, by_column(o, True)).then_inc(sem("mix"), 1)
                        else:
                            k = 2 + h // 2 if kind == "n" else 4 + h // 2
                            V.tensor_copy(hTv[:, k, t * P:(t + 1) * P], o).then_inc(sem("mix"), 1)

            def gate_rows(l, half):
                s = 0 if half == "a" else 1
                if half == "a":
                    dve.wait_ge(sem("pv"), len(units(l)) // 2 + l * PER["pv"])
                for wch in range(2 if l < DEPTH - 1 else 1):
                    g0 = l * PARAMS + P_GAIN + 16 * s + 8
                    link(V.tensor_tensor(gcol[:, 8 * wch:8 * wch + 8], modv[:, l, 24 * s + 16:24 * s + 24, wch], prm[:, g0:g0 + KC], ALU.mult))
                    V.tensor_tensor(v3(DIAG[wch], KC), ident.unsqueeze(1).broadcast_to([P, KC, P]),
                                    gcol[:, 8 * wch:8 * wch + 8].unsqueeze(2).broadcast_to([P, KC, P]), ALU.mult)\
                        .then_inc(sem("diag"), 1)

            def post(l, half):
                dve.wait_ge(sem("grow_out"), 1 + before("grow_out", l, half))
                nxt = (l, "f") if half == "a" else (l + 1, "a")
                if half == "f":
                    last_add(l, 0)
                for i, t in enumerate(tiles(l)):
                    if half == "f" and i + 1 < len(tiles(l)):
                        last_add(l, i + 1)
                    dve.wait_ge(sem("psq"), i + 1 + before("psq", l, half))
                    link(V.reciprocal(rs[:, t:t + 1], ss[:, t:t + 1]))
                    src = ps[:, (i % 2) * D:(i % 2) * D + D] if half == "a" else ACC[:, t, :]
                    V.scalar_tensor_tensor(GAIN_X, src, rs[:, t:t + 1], GROW[:, 0 if t < NLT else 1, :], ALU.mult, ALU.mult)\
                        .then_inc(sem("y_used"), 1)
                    dve.wait_ge(sem("y_used"), i + 1 + before("y_used", l, half))
                    if half == "a":
                        dve.wait_ge(sem(f"x_back{t}"), 16 * (l + 1 if t < NLT else 1))
                        done, n = "x_mid", i + 1 + l * PER["x_mid"]
                    else:
                        dve.wait_ge(sem(f"x_again{t}"), 16 * (l + 1 if t < NLT else 1))
                        done, n = ("x_ready", t + 1 + l * NLT) if t < NLT else ("xc_ready", t - NLT + 1)
                    V.tensor_tensor(X[:, t, :], X[:, t, :], GAIN_X, ALU.add).then_inc(sem(done), 1)
                    dve.wait_ge(sem(done), n)
                    if i and nxt[0] < DEPTH:
                        rms(*nxt, i - 1, tiles(l)[i - 1])
                if nxt[0] < DEPTH:
                    rms(*nxt, i, t)

            def route(l):
                nt = len(tiles(l))
                ctx_too = l < DEPTH - 1
                dve.wait_ge(sem("logits"), 1 + l * PER["logits"])
                lg = v3(bank(5, NT * NE), NT)[:, 0:nt, :]
                st = AFM
                link(V.reduce_max(st[:, 0:nt], lg, AX))
                V.tensor_tensor(LOG[:, 0:nt, :], lg, st[:, 0:nt].unsqueeze(2).broadcast_to([P, nt, NE]), ALU.subtract)\
                    .then_inc(sem("logit_sub"), 1)
                link(V.memset(AFF, -1.0))
                dve.wait_ge(sem("logit_exp"), 1 + l * PER["logit_exp"])
                link(V.reduce_sum(st[:, 8:8 + nt], LOG[:, 0:nt, :], AX))
                link(V.reciprocal(st[:, 8:8 + nt], st[:, 8:8 + nt]))
                if ctx_too:
                    V.tensor_tensor(AFF[:, 0:NCT, 32:48], LOG[:, NLT:NT, :], st[:, 12:14].unsqueeze(2).broadcast_to([P, NCT, NE]), ALU.mult)
                V.tensor_tensor(AFF[:, :, 0:NE], LOG[:, 0:NLT, :], st[:, 8:12].unsqueeze(2).broadcast_to([P, NLT, NE]), ALU.mult)\
                    .then_inc(sem("aff"), 1)
                dve.wait_ge(sem("affT"), 1 + l * PER["affT"])
                a = [AFT0[0:48, 0:LAT], AFT1[0:48, 0:LAT]]
                link(V.tensor_copy(a[0], ps[0:48, 7 * 512:8 * 512]))
                for r in range(CAP_L // 8):
                    sl = slice(8 * r, 8 * r + 8)
                    src, dst = a[r % 2], a[(r + 1) % 2]
                    link(V.max(VALS[0:48, sl], src))
                    V.max_index(idxu[0:48, sl], VALS[0:48, sl], src)
                    link(V.match_replace(dst, VALS[0:48, sl], src, -1.0))
                V.tensor_copy(IDXF[0:48, :], idxu[0:48, :]).then_inc(sem("picked"), 1)

            def ffn(l):
                ctx_too = l < DEPTH - 1
                nt = len(tiles(l))
                per = 2 * nt
                dve.wait_ge(sem("idx_in"), l * 32 + (32 if ctx_too else 16))
                dve.wait_ge(sem("acc_zero"), nt + l * PER["acc_zero"])
                if ctx_too:
                    link(V.memset(HIDC[0:64, :], 0.0))

                def select(i):
                    for t in range(NLT):
                        last = V.tensor_scalar(SEL_L[:, t, :], IDXL[:, bass.ts(i, P)], cst[:, C_IOTA + t:C_IOTA + t + 1], None, ALU.is_equal)
                    if ctx_too:
                        for t in range(NCT):
                            last = V.tensor_scalar(SEL_C[:, t, :], IDXC[:, bass.ts(i, 64)], cst[:, C_IOTA + t:C_IOTA + t + 1], None, ALU.is_equal)
                    last.then_inc(sem("sel"), 1)

                def slots(i):
                    for sw in range(2):
                        last = V.tensor_scalar(PT_L[sw], IOTAR, COLS_L[:, sw, bass.ds(i, 1)], COLS_L[:, 2 + sw, bass.ds(i, 1)],
                                               ALU.is_equal, ALU.mult)
                        if ctx_too:
                            last = V.tensor_scalar(PT_C[sw], IOTAR[:, 0:CTX], COLS_C[:, sw, bass.ds(i, 1)], COLS_C[:, 2 + sw, bass.ds(i, 1)],
                                                   ALU.is_equal, ALU.mult)
                    last.then_inc(sem("ptok"), 1)

                def picked_ctx(i):
                    dve.wait_ge(sem("gather"), i * 3 + 3)
                    for k in range(KC):
                        last = V.tensor_scalar(XST[:, k, :, CAP_L:CW], v3(bank(1, 64, k * 64), 2), colv[:, 1, 1, 0, k:k + 1],
                                               colv[:, 1, 1, 1, k:k + 1], ALU.mult, ALU.add)
                    last.then_inc(sem("xs_ctx"), 1)

                def add(i):
                    for c in range(per):
                        t, half = tiles(l)[c // 2], c % 2
                        dve.wait_ge(sem("comb"), i * per + (c + 1 + l * PER["comb"]))
                        d = ACC[:, t, half * 512:half * 512 + 512]
                        V.tensor_tensor(d, d, bank(COMB_BANKS[c % 3]), ALU.add).then_inc(sem("acc"), 1)

                def expert(i, e, first, last_pair):
                    dve.wait_ge(sem("silu"), i * 2 + (e + 1 + l * NE))
                    V.tensor_tensor(HIDL, SGL, bank(1), ALU.mult).then_inc(sem("hid"), 1)
                    if ctx_too:
                        dve.wait_ge(sem("silu_ctx"), i * 2 + (e + 1))
                        V.tensor_tensor(HIDC[64:P, :], SGC[64:P, :], bank(2)[64:P, :], ALU.mult).then_inc(sem("hid_c"), 1)
                    if e == 0 and not first:
                        add(i - 1)
                    if e == 0:
                        if first:
                            dve.wait_ge(sem("cols_in"), picks(l) + l * picks(0))
                            dve.wait_ge(sem("iota"), 16 + l * PER["iota"])
                        slots(i)
                        if not last_pair:
                            select(i + 1)
                    elif ctx_too and not last_pair:
                        picked_ctx(i + 1)

                select(0)
                if ctx_too:
                    picked_ctx(0)
                for e in range(2):
                    expert(0, e, True, False)
                with dve.Fori(1, PAIRS - 1) as i:
                    for e in range(2):
                        expert(i, e, False, False)
                for e in range(2):
                    expert(PAIRS - 1, e, False, True)
                dve.wait_ge(sem("acc"), (PAIRS - 1) * per + l * PER["acc"])
                dve.wait_ge(sem("ptok"), (l + 1) * PAIRS)

            def last_add(l, i):
                t, done = tiles(l)[i], acc_total(l) - 2 * len(tiles(l))
                for c in (2 * i, 2 * i + 1):
                    dve.wait_ge(sem("comb"), done + c + 1)
                    d = ACC[:, t, (c % 2) * 512:(c % 2) * 512 + 512]
                    V.tensor_tensor(d, d, bank(LAST_BANKS[c % 3]), ALU.add).then_inc(sem("acc"), 1)

            for t in range(NT):
                rms(0, "a", t, t)
            mod_out(0, MOD_EARLY)
            for l in range(DEPTH):
                mod_cols(l, 0)
                dve.wait_ge(sem("const_in"), 16)
                h_out(l, "a")
                gla_decay(l)
                gla_state(l)
                gla_queries(l)
                gla_out(l)
                attend(l)
                if l == 0:
                    mod_out(MOD_UNITS, 2 * MOD_UNITS)
                gate_rows(l, "a")
                mod_cols(l, 1)
                post(l, "a")
                h_out(l, "f")
                route(l)
                ffn(l)
                gate_rows(l, "f")
                post(l, "f")

        @block.tensor
        def _(pe):
            def arrived(n):
                pe.wait_ge(ring_full[lap(n)[0]], 16 * (lap(n)[1] + 1))
                return ringv[:, lap(n)[0], :]

            def mod_rows(n, ob):
                at = mod_at(n)
                u = v3(arrived(at), KC)
                for kc in range(KC):
                    j = kc % 4
                    last = T.matmul(ob[32 * j:32 * j + 32, :], CS32[:, kc, :], u[:, kc, :], start=kc < 4, stop=kc >= 4)
                last.then_inc(sem("modrow"), 1)
                pe.drain().then_inc(ring_used[lap(at)[0]], 1)

            def mod_cols(n, row):
                pe.wait_ge(sem("modrow_out"), n + 1)
                for j in range(4):
                    last = T.matmul(bank(6, 2, 384 + 2 * (4 * (n % MOD_UNITS) + j)), row[:, j * P:(j + 1) * P], cst[:, C_SUM:C_SUM + 2], start=True, stop=True)
                last.then_inc(sem("modcol"), 1)

            def turn_x(l, half):
                ctx_too = half == "a" or l < DEPTH - 1
                pe.wait_ge(sem("xn"), (NT if half == "a" else len(tiles(l))) + before("xn", l, half))
                per = 2 if ctx_too else 1
                for k in range(KC):
                    if k >= 2:
                        pe.wait_ge(sem("h_t"), k - 1 + before("h_t", l, half))
                        if ctx_too:
                            pe.wait_ge(sem("h_ctx"), k - 1 + before("h_ctx", l, half))
                    for wch in range(per):
                        t0 = NLT * wch
                        for t in range(NLT if wch == 0 else NCT):
                            last = T.transpose(bank(2 * (k % 2) + wch, P, t * P), XN[:, t0 + t, k * P:(k + 1) * P], ident)
                        last.then_inc(sem("xT"), 1)
                pe.wait_ge(sem("h_t"), KC + before("h_t", l, half))
                if ctx_too:
                    pe.wait_ge(sem("h_ctx"), KC + before("h_ctx", l, half))

            def project(l, unit):
                n = n_items(l, unit)
                g = IN_AT[l] + unit
                uw = arrived(g)

                def free(n):
                    if n >= 4:
                        pe.wait_ge(sem("proj_out"), n - 3 + l * PER["proj_out"])

                if unit in (1, 2):
                    cols_ = 512 if unit == 1 else 384
                    v = v3(uw[:, 0:KC * cols_], KC)
                    if unit == 1:
                        for b in range(2):
                            free(n)
                            for kc in range(KC):
                                last = T.matmul(bank(n % 4), v[:, kc, 256 + b * P:256 + (b + 1) * P], hTv[:, kc, 0:LAT],
                                                start=kc == 0, stop=kc == KC - 1)
                            last.then_inc(sem("proj"), 1)
                            n += 1
                    for t in range(NT):
                        free(n)
                        k_ = 256 if unit == 1 and t < NLT else P if unit == 2 and t * P >= width(l) else cols_
                        for kc in range(KC):
                            last = T.matmul(bank(n % 4, k_), hTv[:, kc, t * P:(t + 1) * P], v[:, kc, 0:k_], start=kc == 0, stop=kc == KC - 1)
                        last.then_inc(sem("proj"), 1)
                        n += 1
                    if unit == 1:
                        for j in range(2):
                            free(n)
                            for i in range(4):
                                t, b = 2 * j + i // 2, i % 2
                                last = T.transpose(bank(n % 4, P, i * P), FM[:, NQ + b, t * P:(t + 1) * P], ident)
                            last.then_inc(sem("proj"), 1)
                            n += 1
                    if unit == 2:
                        pe.wait_ge(sem("router_in"), 1 + l * PER["router_in"])
                else:
                    for j, b, t0, tn in fm_items(l, unit):
                        free(n)
                        m = 48 if b == AL else P
                        for kc in range(KC):
                            last = T.matmul(bank(n % 4, tn)[0:m, :], uw[:, j * D + kc * P:j * D + kc * P + m], hTv[:, kc, t0:t0 + tn],
                                            start=kc == 0, stop=kc == KC - 1)
                        last.then_inc(sem("proj"), 1)
                        n += 1
                        if unit == 4:
                            rot(l, n - n_items(l, 4) - 1)
                pe.drain().then_inc(ring_used[lap(g)[0]], 1)

            def gla_z(l):
                pe.wait_ge(sem("proj_out"), n_items(l, 1) + l * PER["proj_out"])
                aup = prm[:, l * PARAMS + P_AUP:l * PARAMS + P_AUP + P]
                for d in range(2):
                    r = slice(32 * d, 32 * d + 16)
                    T.matmul(bank(4 + d), aup[r, :], FM[r, AL, 0:LAT], start=True, stop=True)
                    T.matmul(bank(6 + d, CTX), aup[r, :], FM[r, AL, LAT:TOK], start=True, stop=True).then_inc(sem("z"), 1)

            def gla_keys(l):
                pe.wait_ge(sem("ke"), 2 + l * PER["ke"])
                for g in range(3):
                    for j in range(4):
                        n = 4 * g + j
                        last = T.transpose(bank(4 + g, P, j * P), E[n // NT][:, (n % NT) * P:(n % NT + 1) * P], ident)
                    last.then_inc(sem("keT"), 1)
                pe.wait_ge(sem("keT_out"), 1 + l * PER["keT_out"])
                for i in range(NT - 1):
                    if i >= 2:
                        pe.wait_ge(sem("state"), 2 * (i - 1) + l * PER["state"])
                    for d, order in enumerate((F_ORD, B_ORD)):
                        t = order[i]
                        last = T.matmul(bank(4 + i % 2, 256, 256 * d), KET[:, NT * d + t, :], TM[:, t, TM_GV:TM_GV + 256], start=True, stop=True)
                    last.then_inc(sem("dS"), 1)

            def rot(l, i):
                if i < 5:
                    b = [SK, SQ, SQ + 1, SQ + 2, SQ + 3][i]
                    if i == 0:
                        pe.wait_ge(sem("proj_out"), n_items(l, 4) + l * PER["proj_out"])
                    if i >= 2:
                        pe.wait_ge(sem("rope"), i - 1 + l * PER["rope"])
                    T.matmul(bank(6 + i % 2), cst[:, C_ROT:C_ROT + P], FM[:, b, 0:LAT], start=True, stop=True).then_inc(sem("rot"), 1)

            def gla_out(l):
                pe.wait_ge(sem("qk"), 6 + l * PER["qk"])
                pe.wait_ge(sem("proj_out"), n_items(l, 5) + l * PER["proj_out"])
                pe.wait_ge(sem("rope"), 5 + l * PER["rope"])
                ts = tiles(l)

                def scores(i):
                    pe.wait_ge(sem("qblk"), 2 * i + 2 + l * PER["qblk"])
                    if i >= 2:
                        pe.wait_ge(sem("A"), i - 1 + l * PER["A"])
                    for d in range(2):
                        last = T.matmul(bank((4, 0)[i % 2] + d), E[3 * d + 1][:, ts[i] * P:(ts[i] + 1) * P], QBLK[2 * (i % 2) + d],
                                        start=True, stop=True)
                    last.then_inc(sem("scores"), 1)

                scores(0)
                for i, t in enumerate(ts):
                    if i + 1 < len(ts):
                        scores(i + 1)
                    c = slice(t * P, (t + 1) * P)
                    if i >= 2:
                        pe.wait_ge(sem("o_out"), i - 1 + l * PER["o_out"])
                    for d in range(2):
                        T.matmul(bank(6 + i % 2, 256), E[3 * d + 2][:, c], STATE[d][:, t, :], start=d == 0, stop=False)
                    pe.wait_ge(sem("A"), i + 1 + l * PER["A"])
                    for h in range(GLA_H):
                        last = T.matmul(bank(6 + i % 2, DV, h * DV), A_SB[:, h * P:(h + 1) * P], TM[:, t, TM_GV + h * DV:TM_GV + (h + 1) * DV],
                                        start=False, stop=h == GLA_H - 1)
                    last.then_inc(sem("o"), 1)

            def attend(l):
                us = units(l)
                nt = width(l) // P
                pe.wait_ge(sem("gla_o"), (l + 1) * PER["gla_o"])
                for k in range(2):
                    for t in range(nt):
                        last = T.transpose(ps[:, 4 * 512 + k * TOK + t * P:4 * 512 + k * TOK + (t + 1) * P],
                                           glao[:, t * 256 + k * P:t * 256 + (k + 1) * P], ident)
                last.then_inc(sem("glaT"), 1)
                pe.wait_ge(sem("keys"), 6 * (l + 1))
                pe.wait_ge(sem("band_lo"), 1)

                def scores(u):
                    ti, t, kind, h = us[u]
                    k0, nl = local_keys(t)
                    qb, kb = (NQ + h // 2, NK + h // 2) if kind == "n" else (SQ + h // 2, SK)
                    if h % 2:
                        kb = dict(KEY_COPY)[kb]
                    q = FM[:, qb, t * P:(t + 1) * P]
                    if u >= 2:
                        pe.wait_ge(sem("exp"), u - 1 + l * PER["exp"])
                    local, context, both = score_place(u, nl)
                    if nl:
                        T.matmul(local, q, FM[:, kb, k0:k0 + nl], start=True, stop=kind == "n")
                    if nl and kind == "s":
                        off = P if t == 0 else 0
                        T.matmul(local, ident_lo, band_lo[:, off:off + nl], start=False, stop=True)
                    T.matmul(context, q, FM[:, kb, LAT:TOK], start=True, stop=True).then_inc(sem("s"), 1)

                def products(u):
                    if u == 0:
                        pe.wait_ge(sem("glaT_out"), l + 1)
                    pe.wait_ge(sem("pt_out"), u + 2 + l * PER["pt_out"])
                    if u >= 2:
                        pe.wait_ge(sem("mix"), u // 2 + l * PER["mix"])
                    n = MOD_SLOT.get(u // 2, 0)
                    if l == 0 and n > MOD_EARLY:
                        mod_cols(n - 1, MODROW)
                    t = us[u][1]
                    k0, nl = local_keys(t)
                    kt = [k0 // P + j for j in range(nl // P)] + [NLT, NLT + 1]
                    for j, tk in enumerate(kt):
                        for v in (u, u + 1):
                            kind, h = us[v][2:]
                            c = TM_NV + h * HD if kind == "n" else TM_SV + (h % 2) * HD
                            r_ = 64 * (v % 2)
                            last = T.matmul(bank(6, P)[r_:r_ + 64, :], TM[:, tk, c:c + HD], PT[v % 4][:, j * P:(j + 1) * P],
                                            start=j == 0, stop=j == len(kt) - 1)
                    last.then_inc(sem("pv"), 1)

                scores(0)
                for u in range(len(us) + 3):
                    if u + 1 < len(us):
                        scores(u + 1)
                    v = u - 1
                    if 0 <= v < len(us):
                        nk = (local_keys(us[v][1])[1] + CTX) // P
                        pe.wait_ge(sem("diagr"), v + 1 + l * PER["diagr"])
                        if v == 0:
                            pe.wait_ge(sem("glaT_out"), l + 1)
                        if v >= 1:
                            pe.wait_ge(sem("pt_out"), v + l * PER["pt_out"])
                        for j in range(nk):
                            last = T.matmul(ps[:, 4 * 512 + j * P:4 * 512 + (j + 1) * P], PR[v % 2][:, j * P:(j + 1) * P], RDIAG[v % 2],
                                            start=True, stop=True)
                        last.then_inc(sem("T"), 1)
                    v = u - 3
                    if v >= 0 and v % 2 == 0:
                        products(v)
                        if l == 0 and v // 2 in MOD_SLOT:
                            mod_rows(MOD_SLOT[v // 2], bank(7))
                if l == 0:
                    pe.wait_ge(sem("mix"), len(us) // 2)
                    mod_cols(2 * MOD_UNITS - 1, MODROW)

            def gate_rows(l, half):
                n = 2 if l < DEPTH - 1 else 1
                if half == "a":
                    pe.wait_ge(sem("mix"), len(units(l)) // 2 + l * PER["mix"])
                    if l == 0:
                        pe.wait_ge(sem("mod_out"), 3)
                for wch in range(n):
                    pe.wait_ge(sem("diag"), wch + 1 + before("diag", l, half))
                    for j in range(2):
                        last = T.matmul(bank(4 + 2 * wch + j), ones[:, :], DIAG[wch][:, j * 512:(j + 1) * 512], start=True, stop=True)
                    last.then_inc(sem("grow"), 1)

            def w_out(l):
                u = [v3(arrived(OUT_AT[l] + j), KC) for j in range(2)]
                for i, t in enumerate(tiles(l)):
                    if i >= 2:
                        pe.wait_ge(sem("y_used"), i - 1 + before("y_used", l, "a"))
                    for j in range(2):
                        for kc in range(KC):
                            last = T.matmul(bank(2 * (i % 2) + j), hTv[:, kc, t * P:(t + 1) * P], u[j][:, kc, :], start=kc == 0, stop=kc == KC - 1)
                    last.then_inc(sem("wo"), 1)
                for j in range(OUT_UNITS):
                    pe.drain().then_inc(ring_used[lap(OUT_AT[l] + j)[0]], 1)

            def route(l):
                for b, t0, n in ((6, 0, LAT), (7, LAT, CTX))[:2 if l < DEPTH - 1 else 1]:
                    for kc in range(KC):
                        j = kc % 4
                        last = T.matmul(bank(b, n)[32 * j:32 * j + 32, :], router[:, kc, :], hTv[:, kc, t0:t0 + n],
                                        start=kc < 4, stop=kc >= 4)
                last.then_inc(sem("router_parts"), 1)
                pe.wait_ge(sem("router_sb"), 1 + l * PER["router_sb"])
                for t in sorted(tiles(l)):
                    last = T.matmul(bank(5, NE, t * NE), RPART[:, t * P:(t + 1) * P], cst[:, C_SUM:C_SUM + NE], start=True, stop=True)
                last.then_inc(sem("logits"), 1)
                pe.wait_ge(sem("aff"), 1 + l * PER["aff"])
                for t in range(NLT):
                    last = T.transpose(ps[0:48, 7 * 512 + t * P:7 * 512 + (t + 1) * P], AFF[:, t, :], ident)
                last.then_inc(sem("affT"), 1)
                pe.wait_ge(sem("picked"), 1 + l * PER["picked"])

            def ffn(l):
                ctx_too = l < DEPTH - 1
                nt = len(tiles(l))
                per = 2 * nt
                gate_up = [v3(slot[j], 2) for j in range(4)]
                down = [v3(slot[4 + j], 4) for j in range(2)]

                def gather(i, g):
                    for k in range(4):
                        c0 = (4 * g + k) * P
                        for t in range(NLT):
                            last = T.matmul(bank((7, 0)[g], P, k * P), XN[:, t, c0:c0 + P], SEL_L[:, t, :], start=t == 0, stop=t == NLT - 1)
                    last.then_inc(sem("gather"), 1)

                def gather_ctx(i):
                    for k in range(KC):
                        for t in range(NCT):
                            last = T.matmul(bank(1, 64, k * 64), XN[:, NLT + t, k * P:(k + 1) * P], SEL_C[:, t, :], start=t == 0, stop=t == NCT - 1)
                    last.then_inc(sem("gather"), 1)

                def combine(i, cs, wait_hid=None, banks=COMB_BANKS):
                    for c in cs:
                        t, half = tiles(l)[c // 2], c % 2
                        if c >= 3:
                            pe.wait_ge(sem("acc"), i * per + (c - 2 + l * PER["acc"]))
                        elif c == 1 and wait_hid is not None:
                            pe.wait_ge(sem("hid"), wait_hid)
                        ob = bank(banks[c % 3])
                        if t < NLT:
                            last = T.matmul(ob, PT_L[half][:, t * P:(t + 1) * P], YL[half], start=True, stop=True)
                        else:
                            last = T.matmul(ob, PT_C[half][:, (t - NLT) * P:(t - NLT + 1) * P], YC[half], start=True, stop=True)
                        last.then_inc(sem("comb"), 1)

                def turn_hidden(i, e):
                    pe.wait_ge(sem("hid"), i * 2 + (e + 1 + l * NE))
                    for j in range(4):
                        last = T.transpose(bank(5, P, j * P), HIDL[:, j * P:(j + 1) * P], ident)
                    last.then_inc(sem("hidT"), 1)

                def turn_hidden_ctx(i, e):
                    pe.wait_ge(sem("hid_c"), i * 2 + (e + 1))
                    for j in range(4):
                        last = T.transpose(bank(6, P, j * P), HIDC[:, j * P:(j + 1) * P], ident)
                    last.then_inc(sem("hidT_c"), 1)

                def turn_all(i, e):
                    turn_hidden(i, e)
                    if ctx_too:
                        turn_hidden_ctx(i, e)

                def expert(i, e, first, last_pair):
                    if e == 0:
                        pe.wait_ge(sem("xs"), i + (1 + l * PAIRS))
                        if ctx_too:
                            pe.wait_ge(sem("xs_ctx"), i + 1)
                    elif not first:
                        pe.wait_ge(sem("acc"), i * per + l * PER["acc"])
                    for j in range(4):
                        pe.wait_ge(ffn_full[j], i * 32 + 16 * (e + 1 + l * NE))
                        for kk in range(2):
                            kc = 2 * j + kk
                            for m in range(2):
                                for h in range(2):
                                    last = T.matmul(bank(m)[64 * h:64 * h + 64, :], XST[:, kc, e, 0:CAP_L],
                                                    gate_up[j][:, kk, m * D + h * 512:m * D + (h + 1) * 512], start=kc == 0, stop=kc == KC - 1)
                            if ctx_too:
                                for g in range(4):
                                    last = T.matmul(bank(2)[32 * g:32 * g + 32, :], XST[:, kc, e, CAP_L:CW],
                                                    gate_up[j][:, kk, g * 512:(g + 1) * 512], start=kc == 0, stop=kc == KC - 1)
                        last.then_inc(ffn_used[j], 1)
                    if e == 0 and not first:
                        pe.wait_ge(sem("yev"), i * 2 + l * NE)
                        pe.wait_ge(sem("ptok"), i + l * PAIRS)
                        combine(i - 1, range(per // 2), i * 2 + (e + 1 + l * NE))
                        turn_all(i, e)
                        combine(i - 1, range(per // 2, per))
                    elif e and not last_pair:
                        pe.wait_ge(sem("sel"), i + (2 + l * PAIRS))
                        gather(i + 1, 0)
                        turn_all(i, e)
                        gather(i + 1, 1)
                        if ctx_too:
                            gather_ctx(i + 1)
                    else:
                        turn_all(i, e)
                    pe.wait_ge(sem("ht"), i * 2 + (e + 1 + l * NE))
                    if ctx_too:
                        pe.wait_ge(sem("ht_c"), i * 2 + (e + 1))
                    if e or l or not first:
                        pe.wait_ge(sem("yev"), i * 2 + (e + l * NE))
                    for kc in range(KC):
                        if kc % 4 == 0:
                            pe.wait_ge(ffn_full[4 + kc // 4], i * 32 + 16 * (e + 1 + l * NE))
                        for g in range(2):
                            h = g ^ e
                            last = T.matmul(bank(3)[64 * g:64 * g + 64, :], HT[:, kc, 0:CAP_L],
                                            down[kc // 4][:, kc % 4, h * 512:(h + 1) * 512], start=kc == 0, stop=kc == KC - 1)
                        if ctx_too and kc % 2:
                            for g in range(4):
                                h, k = (g // 2) ^ e, kc - 1 + g % 2
                                last = T.matmul(bank(4)[32 * g:32 * g + 32, :], HT[:, k, CAP_L:CW],
                                                down[k // 4][:, k % 4, h * 512:(h + 1) * 512], start=kc == 1, stop=kc == KC - 1)
                        if kc % 4 == 3:
                            last.then_inc(ffn_used[4 + kc // 4], 1)

                pe.wait_ge(sem("sel"), 1 + l * PAIRS)
                gather(0, 0)
                gather(0, 1)
                if ctx_too:
                    gather_ctx(0)
                for e in range(2):
                    expert(0, e, True, False)
                with pe.Fori(1, PAIRS - 1) as i:
                    for e in range(2):
                        expert(i, e, False, False)
                for e in range(2):
                    expert(PAIRS - 1, e, False, True)
                pe.wait_ge(sem("yev"), NE + l * NE)
                pe.wait_ge(sem("ptok"), (l + 1) * PAIRS)
                gate_rows(l, "f")
                combine(PAIRS - 1, range(per), banks=LAST_BANKS)

            pe.wait_ge(sem("silu_c"), 1)
            pe.wait_ge(sem("const_in"), 16)
            for n in range(MOD_EARLY + 1):
                if n < MOD_EARLY:
                    if n >= 2:
                        pe.wait_ge(sem("modrow_out"), n - 1)
                    mod_rows(n, bank(n % 2))
                if n:
                    mod_cols(n - 1, w(512 + 512 * ((n - 1) % 2), 512))
            pe.wait_ge(sem("param_in"), 16)
            pe.wait_ge(sem("ones_set"), 1)
            for l in range(DEPTH):
                turn_x(l, "a")
                project(l, 0)
                project(l, 1)
                gla_z(l)
                project(l, 2)
                project(l, 3)
                gla_keys(l)
                project(l, 4)
                gla_out(l)
                attend(l)
                gate_rows(l, "a")
                w_out(l)
                turn_x(l, "f")
                route(l)
                ffn(l)


def _constants(np):
    c = np.zeros((P, CONSTS), np.float32)
    i = np.arange(P)
    c[:, C_ID:C_ID + P] = np.eye(P)
    c[:, C_MF:C_MF + P] = i[:, None] <= i[None, :]
    c[:, C_MB:C_MB + P] = i[:, None] >= i[None, :]
    d, t = np.arange(P) % HD, np.arange(LAT)
    quarter = HD // 4
    freq = np.float32(10000.0) ** (-np.arange(quarter, dtype=np.float32) / np.float32(quarter))
    pos = np.where((d < HD // 2)[:, None], (t // GRID_W)[None, :], (t % GRID_W)[None, :]).astype(np.float32)
    ang = pos * freq[d % quarter][:, None].astype(np.float32)
    c[:, C_COS:C_COS + LAT] = np.cos(ang)
    c[:, C_SIN:C_SIN + LAT] = np.sin(ang)
    for m in range(P):
        if m % (2 * quarter) < quarter:
            c[m + quarter, C_ROT + m] = -1.0
        else:
            c[m - quarter, C_ROT + m] = 1.0
    c[:, C_HM:C_HM + GLA_H] = (i[:, None] // DK) == np.arange(GLA_H)[None, :]
    c[:, C_IOTA:C_IOTA + NLT] = i[:, None] + P * np.arange(NLT)[None, :]
    c[:, C_SUM:C_SUM + NE] = (i[:, None] % 32) == np.arange(NE)[None, :]
    return c


def _band(np):
    distance = np.arange(3 * P)[None, :] - P - np.arange(P)[:, None]
    return np.where(np.abs(distance) <= WINDOW, 0.0, NEG).astype(np.float32)


def _layout(np, a):
    f = np.float32
    x_all = np.concatenate([a["x"][0], a["ctx"][0]], 0)
    cvec = np.stack([a["c"][0].reshape(KC, P).T, a["c_ctx"].reshape(KC, P).T], 2).reshape(P, 2 * KC)
    widths = (GLA_H * DK, GLA_H * DV, 16, 16, NAT_H * HD, NAT_H * HD, 2 * HD, 2 * HD, GLA_H * DK, GLA_H * DV, NAT_H * HD, SWA_H * HD)
    at = np.concatenate([[0], np.cumsum(widths)])
    sq_order = np.concatenate([np.arange(HD) + HD * (p // 2 + 4 * (p % 2)) for p in range(SWA_H)])

    def rows(w):
        return w.reshape(KC, P, -1).transpose(1, 0, 2)

    def blocks(w):
        return w.reshape(KC, P, 4, P).transpose(1, 2, 0, 3).reshape(P, UNIT)

    stream = np.zeros((N_UNITS, P, UNIT), f)
    params = np.zeros((DEPTH, P, PARAMS), f)
    for l in range(DEPTH):
        for k in range(MOD_UNITS):
            stream[mod_at(l * MOD_UNITS + k)] = rows(a["w_mod"][l][:, 512 * k:512 * (k + 1)]).reshape(P, UNIT)
        gk, gv, gaf, gab, nk, nv, sk, sv, gq, gg, nq, sq = (a["w_in"][l][:, at[i]:at[i + 1]] for i in range(12))
        z16 = np.zeros((D, 16), f)
        al = np.concatenate([gaf, z16, gab, z16, z16, z16, z16, z16], 1)
        u = IN_AT[l]
        stream[u] = blocks(np.concatenate([gk, al, gq, sk], 1))
        stream[u + 1] = rows(np.concatenate([gv, nv], 1)).reshape(P, UNIT)
        stream[u + 2, :, 0:KC * 384] = rows(np.concatenate([sv, gg], 1)).reshape(P, -1)
        stream[u + 2, :, KC * 384:KC * 400] = rows(a["w_router"][l]).reshape(P, -1)
        stream[u + 3] = blocks(sq[:, sq_order])
        stream[u + 4] = blocks(np.concatenate([nk, nq], 1))
        for j in range(2):
            wo = np.concatenate([a["w_out"][l][0:512], a["w_out"][l][512:][sq_order]], 0)
            stream[OUT_AT[l] + j] = rows(wo[:, 512 * j:512 * (j + 1)]).reshape(P, UNIT)
        for e in range(NE):
            u = FFN_AT[l] + 6 * e
            gu = np.concatenate([rows(a["w_gate"][l, e]), rows(a["w_up"][l, e])], 2)
            stream[u:u + 4] = gu.reshape(P, 4, UNIT).transpose(1, 0, 2)
            stream[u + 4:u + 6] = rows(a["w_down"][l, e]).reshape(P, 2, UNIT).transpose(1, 0, 2)
        params[l, :, P_BMOD:P_BMOD + 96] = np.repeat(a["b_mod"][l].reshape(48, P).T[:, :, None], 2, 2).reshape(P, 96)
        params[l, :, P_GAIN:P_GAIN + 32] = a["norm_gains"][l].reshape(4, KC, P).transpose(2, 0, 1).reshape(P, 32)
        params[l, 0:16, P_AUP:P_AUP + P] = a["gla_a_up"][l, 0]
        params[l, 32:48, P_AUP:P_AUP + P] = a["gla_a_up"][l, 1]
        params[l, :, P_AB:P_AB + 2] = a["gla_a_bias"][l].T
        params[l, :, P_GG:P_GG + DV] = a["gla_norm"][l][None, :]
        params[l, :, P_SINK:P_SINK + SWA_H] = a["swa_sink"][l][None, :]
    t = np.arange(LAT)
    c, r = t // NAT_ROWS, t % NAT_ROWS
    start = np.clip(c - NAT_COLS // 2, 0, GRID_W - NAT_COLS)
    seen = (c[None, :] >= start[:, None]) & (c[None, :] < start[:, None] + NAT_COLS)
    ri = r[None, :] - r[:, None] + NAT_ROWS - 1
    ci = np.clip(c[None, :] - c[:, None] + NAT_COLS - 1, 0, 2 * NAT_COLS - 2)
    full = np.where(seen, a["nat_rpb"][:, :, ri, ci], f(NEG)).astype(f)
    bias = np.full((DEPTH, NLT, NAT_H, P, 3 * P), NEG, f)
    for j in range(NLT):
        k0, k1 = max(j - 1, 0) * P, min(j + 2, NLT) * P
        assert not seen[j * P:(j + 1) * P, :k0].any() and not seen[j * P:(j + 1) * P, k1:].any()
        bias[:, j, :, :, 0:k1 - k0] = full[:, :, j * P:(j + 1) * P, k0:k1]
    iotarow = np.broadcast_to(np.arange(LAT, dtype=f), (P, LAT))
    return {"x_all": x_all, "cvec": cvec, "consts": _constants(np), "band": _band(np), "iotarow": iotarow, "params": params,
            "nat_bias": bias, "wstream": stream}


def kernel(**inputs):
    import numpy as np
    import concourse.bacc as bacc
    from concourse import mybir as mb
    from concourse.bass_utils import run_bass_kernel_spmd as run

    nc = bacc.Bacc("TRN2", target_bir_lowering=False, num_devices=1)
    arrays, args = {}, []
    laid = _layout(np, {k: np.asarray(v) for k, v in inputs.items()})
    for name in ("x_all", "cvec", "consts", "band", "iotarow", "params", "nat_bias", "wstream"):
        v = np.ascontiguousarray(laid[name])
        arrays[f"in_{name}"] = v
        args.append(nc.dram_tensor(f"in_{name}", v.shape, mb.dt.from_np(v.dtype), kind="ExternalInput").ap())
    args.append(nc.dram_tensor("x_kept", (TOK, D), mb.dt.float32).ap())
    args.append(nc.dram_tensor("picked", (DEPTH, 2, 2, NE * CAP_L), mb.dt.float32).ap())
    args.append(nc.dram_tensor("out_x", (LAT, D), mb.dt.float32, kind="ExternalOutput").ap())
    bass_hybrid_dit(nc, *args)
    r = run(nc, [arrays], core_ids=[0])
    return r.results[0]["out_x"].reshape(1, LAT, D)
```
